# Optimizing a Trainium2 kernel written in Bass

```python
import math
import jax, jax.numpy as jnp
from jax import lax
import numpy as np

D_MODEL = 1024
BATCH = 1
SEQ = 1024
DEPTH = 2

N_MIXERS = 2
N_MLA = (DEPTH + 1) // 2
N_LRU = DEPTH // 2

MLA_HEADS = 8
QK_NOPE_DIM = 128
QK_ROPE_DIM = 64
V_HEAD_DIM = 128
Q_LORA_RANK = 384
KV_LORA_RANK = 256
ROPE_THETA = 10000.0
Q_BLOCK = 128
ATTN_SCALE = 1.0 / math.sqrt(QK_NOPE_DIM + QK_ROPE_DIM)

LRU_WIDTH = D_MODEL
LRU_BLOCKS = 8
LRU_BLOCK_SIZE = LRU_WIDTH // LRU_BLOCKS
CONV_WIDTH = 4
LRU_C = 8.0

FFN_HIDDEN = 4 * D_MODEL
NORM_EPS = 1e-6

kernel_name = "hybrid_mla_rglru_sandwich_trunk"

def _rmsnorm(x, g):
    x32 = x.astype(jnp.float32)
    y = x32 * lax.rsqrt(jnp.mean(x32 * x32, axis=-1, keepdims=True) + NORM_EPS)
    return (y * g.astype(jnp.float32)).astype(x.dtype)

def _rotary(x, cos, sin):
    half = x.shape[-1] // 2
    x1, x2 = x[..., :half], x[..., half:]
    return jnp.concatenate([x1 * cos - x2 * sin, x2 * cos + x1 * sin], axis=-1)

def _mla(h, positions, w_in, q_norm, kv_norm, w_uq, w_ukv, w_o):
    B, S, _ = h.shape
    H = MLA_HEADS
    proj = h @ w_in
    c_q = _rmsnorm(proj[..., :Q_LORA_RANK], q_norm)
    c_kv = _rmsnorm(proj[..., Q_LORA_RANK:Q_LORA_RANK + KV_LORA_RANK], kv_norm)
    k_rope = proj[..., Q_LORA_RANK + KV_LORA_RANK:]
    q = (c_q @ w_uq).reshape(B, S, H, QK_NOPE_DIM + QK_ROPE_DIM)
    q_nope, q_rope = q[..., :QK_NOPE_DIM], q[..., QK_NOPE_DIM:]
    kv = (c_kv @ w_ukv).reshape(B, S, H, QK_NOPE_DIM + V_HEAD_DIM)
    k_nope, v = kv[..., :QK_NOPE_DIM], kv[..., QK_NOPE_DIM:]

    inv_freq = ROPE_THETA ** (-jnp.arange(0, QK_ROPE_DIM, 2, dtype=jnp.float32) / QK_ROPE_DIM)
    ang = positions.astype(jnp.float32)[..., None] * inv_freq
    cos, sin = jnp.cos(ang).astype(h.dtype), jnp.sin(ang).astype(h.dtype)
    q_rope = _rotary(q_rope, cos[:, :, None, :], sin[:, :, None, :])
    k_rope = _rotary(k_rope, cos, sin)

    nqb = S // Q_BLOCK
    qn_b = q_nope.reshape(B, nqb, Q_BLOCK, H, QK_NOPE_DIM).transpose(1, 0, 2, 3, 4)
    qr_b = q_rope.reshape(B, nqb, Q_BLOCK, H, QK_ROPE_DIM).transpose(1, 0, 2, 3, 4)
    kpos = jnp.arange(S)

    def attend(args):
        qn, qr, blk = args
        s = (jnp.einsum('bqhd,bkhd->bhqk', qn, k_nope)
             + jnp.einsum('bqhr,bkr->bhqk', qr, k_rope)).astype(jnp.float32) * ATTN_SCALE
        qpos = blk * Q_BLOCK + jnp.arange(Q_BLOCK)
        s = jnp.where(kpos[None, :] <= qpos[:, None], s, -jnp.inf)
        p = jax.nn.softmax(s, axis=-1).astype(v.dtype)
        return jnp.einsum('bhqk,bkhd->bqhd', p, v)

    o = lax.map(attend, (qn_b, qr_b, jnp.arange(nqb)))
    o = o.transpose(1, 0, 2, 3, 4).reshape(B, S, H * V_HEAD_DIM)
    return o @ w_o

def _rglru_block(h, w_in, conv_w, conv_b, w_a, b_a, w_x, b_x, lam, w_out):
    B, S, _ = h.shape
    proj = h @ w_in
    gate = jax.nn.gelu(proj[..., :LRU_WIDTH], approximate=True)
    rec = proj[..., LRU_WIDTH:]
    xp = jnp.pad(rec, ((0, 0), (CONV_WIDTH - 1, 0), (0, 0)))
    xc = conv_b + sum(xp[:, k:k + S] * conv_w[k] for k in range(CONV_WIDTH))
    xc32 = xc.astype(jnp.float32)
    xb = xc32.reshape(B, S, LRU_BLOCKS, LRU_BLOCK_SIZE)
    r = jax.nn.sigmoid(jnp.einsum('bsnc,ncd->bsnd', xb, w_a.astype(jnp.float32)).reshape(B, S, LRU_WIDTH)
                       + b_a.astype(jnp.float32))
    i = jax.nn.sigmoid(jnp.einsum('bsnc,ncd->bsnd', xb, w_x.astype(jnp.float32)).reshape(B, S, LRU_WIDTH)
                       + b_x.astype(jnp.float32))
    log_a = -LRU_C * r * jax.nn.softplus(-lam.astype(jnp.float32))
    a = jnp.exp(log_a)
    b = jnp.sqrt(-jnp.expm1(2.0 * log_a)) * (i * xc32)

    def combine(left, right):
        a1, b1 = left
        a2, b2 = right
        return a1 * a2, a2 * b1 + b2

    _, hs = lax.associative_scan(combine, (a, b), axis=1)
    return (gate * hs.astype(h.dtype)) @ w_out

def _sq_relu_mlp(h, w_up, w_down):
    u = jax.nn.relu(h @ w_up)
    return (u * u) @ w_down

def setup_inputs(seed: int = 0) -> dict:
    key = jax.random.key(seed)
    ks = jax.random.split(key, 24)
    f32 = jnp.float32

    def nrm(k, shape, fan_in):
        return jax.random.normal(k, shape, f32) * (fan_in ** -0.5)

    def gain(k, shape):
        return 1.0 + 0.05 * jax.random.normal(k, shape, f32)

    x = jax.random.normal(ks[0], (BATCH, SEQ, D_MODEL), f32)
    positions = jnp.broadcast_to(jnp.arange(SEQ, dtype=jnp.int32), (BATCH, SEQ))
    mla_in = Q_LORA_RANK + KV_LORA_RANK + QK_ROPE_DIM
    u = jax.random.uniform(ks[14], (N_LRU, LRU_WIDTH), f32, 0.9, 0.999)
    s0 = u ** (1.0 / LRU_C)
    lam = jnp.log(s0) - jnp.log1p(-s0)
    return {
        "x": x,
        "positions": positions,
        "mix_pre_norm": gain(ks[1], (DEPTH, D_MODEL)),
        "mix_post_norm": gain(ks[2], (DEPTH, D_MODEL)),
        "ffn_pre_norm": gain(ks[3], (DEPTH, D_MODEL)),
        "ffn_post_norm": gain(ks[4], (DEPTH, D_MODEL)),
        "mla_w_in": nrm(ks[5], (N_MLA, D_MODEL, mla_in), D_MODEL),
        "mla_q_norm": gain(ks[6], (N_MLA, Q_LORA_RANK)),
        "mla_kv_norm": gain(ks[7], (N_MLA, KV_LORA_RANK)),
        "mla_w_uq": nrm(ks[8], (N_MLA, Q_LORA_RANK, MLA_HEADS * (QK_NOPE_DIM + QK_ROPE_DIM)), Q_LORA_RANK),
        "mla_w_ukv": nrm(ks[9], (N_MLA, KV_LORA_RANK, MLA_HEADS * (QK_NOPE_DIM + V_HEAD_DIM)), KV_LORA_RANK),
        "mla_w_o": nrm(ks[10], (N_MLA, MLA_HEADS * V_HEAD_DIM, D_MODEL), MLA_HEADS * V_HEAD_DIM),
        "lru_w_in": nrm(ks[11], (N_LRU, D_MODEL, 2 * LRU_WIDTH), D_MODEL),
        "lru_conv_w": nrm(ks[12], (N_LRU, CONV_WIDTH, LRU_WIDTH), CONV_WIDTH),
        "lru_conv_b": 0.01 * jax.random.normal(ks[13], (N_LRU, LRU_WIDTH), f32),
        "lru_w_a": nrm(ks[15], (N_LRU, LRU_BLOCKS, LRU_BLOCK_SIZE, LRU_BLOCK_SIZE), LRU_BLOCK_SIZE),
        "lru_b_a": 0.01 * jax.random.normal(ks[16], (N_LRU, LRU_WIDTH), f32),
        "lru_w_x": nrm(ks[17], (N_LRU, LRU_BLOCKS, LRU_BLOCK_SIZE, LRU_BLOCK_SIZE), LRU_BLOCK_SIZE),
        "lru_b_x": 0.01 * jax.random.normal(ks[18], (N_LRU, LRU_WIDTH), f32),
        "lru_lambda": lam,
        "lru_w_out": nrm(ks[19], (N_LRU, LRU_WIDTH, D_MODEL), LRU_WIDTH),
        "ffn_w_up": nrm(ks[20], (DEPTH, D_MODEL, FFN_HIDDEN), D_MODEL),
        "ffn_w_down": nrm(ks[21], (DEPTH, FFN_HIDDEN, D_MODEL), FFN_HIDDEN),
    }

def reference(x, positions, mix_pre_norm, mix_post_norm, ffn_pre_norm, ffn_post_norm,
              mla_w_in, mla_q_norm, mla_kv_norm, mla_w_uq, mla_w_ukv, mla_w_o,
              lru_w_in, lru_conv_w, lru_conv_b, lru_w_a, lru_b_a, lru_w_x, lru_b_x,
              lru_lambda, lru_w_out, ffn_w_up, ffn_w_down):
    for layer in range(DEPTH):
        j = layer // N_MIXERS
        hn = _rmsnorm(x, mix_pre_norm[layer])
        if layer % N_MIXERS == 0:
            y = _mla(hn, positions, mla_w_in[j], mla_q_norm[j], mla_kv_norm[j],
                     mla_w_uq[j], mla_w_ukv[j], mla_w_o[j])
        else:
            y = _rglru_block(hn, lru_w_in[j], lru_conv_w[j], lru_conv_b[j], lru_w_a[j], lru_b_a[j],
                             lru_w_x[j], lru_b_x[j], lru_lambda[j], lru_w_out[j])
        x = x + _rmsnorm(y, mix_post_norm[layer])
        hn = _rmsnorm(x, ffn_pre_norm[layer])
        y = _sq_relu_mlp(hn, ffn_w_up[layer], ffn_w_down[layer])
        x = x + _rmsnorm(y, ffn_post_norm[layer])
    return x


_drawn_inputs = setup_inputs


def setup_inputs(seed=0):
    import zlib

    import numpy as np

    out = dict(_drawn_inputs(seed))
    spreads = {}
    factors = {'lru_conv_b': 4.212, 'lru_b_a': 63.146, 'lru_b_x': 24.706}
    for name, (base, spread) in spreads.items():
        noise = np.random.default_rng([zlib.crc32(name.encode()), seed]).standard_normal(out[name].shape)
        drawn = base * np.exp(spread * noise) if base else spread * noise
        out[name] = __import__('jax').numpy.asarray(drawn.astype(out[name].dtype))
    for name, factor in factors.items():
        out[name] = (out[name] * factor).astype(out[name].dtype)
    return out
```

```python
from collections import namedtuple
from contextlib import ExitStack

import numpy as np

import concourse.bass as bass
from concourse import mybir

F32 = mybir.dt.float32
F32R = mybir.dt.float32r
BF16 = mybir.dt.bfloat16
I32 = mybir.dt.int32
ACT = mybir.ActivationFunctionType
ALU = mybir.AluOpType
AX = mybir.AxisListType

P = 128
D = 1024
SEQ = 1024
TB = SEQ // P
KT = D // P
HALF = 512
NORM_EPS = 1e-6

HEADS = 8
NOPE, ROPE, VDIM = 128, 64, 128
QRANK, KVRANK = 384, 256
QK, KK = QRANK // P, KVRANK // P
RH = ROPE // 2
SCALE = float(1.0 / np.sqrt(NOPE + ROPE))
ROPE_THETA = 10000.0
GH = 4
GROUPS = HEADS // GH
HEADW = (QK + 2 * KK) * P
ROPEW = QK * GH * ROPE
MASKED = -float(2.0 ** 100)

FFN = 4 * D
FG = 4
MLP_GROUPS = FFN // P // FG
CONV = 4
CH = D // P
LRU_C = 8.0
VEC_IN = CONV + 4
VEC = VEC_IN + 2

KB = 1024
AT_HT = 7 * KB
AT_S = AT_HT + 64 * KB
AT_RAW = AT_S + 32 * KB
AT_W = AT_RAW + 16 * KB


def inverse_frequencies():
    return (ROPE_THETA ** (-np.arange(0, ROPE, 2) / ROPE)).astype(np.float32)


def trunk(nc, x, positions, inv_freq, gains, qkv_gain, w_in_q, w_in_kv, w_heads, w_rope, w_o,
          w_rec, w_gate, w_ax, lru_vec, w_out, w_up, w_down, out):
    base = (nc.sbuf_base + 31) // 32 * 32

    def at(name, shape, dtype, offset):
        return nc.alloc_sbuf_tensor_at(name, [P, *shape], dtype, offset=base + offset)

    with ExitStack() as ctx:
        def sems(stage, *names):
            return namedtuple(stage, names)(*(ctx.enter_context(nc.semaphore(f"{stage}_{n}")) for n in names))

        xs = [nc.dram_tensor(f"x_after_{n}", (TB, P, D), F32, kind="Internal").ap() for n in range(3)]

        ps = ctx.enter_context(nc.psum_tensor("ps", [P, 8, HALF], F32))
        psf = ps[:].rearrange("p b n -> p (b n)")

        ident = at("ident", [P], F32, 0)
        identr = at("identr", [P], F32R, 512)
        mask = at("mask", [P], F32, 1024)
        maskr = at("maskr", [P], F32R, 1536)
        junk = at("junk", [D], BF16, 2048)
        stat = at("stat", [6, 6, TB], F32, 4096)
        power = at("power", [1], F32, 5248)
        neg_max = at("neg_max", [TB], F32, 5280)
        row_sum = at("row_sum", [TB], F32, 5312)
        row_inv = at("row_inv", [TB], F32, 5344)
        row_max = at("row_max", [TB], F32, 5376)
        stat1 = at("stat1", [3, 2 * TB], F32, 5856)

        hth = at("hth", [KT, SEQ], F32R, AT_HT)
        htl = at("htl", [KT, SEQ], F32R, AT_HT + 32 * KB)
        raw = at("raw", [4, D], F32, AT_RAW)
        rows = at("rows", [TB, D], F32, AT_S)
        gain0 = at("gain0", [D], F32, AT_W + 64 * KB)
        GAIN = 2
        xt = at("xt", [2, D], F32, AT_W + 80 * KB)

        def f32(ap):
            return ap.bitcast(F32)

        def three_passes(pe, dst, wh, wl, xh, xl, first, last):
            pe.matmul(dst, wh, xh, start=first, stop=False)
            pe.matmul(dst, wh, xl, start=False, stop=False)
            return pe.matmul(dst, wl, xh, start=False, stop=last)

        E = sems("end", "x_in0", "x_in1", "gain_in", "y_ready", "ss_y", "var_y", "rstd_y", "scaled", "x_new", "ss_x", "var_x",
                 "rstd_x", "hn", "turned", "ht_hi", "ht_lo", "x_out0", "x_out1")

        X_IN = sems("input", *(f"block{tb}" for tb in range(TB)))

        def pre(n, k):
            return TB * n + k

        def post(n, k):
            return TB * (n - 1) + k

        def x_loaded(n, tb):
            if n == 0:
                return X_IN[tb], 16
            return (E.x_in0, E.x_in1)[tb % 2], 16 * (TB // 2 * (n - 1) + tb // 2 + 1)

        def x_stored(n, tb):
            return (E.x_out0, E.x_out1)[tb % 2], 16 * (TB // 2 * (n - 1) + tb // 2 + 1)

        def x_block(n, tb):
            return rows[:, tb, :] if n == 0 else xt[:, tb % 2, :]

        def gains_loaded(n):
            return 16 * (2 * n + 1 if n < 4 else 2 * n)

        x_src = [x, x, *xs]
        x_dst = [None, *xs, out]

        def end_loads(sp, n):
            if n == 0:
                sp.dma_start(rows[:, 0, :], x_src[0][0]).then_inc(x_loaded(0, 0)[0], 16)
                sp.dma_start(gain0[:], gains[0:1, :].partition_broadcast(P)).then_inc(E.gain_in, 16)
                for tb in range(1, TB):
                    sp.dma_start(rows[:, tb, :], x_src[0][tb]).then_inc(x_loaded(0, tb)[0], 16)
                return
            sp.dma_start(raw[:, GAIN, :], gains[2 * n - 1:2 * n, :].partition_broadcast(P)).then_inc(E.gain_in, 16)
            if n < 4:
                sp.dma_start(raw[:, GAIN + 1, :], gains[2 * n:2 * n + 1, :].partition_broadcast(P)).then_inc(E.gain_in, 16)
            sp.dma_start(xt[:, 0, :], x_src[n][0]).then_inc(E.x_in0, 16)
            sp.dma_start(xt[:, 1, :], x_src[n][1]).then_inc(E.x_in1, 16)

        def end_sync(sp, n):
            for tb in range(TB):
                sp.wait_ge(E.x_new, post(n, tb + 1))
                sp.dma_start(x_dst[n][tb], xt[:, tb % 2, :]).then_inc(x_stored(n, tb)[0], 16)
                if tb + 2 < TB:
                    sp.wait_ge(*x_stored(n, tb))
                    if n < 4:
                        sp.wait_ge(E.hn, pre(n, tb + 1))
                    sp.dma_start(xt[:, tb % 2, :], x_src[n][tb + 2]).then_inc(x_loaded(n, tb + 2)[0], 16)
            sp.wait_ge(*x_stored(n, TB - 2))
            sp.wait_ge(*x_stored(n, TB - 1))
            if n < 4:
                sp.wait_ge(E.hn, pre(n, TB))

        DVE_SUMS = 6

        def end_scalar(act, n, step, copies):
            if step < TB and n > 0:
                if copies:
                    act.wait_ge(copies, step + 1)
                    act.activation(rows[:, step, :], psf[:, step % 2 * D:step % 2 * D + D], ACT.Copy).then_inc(E.y_ready, 1)
                act.wait_ge(E.y_ready, post(n, step + 1))
                act.wait_ge(E.ss_x, pre(min(n, 3), max(0, step - 1)) if n < 4 else pre(3, TB))
                act.wait_ge(E.ss_y, post(n, step))
                act.activation(junk[:], rows[:, step, :], ACT.Square,
                               accum_out=stat[:, 0, n, step:step + 1]).then_inc(E.ss_y, 1)
            tb = step - 1
            if 0 <= tb < TB and n < 4:
                if n > 0:
                    act.wait_ge(E.x_new, post(n, tb + 1))
                else:
                    act.wait_ge(*x_loaded(n, tb))
                act.wait_ge(E.ss_x, pre(n, tb))
                if n > 0:
                    act.wait_ge(E.ss_y, post(n, min(step + 1, TB)))
                act.activation(junk[:], x_block(n, tb), ACT.Square,
                               accum_out=stat[:, 3, n, tb:tb + 1]).then_inc(E.ss_x, 1)
            tb = step - 3
            if 0 <= tb < TB and n < 4:
                act.wait_ge(E.turned, pre(n, tb + 1))
                src = psf[:, 2 * D + tb % 2 * D:3 * D + tb % 2 * D].rearrange("p (f t) -> p f t", f=KT)
                act.activation(hth[:, :, tb * P:(tb + 1) * P], src, ACT.Copy).then_inc(E.ht_hi, 1)

        def end_gpsimd(pool, n, step):
            if step < TB and n > 0:
                col = slice(step, step + 1)
                pool.wait_ge(E.ss_y, post(n, step + 1))
                pool.tensor_scalar(stat[:, 1, n, col], stat[:, 0, n, col], 1.0 / D, NORM_EPS, ALU.mult, ALU.add).then_inc(E.var_y, 1)
                pool.wait_ge(E.var_y, post(n, step + 1))
                pool.tensor_tensor(stat[:, 2, n, col], stat[:, 1, n, col], power[:], ALU.pow).then_inc(E.rstd_y, 1)
            tb = step - 1
            if 0 <= tb < TB:
                col = slice(tb, tb + 1)
                if 0 < n and tb < DVE_SUMS:
                    pool.wait_ge(*x_loaded(n, tb))
                    pool.wait_ge(E.scaled, post(n, tb + 1))
                    pool.tensor_tensor(xt[:, tb % 2, :], xt[:, tb % 2, :], rows[:, tb, :], ALU.add).then_inc(E.x_new, 1)
                if n < 4:
                    pool.wait_ge(E.ss_x, pre(n, tb + 1))
                    pool.tensor_scalar(stat[:, 4, n, col], stat[:, 3, n, col], 1.0 / D, NORM_EPS, ALU.mult, ALU.add).then_inc(E.var_x, 1)
                    pool.wait_ge(E.var_x, pre(n, tb + 1))
                    pool.tensor_tensor(stat[:, 5, n, col], stat[:, 4, n, col], power[:], ALU.pow).then_inc(E.rstd_x, 1)

        def end_vector(dve, n, step):
            tb = step - 1
            if 0 <= tb < TB and n > 0:
                if tb == 0:
                    dve.wait_ge(E.gain_in, gains_loaded(n))
                dve.wait_ge(E.rstd_y, post(n, tb + 1))
                dve.scalar_tensor_tensor(out=rows[:, tb, :], in0=rows[:, tb, :], scalar=stat[:, 2, n, tb:tb + 1],
                                         in1=raw[:, GAIN, :], op0=ALU.mult, op1=ALU.mult).then_inc(E.scaled, 1)
                if tb >= DVE_SUMS:
                    dve.wait_ge(*x_loaded(n, tb))
                    dve.wait_ge(E.scaled, post(n, tb + 1))
                    dve.wait_ge(E.x_new, post(n, tb))
                    dve.tensor_tensor(xt[:, tb % 2, :], xt[:, tb % 2, :], rows[:, tb, :], ALU.add).then_inc(E.x_new, 1)
            tb = step - 2
            if 0 <= tb < TB and n < 4:
                if n == 0 and tb == 0:
                    dve.wait_ge(E.gain_in, gains_loaded(n))
                if n == 0:
                    dve.wait_ge(*x_loaded(n, tb))
                else:
                    dve.wait_ge(E.x_new, post(n, tb + 1))
                dve.wait_ge(E.rstd_x, pre(n, tb + 1))
                dve.scalar_tensor_tensor(out=rows[:, tb, :], in0=x_block(n, tb), scalar=stat[:, 5, n, tb:tb + 1],
                                         in1=gain0[:] if n == 0 else raw[:, GAIN + 1, :], op0=ALU.mult, op1=ALU.mult).then_inc(E.hn, 1)
            tb = step - 3
            if 0 <= tb < TB and n < 4:
                dve.wait_ge(E.ht_hi, pre(n, tb + 1))
                src = psf[:, 2 * D + tb % 2 * D:3 * D + tb % 2 * D].rearrange("p (f t) -> p f t", f=KT)
                dst = slice(tb * P, (tb + 1) * P)
                dve.tensor_tensor(htl[:, :, dst], src, f32(hth[:, :, dst]), ALU.subtract).then_inc(E.ht_lo, 1)

        def end_tensor(pe, n, tb):
            if not 0 <= tb < TB or n == 4:
                return
            pe.wait_ge(E.hn, pre(n, tb + 1))
            if tb >= 2:
                pe.wait_ge(E.ht_lo, pre(n, tb - 1))
            for f in range(KT):
                col = 2 * D + tb % 2 * D + f * P
                mm = pe.transpose(psf[:, col:col + P], rows[:, tb, f * P:(f + 1) * P], ident[:])
            mm.then_inc(E.turned, 1)

        STEPS = TB + 3
        EARLY = (5, 7)

        aT = at("aT", [KT * SEQ], F32, AT_S)
        wo_h = [at(f"wo_h{k}", [D], F32R, AT_W + 8 * KB * k) for k in range(KT)]
        wo_l = [at(f"wo_l{k}", [D], F32R, AT_W + 8 * KB * k + 4 * KB) for k in range(KT)]
        PROJ = {n: sems(f"proj{n}", "raw_in0", "raw_in1", "raw_in2", "raw_in3", "w_hi", "w_lo", "a_hi", "a_lo", "y_done")
                for n in (1, 3)}

        def proj_loads(sp, n, w, chunks):
            q = PROJ[n]
            for k in chunks:
                if k >= 4:
                    sp.wait_ge(q.w_lo, k - 3)
                sp.dma_start(raw[:, k % 4, :], w[k]).then_inc((q.raw_in0, q.raw_in1, q.raw_in2, q.raw_in3)[k % 4], 16)

        def proj_scalar(act, n, w_free, w_free_count, a_done, a_count):
            q = PROJ[n]
            act.wait_ge(w_free, w_free_count)
            for k in range(KT):
                act.wait_ge((q.raw_in0, q.raw_in1, q.raw_in2, q.raw_in3)[k % 4], 16 * (k // 4 + 1))
                act.activation(wo_h[k][:], raw[:, k % 4, :], ACT.Copy).then_inc(q.w_hi, 1)
                if k == 0:
                    act.wait_ge(a_done, a_count)
                act.activation(hth[:, k, :], aT[:, k * SEQ:(k + 1) * SEQ], ACT.Copy).then_inc(q.a_hi, 1)
            act.wait_ge(q.a_lo, KT)

        def proj_vector(dve, n):
            q = PROJ[n]
            for k in range(KT):
                dve.wait_ge(q.w_hi, k + 1)
                dve.tensor_tensor(wo_l[k][:], raw[:, k % 4, :], f32(wo_h[k][:]), ALU.subtract).then_inc(q.w_lo, 1)
                dve.wait_ge(q.a_hi, k + 1)
                dve.tensor_tensor(htl[:, k, :], aT[:, k * SEQ:(k + 1) * SEQ], f32(hth[:, k, :]), ALU.subtract).then_inc(q.a_lo, 1)

        def proj_tensor(pe, n):
            q = PROJ[n]
            for step in range(STEPS):
                if step < TB:
                    tb = step
                    if tb >= 2:
                        pe.wait_ge(E.y_ready, post(n, tb - 1))
                    for k in range(KT):
                        if tb == 0:
                            pe.wait_ge(q.w_lo, k + 1)
                            pe.wait_ge(q.a_lo, k + 1)
                        blk = slice(tb * P, (tb + 1) * P)
                        for c in range(D // HALF):
                            dst = ps[:, tb % 2 * 2 + c, :]
                            cut = slice(c * HALF, (c + 1) * HALF)
                            mm = three_passes(pe, dst, hth[:, k, blk], htl[:, k, blk], wo_h[k][:, cut], wo_l[k][:, cut],
                                              k == 0, k == KT - 1)
                    mm.then_inc(q.y_done, 1)
                end_tensor(pe, n, step - 3)

        u_h = at("u_h", [FG, SEQ], F32R, AT_W)
        u_l = at("u_l", [FG, SEQ], F32R, AT_W + 16 * KB)
        dn_h = at("dn_h", [FG, D], F32R, AT_W + 32 * KB)
        dn_l = at("dn_l", [FG, D], F32R, AT_W + 48 * KB)
        up_h = [at(f"up_h{s}", [KT, P], F32R, AT_W + (72 - 8 * s) * KB) for s in range(2)]
        up_l = [at(f"up_l{s}", [KT, P], F32R, AT_W + (76 - 8 * s) * KB) for s in range(2)]
        relu = at("relu", [2, HALF], F32, AT_W + 80 * KB)
        squared = at("squared", [2, HALF], F32, AT_W + 84 * KB)
        MLP = {n: sems(f"mlp{n}", "raw_in0", "raw_in1", "raw_in2", "raw_in3", "w_hi", "w_lo", "up_done", "relu", "sq",
                       "u_hi", "u_lo", "down_done", "y_sum") for n in (2, 4)}
        SLOT = {("up", 0): 0, ("up", 1): 1, ("down", 0): 2, ("down", 1): 3,
                ("up", 2): 0, ("down", 2): 1, ("up", 3): 2, ("down", 3): 3}

        def mlp_loads_first(sp, n, layer, kinds):
            q = MLP[n]
            if "up" in kinds:
                sp.dma_start(raw[:, 0, :], w_up[layer, 0]).then_inc(q.raw_in0, 16)
                sp.dma_start(raw[:, 1, :], w_up[layer, 1]).then_inc(q.raw_in1, 16)
            if "down" in kinds:
                sp.dma_start(raw[:, 2, :], w_down[layer, 0]).then_inc(q.raw_in2, 16)
                sp.dma_start(raw[:, 3, :], w_down[layer, 1]).then_inc(q.raw_in3, 16)

        SPLITS = [("down", 0), ("down", 1), ("up", 2), ("down", 2), ("up", 3), ("down", 3), ("up", 4), ("up", 5)]

        UP_ORDER = [(0, 0), (1, 0), (0, 1), (1, 1), (2, 0), (2, 1), (3, 0), (3, 1)]

        def mlp_sync(sp, n, layer):
            q = MLP[n]
            ins = (q.raw_in0, q.raw_in1, q.raw_in2, q.raw_in3)

            def load(src, row, slot, split_before):
                sp.wait_ge(q.w_lo, split_before)
                sp.dma_start(raw[:, slot, :], src[layer, row]).then_inc(ins[slot], 16)

            def group(g, last):
                rows_ = [sp.snap(g * FG + i) for i in range(2, FG + 2)] if not isinstance(g, int) else [g * FG + i for i in range(2, FG + 2)]
                load(w_up, rows_[0], 0, 8 * g + 1)
                load(w_down, rows_[0], 1, 8 * g + 2)
                load(w_up, rows_[1], 2, 8 * g + 3)
                load(w_down, rows_[1], 3, 8 * g + 4)
                if not last:
                    load(w_up, rows_[2], 0, 8 * g + 5)
                    load(w_up, rows_[3], 1, 8 * g + 6)
                    load(w_down, rows_[2], 2, 8 * g + 7)
                    load(w_down, rows_[3], 3, 8 * g + 8)

            with sp.Fori(0, MLP_GROUPS - 1) as g:
                group(g, False)
            group(MLP_GROUPS - 1, True)

        def mlp_chunk(n, g, kind, i):
            slot = SLOT[kind, i % FG]
            early = (kind, i) in (("down", 0), ("down", 1))
            arrived = 32 * g + (16 if early else 32 if i < FG else 48)
            if kind == "up":
                return slot, arrived, up_h[i % 2][:].rearrange("p a b -> p (a b)"), up_l[i % 2][:].rearrange("p a b -> p (a b)")
            return slot, arrived, dn_h[:, i, :], dn_l[:, i, :]

        def mlp_first_up(n, i):
            return i, 16, up_h[i][:].rearrange("p a b -> p (a b)"), up_l[i][:].rearrange("p a b -> p (a b)")

        def split_hi(act, q, chunk):
            slot, arrived, hi, lo = chunk
            act.wait_ge((q.raw_in0, q.raw_in1, q.raw_in2, q.raw_in3)[slot], arrived)
            act.activation(hi, raw[:, slot, 0:hi.shape[1]], ACT.Copy).then_inc(q.w_hi, 1)

        def split_lo(dve, q, chunk, count):
            slot, arrived, hi, lo = chunk
            dve.wait_ge(q.w_hi, count)
            dve.tensor_tensor(lo, raw[:, slot, 0:hi.shape[1]], f32(hi), ALU.subtract).then_inc(q.w_lo, 1)

        def mlp_scalar(act, n):
            q = MLP[n]

            def evacuate(g, *numbers):
                for i in numbers:
                    ft, half = UP_ORDER[i]
                    act.wait_ge(q.up_done, 8 * g + i + 1)
                    if i >= 2:
                        act.wait_ge(q.sq, 8 * g + i - 1)
                    act.activation(relu[:, i % 2, :], ps[:, 4 + i % 4, :], ACT.Relu).then_inc(q.relu, 1)
                    act.wait_ge(q.relu, 8 * g + i + 1)
                    act.activation(u_h[:, ft, half * HALF:(half + 1) * HALF], relu[:, i % 2, :], ACT.Square).then_inc(q.u_hi, 1)

            def group(g, last):
                split_hi(act, q, mlp_chunk(n, g, *SPLITS[0]))
                split_hi(act, q, mlp_chunk(n, g, *SPLITS[1]))
                evacuate(g, 0, 1, 2)
                split_hi(act, q, mlp_chunk(n, g, *SPLITS[2]))
                split_hi(act, q, mlp_chunk(n, g, *SPLITS[3]))
                evacuate(g, 3)
                split_hi(act, q, mlp_chunk(n, g, *SPLITS[4]))
                split_hi(act, q, mlp_chunk(n, g, *SPLITS[5]))
                evacuate(g, 4, 5)
                if not last:
                    split_hi(act, q, mlp_chunk(n, g, *SPLITS[6]))
                evacuate(g, 6, 7)
                if not last:
                    split_hi(act, q, mlp_chunk(n, g, *SPLITS[7]))

            act.wait_ge(*x_stored(n - 1, TB - 2))
            act.wait_ge(*x_stored(n - 1, TB - 1))
            with act.Fori(0, MLP_GROUPS - 1) as g:
                group(g, False)
                act.wait_ge(q.down_done, 8 * g + 8)
            group(MLP_GROUPS - 1, True)

        def mlp_vector(dve, n, early):
            q = MLP[n]

            def evacuate(g, *numbers):
                for i in numbers:
                    ft, half = UP_ORDER[i]
                    cut = slice(half * HALF, (half + 1) * HALF)
                    dve.wait_ge(q.sq, 8 * g + i + 1)
                    dve.wait_ge(q.u_hi, 8 * g + i + 1)
                    dve.tensor_tensor(u_l[:, ft, cut], squared[:, i % 2, :], f32(u_h[:, ft, cut]), ALU.subtract).then_inc(q.u_lo, 1)

            def group(g, last):
                split_lo(dve, q, mlp_chunk(n, g, *SPLITS[0]), 8 * g + 3)
                split_lo(dve, q, mlp_chunk(n, g, *SPLITS[1]), 8 * g + 4)
                evacuate(g, 0, 1, 2)
                split_lo(dve, q, mlp_chunk(n, g, *SPLITS[2]), 8 * g + 5)
                split_lo(dve, q, mlp_chunk(n, g, *SPLITS[3]), 8 * g + 6)
                evacuate(g, 3)
                split_lo(dve, q, mlp_chunk(n, g, *SPLITS[4]), 8 * g + 7)
                split_lo(dve, q, mlp_chunk(n, g, *SPLITS[5]), 8 * g + 8)
                evacuate(g, 4, 5)
                if not last:
                    split_lo(dve, q, mlp_chunk(n, g, *SPLITS[6]), 8 * g + 9)
                evacuate(g, 6, 7)
                if not last:
                    split_lo(dve, q, mlp_chunk(n, g, *SPLITS[7]), 8 * g + 10)

            def add(g, tb, signal):
                dve.wait_ge(q.down_done, 8 * g + tb + 1)
                ins = dve.tensor_tensor(rows[:, tb, :], psf[:, tb % 2 * D:tb % 2 * D + D], rows[:, tb, :], ALU.add)
                ins.then_inc(signal, 1)

            dve.wait_ge(q.y_sum, 1)
            with dve.Fori(0, MLP_GROUPS - 1) as g:
                group(g, False)
                for tb in range(TB):
                    add(g, tb, q.y_sum)
            group(MLP_GROUPS - 1, True)
            dve.wait_ge(q.y_sum, 1 + TB * (MLP_GROUPS - 1))
            for step in range(STEPS):
                if step < TB:
                    add(MLP_GROUPS - 1, step, E.y_ready)
                end_vector(dve, n, step)
                if step in EARLY:
                    early(EARLY.index(step))

        def mlp_gpsimd(pool, n):
            q = MLP[n]
            pool.wait_ge(E.turned, pre(n - 1, TB))
            pool.memset(rows[:], 0.0).then_inc(q.y_sum, 1)

            def group(g):
                for i in range(2 * FG):
                    pool.wait_ge(q.relu, 8 * g + i + 1)
                    if i >= 2:
                        pool.wait_ge(q.u_lo, 8 * g + i - 1)
                    pool.tensor_tensor(squared[:, i % 2, :], relu[:, i % 2, :], relu[:, i % 2, :], ALU.mult).then_inc(q.sq, 1)

            with pool.Fori(0, MLP_GROUPS - 1) as g:
                group(g)
            group(MLP_GROUPS - 1)

        def mlp_tensor(pe, n):
            q = MLP[n]

            def up(g):
                for i, (ft, half) in enumerate(UP_ORDER):
                    if i in (0, 2):
                        pe.wait_ge(E.ht_lo, pre(n - 1, TB - 1 + half))
                    if ft < 2:
                        pe.wait_ge(q.w_lo, 8 * g + 1 + ft if isinstance(g, int) and g == 0 else 8 * g + ft + 1)
                    else:
                        pe.wait_ge(q.w_lo, 8 * g + (5 if ft == 2 else 7))
                    if i >= 4:
                        pe.wait_ge(q.relu, 8 * g + i - 3)
                    for k in range(KT):
                        mm = three_passes(pe, ps[:, 4 + i % 4, :], up_h[ft % 2][:, k, :], up_l[ft % 2][:, k, :],
                                          hth[:, k, half * HALF:(half + 1) * HALF], htl[:, k, half * HALF:(half + 1) * HALF],
                                          k == 0, k == KT - 1)
                    mm.then_inc(q.up_done, 1)

            def down(g, tb, bank_free):
                blk = slice(tb * P, (tb + 1) * P)
                if tb == 0:
                    pe.wait_ge(q.w_lo, 8 * g + 8)
                bank_free(tb)
                for ft in range(FG):
                    if tb == 0:
                        pe.wait_ge(q.u_lo, 8 * g + UP_ORDER.index((ft, 1)) + 1)
                    for c in range(D // HALF):
                        cut = slice(c * HALF, (c + 1) * HALF)
                        mm = three_passes(pe, ps[:, tb % 2 * 2 + c, :], u_h[:, ft, blk], u_l[:, ft, blk],
                                          dn_h[:, ft, cut], dn_l[:, ft, cut], ft == 0, ft == FG - 1)
                mm.then_inc(q.down_done, 1)

            with pe.Fori(0, MLP_GROUPS - 1) as g:
                up(g)

                def bank_free(tb):
                    pe.wait_ge(q.y_sum, 8 * g + tb if tb >= 2 else 8 * g + 1)

                for tb in range(TB):
                    down(g, tb, bank_free)
            up(MLP_GROUPS - 1)

            def last_bank_free(tb):
                if tb < 2:
                    pe.wait_ge(q.y_sum, 1 + TB * (MLP_GROUPS - 1))
                else:
                    pe.wait_ge(E.y_ready, post(n, tb - 1))

            for step in range(STEPS):
                if step < TB:
                    down(MLP_GROUPS - 1, step, last_bank_free)
                if step == 0:
                    pe.wait_ge(q.relu, 8 * MLP_GROUPS)
                end_tensor(pe, n, step - 3)

        wq_h = at("wq_h", [KT, QRANK], F32R, AT_W)
        wq_l = at("wq_l", [KT, QRANK], F32R, AT_W + 12 * KB)
        KVW = KVRANK + ROPE
        wkv_h = at("wkv_h", [KT, KVW], F32R, AT_W + 24 * KB)
        wkv_l = at("wkv_l", [KT, KVW], F32R, AT_W + 34 * KB)
        cq_h = at("cq_h", [QK, SEQ], F32R, AT_W + 44 * KB)
        cq_l = at("cq_l", [QK, SEQ], F32R, AT_W + 56 * KB)
        ckv_h = at("ckv_h", [KK, SEQ], F32R, AT_W)
        ckv_l = at("ckv_l", [KK, SEQ], F32R, AT_W + 8 * KB)
        krot_h = at("krot_h", [SEQ], F32R, AT_W + 16 * KB)
        krot_l = at("krot_l", [SEQ], F32R, AT_W + 20 * KB)
        o = AT_W + 68 * KB
        latent = at("latent", [2, QRANK], F32, o)
        krope = at("krope", [TB, ROPE], F32, o + 3 * KB)
        kturn = at("kturn", [TB, 2, ROPE], F32, o + 5 * KB)
        lgain = at("lgain", [QRANK + KVRANK], F32, o + 9 * KB)
        angle = at("angle", [TB, RH], F32, o + 12 * KB)
        turns = at("turns", [TB, RH], F32, o + 13 * KB)
        ktmp = at("ktmp", [4, TB, RH], F32, o + 14 * KB)
        sine = at("sine", [TB, RH], F32, o + 18 * KB)
        cosine = at("cosine", [TB, RH], F32, o + 19 * KB)
        pos_i = at("pos_i", [TB], I32, 6112)
        pos_f = at("pos_f", [TB], F32, 6144)
        freq = at("freq", [RH], F32, 6176)

        A = sems("mla_in", "raw_in0", "raw_in1", "raw_in2", "raw_in3", "w_hi", "w_lo", "small_in", "lgain_in", "product", "ss", "var",
                 "rstd", "normed", "krope", "turned", "hi", "lo", "trig", "reduced", "half_sine", "krot", "kturned", "k_hi", "k_lo")
        IN_CHUNKS = [(w_in_q, wq_h, wq_l, 0), (w_in_q, wq_h, wq_l, 1), (w_in_q, wq_h, wq_l, 2),
                     (w_in_kv, wkv_h, wkv_l, 0), (w_in_kv, wkv_h, wkv_l, 1), (w_in_kv, wkv_h, wkv_l, 2)]

        def flat(t):
            return t[:].rearrange("p a b -> p (a b)")

        def in_cut(c):
            w, hi, lo, i = IN_CHUNKS[c]
            return slice(i * D, min((i + 1) * D, w.shape[1]))

        def mla_in_loads(sp, chunks):
            for c in chunks:
                w, cut = IN_CHUNKS[c][0], in_cut(c)
                if c >= 4:
                    sp.wait_ge(A.w_lo, c - 3)
                sp.dma_start(raw[:, c % 4, 0:cut.stop - cut.start], w[:, cut]).then_inc((A.raw_in0, A.raw_in1, A.raw_in2, A.raw_in3)[c % 4], 16)

        def mla_in_small(sp):
            with nc.allow_non_contiguous_dma(reason="1024 positions, 4 bytes each"):
                sp.dma_start(pos_i[:], positions).then_inc(A.small_in, 16)
            sp.dma_start(freq[:], inv_freq[0:1, :].partition_broadcast(P)).then_inc(A.small_in, 16)
            sp.dma_start(lgain[:], qkv_gain[0:1, :].partition_broadcast(P)).then_inc(A.lgain_in, 16)

        def mla_in_split_hi(act, chunks):
            for c in chunks:
                w, hi, lo, i = IN_CHUNKS[c]
                cut = in_cut(c)
                act.wait_ge((A.raw_in0, A.raw_in1, A.raw_in2, A.raw_in3)[c % 4], 16 * (c // 4 + 1))
                act.activation(flat(hi)[:, cut], raw[:, c % 4, 0:cut.stop - cut.start], ACT.Copy).then_inc(A.w_hi, 1)

        def mla_in_split_lo(dve, chunks):
            for c in chunks:
                w, hi, lo, i = IN_CHUNKS[c]
                cut = in_cut(c)
                dve.wait_ge(A.w_hi, c + 1)
                dve.tensor_tensor(flat(lo)[:, cut], raw[:, c % 4, 0:cut.stop - cut.start], f32(flat(hi)[:, cut]),
                                  ALU.subtract).then_inc(A.w_lo, 1)

        def latent_of(i):
            return (QRANK, 0, QK, cq_h, cq_l) if i < TB else (KVRANK, QRANK, KK, ckv_h, ckv_l)

        def mla_in_scalar(act):
            for i in range(2 * TB + 1):
                if i < 2 * TB:
                    rank = latent_of(i)[0]
                    act.wait_ge(A.product, i + 1)
                    act.wait_ge(A.ss, i) if i else act.wait_ge(E.ss_x, pre(0, TB))
                    act.activation(junk[:, 0:rank], ps[:, i % 2, 0:rank], ACT.Square,
                                   accum_out=stat1[:, 0, i:i + 1]).then_inc(A.ss, 1)
                if i >= 1:
                    tb, (rank, _, tiles, hi, lo) = (i - 1) % TB, latent_of(i - 1)
                    act.wait_ge(A.turned, i)
                    if i - 1 == TB:
                        act.wait_ge(A.product, TB)
                    src = ps[:, 2 + (i - 1) % 2, 0:tiles * P].rearrange("p (f t) -> p f t", f=tiles)
                    act.activation(hi[:, :, tb * P:(tb + 1) * P], src, ACT.Copy).then_inc(A.hi, 1)
                if i == 4:
                    act.wait_ge(A.trig, 6)
                    act.activation(sine[:], angle[:], ACT.Sin).then_inc(A.half_sine, 1)
                    act.activation(cosine[:], angle[:], ACT.Sin, scale=0.5).then_inc(A.half_sine, 1)
            act.wait_ge(A.ss, 2 * TB)
            for c in range(2):
                act.wait_ge(A.kturned, c + 1)
                act.activation(krot_h[:, c * HALF:(c + 1) * HALF], ps[:, 4 + c, :], ACT.Copy).then_inc(A.k_hi, 1)

        def mla_in_gpsimd(pool):
            for i in range(2 * TB):
                rank = latent_of(i)[0]
                col = slice(i, i + 1)
                pool.wait_ge(A.ss, i + 1)
                pool.tensor_scalar(stat1[:, 1, col], stat1[:, 0, col], 1.0 / rank, NORM_EPS, ALU.mult, ALU.add).then_inc(A.var, 1)
                pool.wait_ge(A.var, i + 1)
                pool.tensor_tensor(stat1[:, 2, col], stat1[:, 1, col], power[:], ALU.pow).then_inc(A.rstd, 1)

        def mla_angles(dve):
            two_pi = 2 * np.pi
            parts, rest = [], two_pi
            for _ in range(3):
                e = np.floor(np.log2(rest)) - 7
                part = np.floor(rest / 2.0 ** e) * 2.0 ** e
                parts.append(float(part))
                rest -= part
            parts.append(float(np.float32(rest)))
            dve.wait_ge(A.small_in, 32)
            dve.tensor_copy(pos_f[:], pos_i[:]).then_inc(A.trig, 1)
            dve.wait_ge(A.trig, 1)
            for tb in range(TB):
                ins = dve.tensor_scalar(angle[:, tb, :], freq[:], pos_f[:, tb:tb + 1], None, ALU.mult)
            ins.then_inc(A.trig, 1)
            dve.wait_ge(A.trig, 2)
            half_ulp = float(1.5 * 2 ** 23)
            dve.tensor_scalar(turns[:], angle[:], float(1 / two_pi), half_ulp, ALU.mult, ALU.add).then_inc(A.trig, 1)
            dve.wait_ge(A.trig, 3)
            dve.tensor_scalar(turns[:], turns[:], half_ulp, None, ALU.subtract).then_inc(A.trig, 1)
            dve.wait_ge(A.trig, 4)
            for i, part in enumerate(parts):
                ins = dve.scalar_tensor_tensor(out=angle[:], in0=turns[:], scalar=-part, in1=angle[:], op0=ALU.mult, op1=ALU.add)
                if i < 3:
                    ins.then_inc(A.reduced, 1)
                    dve.wait_ge(A.reduced, i + 1)
            ins.then_inc(A.trig, 1)
            dve.wait_ge(A.trig, 5)
            pi = float(np.nextafter(np.float32(np.pi), np.float32(0)))
            dve.tensor_scalar(angle[:], angle[:], pi, -pi, ALU.min, ALU.max).then_inc(A.trig, 1)

        def mla_in_vector(dve):
            for i in range(2 * TB + 1):
                if i < 2 * TB:
                    tb, (rank, off, tiles, hi, lo) = i % TB, latent_of(i)
                    if i == 0:
                        dve.wait_ge(A.lgain_in, 16)
                    dve.wait_ge(A.rstd, i + 1)
                    if i >= 2:
                        dve.wait_ge(A.turned, i - 1)
                    dve.scalar_tensor_tensor(out=latent[:, i % 2, 0:rank], in0=ps[:, i % 2, 0:rank], scalar=stat1[:, 2, i:i + 1],
                                             in1=lgain[:, off:off + rank], op0=ALU.mult, op1=ALU.mult).then_inc(A.normed, 1)
                    if i >= TB:
                        dve.tensor_copy(krope[:, tb, :], ps[:, i % 2, KVRANK:KVW]).then_inc(A.krope, 1)
                if i >= 1:
                    tb, (rank, _, tiles, hi, lo) = (i - 1) % TB, latent_of(i - 1)
                    dst = slice(tb * P, (tb + 1) * P)
                    dve.wait_ge(A.hi, i)
                    src = ps[:, 2 + (i - 1) % 2, 0:tiles * P].rearrange("p (f t) -> p f t", f=tiles)
                    dve.tensor_tensor(lo[:, :, dst], src, f32(hi[:, :, dst]), ALU.subtract).then_inc(A.lo, 1)
                if i == 3:
                    mla_angles(dve)
                if i == 6:
                    dve.wait_ge(A.half_sine, 2)
                    dve.tensor_tensor(cosine[:], cosine[:], cosine[:], ALU.mult).then_inc(A.trig, 1)
                    dve.wait_ge(A.trig, 7)
                    dve.tensor_scalar(cosine[:], cosine[:], -2.0, 1.0, ALU.mult, ALU.add).then_inc(A.trig, 1)
                    dve.wait_ge(A.trig, 8)
            dve.wait_ge(A.krope, TB)
            k1, k2 = krope[:, :, 0:RH], krope[:, :, RH:ROPE]
            dve.tensor_tensor(ktmp[:, 0], k1, cosine[:], ALU.mult)
            dve.tensor_tensor(ktmp[:, 1], k2, sine[:], ALU.mult)
            dve.tensor_tensor(ktmp[:, 2], k2, cosine[:], ALU.mult)
            dve.tensor_tensor(ktmp[:, 3], k1, sine[:], ALU.mult).then_inc(A.krot, 1)
            dve.wait_ge(A.krot, 1)
            for c in range(2):
                dve.tensor_tensor(kturn[:, :, c, 0:RH], ktmp[:, 0], ktmp[:, 1], ALU.subtract)
                ins = dve.tensor_tensor(kturn[:, :, c, RH:ROPE], ktmp[:, 2], ktmp[:, 3], ALU.add)
            ins.then_inc(A.krot, 1)
            for c in range(2):
                cut = slice(c * HALF, (c + 1) * HALF)
                dve.wait_ge(A.k_hi, c + 1)
                dve.tensor_tensor(krot_l[:, cut], ps[:, 4 + c, :], f32(krot_h[:, cut]), ALU.subtract).then_inc(A.k_lo, 1)

        def mla_in_tensor(pe):
            def turn(i):
                tiles = latent_of(i)[2]
                pe.wait_ge(A.normed, i + 1)
                if i >= 2:
                    pe.wait_ge(A.lo, i - 1)
                for f in range(tiles):
                    mm = pe.transpose(ps[:, 2 + i % 2, f * P:(f + 1) * P], latent[:, i % 2, f * P:(f + 1) * P], ident[:])
                mm.then_inc(A.turned, 1)

            for i in range(2 * TB):
                tb = i % TB
                blk = slice(tb * P, (tb + 1) * P)
                if i < TB:
                    pe.wait_ge(E.ht_lo, pre(0, i + 1))
                    width, wh, wl = QRANK, wq_h, wq_l
                else:
                    width, wh, wl = KVW, wkv_h, wkv_l
                if i == 0:
                    pe.wait_ge(A.w_lo, 3)
                if i == TB:
                    pe.wait_ge(A.w_lo, 6)
                if i >= 2:
                    pe.wait_ge(A.normed, i - 1)
                    if i - 2 >= TB:
                        pe.wait_ge(A.krope, i - 2 - TB + 1)
                for k in range(KT):
                    mm = three_passes(pe, ps[:, i % 2, 0:width], hth[:, k, blk], htl[:, k, blk], wh[:, k, :], wl[:, k, :],
                                      k == 0, k == KT - 1)
                mm.then_inc(A.product, 1)
                if i >= 1:
                    turn(i - 1)
            turn(2 * TB - 1)
            pe.wait_ge(A.krot, 2)
            for c in range(2):
                for t in range(4):
                    tb = 4 * c + t
                    mm = pe.transpose(ps[:, 4 + c, t * P:(t + 1) * P], kturn[:, tb].rearrange("p a b -> p (a b)"), ident[:])
                mm.then_inc(A.kturned, 1)

        qn_h = [at(f"qn_h{s}", [SEQ], F32R, AT_HT + (16 * s + 0) * KB) for s in range(2)]
        qn_l = [at(f"qn_l{s}", [SEQ], F32R, AT_HT + (16 * s + 4) * KB) for s in range(2)]
        kn_h = [at(f"kn_h{s}", [SEQ], F32R, AT_HT + (16 * s + 8) * KB) for s in range(2)]
        kn_l = [at(f"kn_l{s}", [SEQ], F32R, AT_HT + (16 * s + 12) * KB) for s in range(2)]
        v_h = at("v_h", [TB, VDIM], F32R, AT_HT + 32 * KB)
        v_l = at("v_l", [TB, VDIM], F32R, AT_HT + 36 * KB)
        pt_h = at("pt_h", [2, HALF], F32R, AT_HT + 40 * KB)
        pt_l = at("pt_l", [2, HALF], F32R, AT_HT + 44 * KB)
        qrot = at("qrot", [GH, SEQ], F32R, AT_HT + 48 * KB)
        hw_h = [at(f"hw_h{s}", [HEADW], F32R, AT_W + (24 + 7 * s) * KB) for s in range(2)]
        hw_l = [at(f"hw_l{s}", [HEADW], F32R, AT_W + (24 + 7 * s) * KB + 4 * HEADW) for s in range(2)]
        rw_h = at("rw_h", [QK, GH * ROPE], F32R, AT_W + 38 * KB)
        rw_l = at("rw_l", [QK, GH * ROPE], F32R, AT_W + 41 * KB)
        probs = at("probs", [4, SEQ], F32, AT_W + 68 * KB)
        qr = at("qr", [2, GH, ROPE], F32, AT_W + 84 * KB)
        qsplit = at("qsplit", [2, GH, 2, ROPE], F32, AT_RAW + 12 * KB)
        qtmp = at("qtmp", [2, 2, GH, ROPE], F32, AT_W + 68 * KB)

        B = sems("mla", "head_in0", "head_in1", "rope_in", "hw_hi", "hw_lo", "rw_hi", "rw_lo", "qr",
                 "qsplit_hi", "qsplit", "projected", "aux_hi", "aux_free", "scores", "max", "neg_max", "exp", "inv", "probs",
                 "turned", "turned_hi", "turned_free", "pv")
        AUX = 4 + 8 * GH
        TURNS = TB + 12 * GH
        PVS = 12 * GH
        ROWSX = TB * GH

        def head_steps(j):
            steps = [("scores", 0), ("scores", 1), ("scores", 2), ("scores", 3)]
            if j < GH - 1:
                steps += [("q", 0), ("q", 1)]
            steps += [("scores", 4), ("turn", 0), ("scores", 5), ("turn", 1), ("pv", 0), ("scores", 6), ("turn", 2), ("pv", 1),
                      ("scores", 7), ("turn", 3), ("pv", 2), ("pv", 3)]
            if j < GH - 1:
                steps += [("k", 0), ("k", 1)]
            steps += [("turn", 4), ("turn", 5), ("pv", 4), ("turn", 6), ("pv", 5), ("turn", 7), ("pv", 6), ("turn", 8), ("pv", 7),
                      ("turn", 9), ("pv", 8), ("turn", 10), ("pv", 9), ("turn", 11), ("pv", 10), ("pv", 11)]
            if j < GH - 1:
                steps += [("v", 0), ("v", 1)]
            return steps

        FIRST_HEAD = [("q", 0), ("q", 1), ("k", 0), ("k", 1), ("v", 0), ("v", 1)]
        aux_order = [("rope", 0, t) for t in range(4)] + [(s, 0, i) for s, i in FIRST_HEAD]
        for j_ in range(GH):
            for s, i in head_steps(j_):
                if s in "qkv":
                    aux_order.append((s, j_ + 1, i))
                if s == "pv" and i in (3, 11):
                    aux_order.append(("out", j_, i // 8))
        assert len(aux_order) == AUX

        def aux(*use):
            return aux_order.index(use)

        projected_order = [u for u in aux_order if u[0] != "out"]
        proj_order = [u for u in aux_order if u[0] in "qkv"]
        NPROJ = len(projected_order)

        def projections(*use):
            return projected_order.index(use) + 1

        def key_block(i):
            half, kb = (0, i) if i < 4 else (1, i - 4)
            return half, kb, max(0, kb - 4 * half) * P

        def mla_loads(sp):
            sp.wait_ge(A.w_lo, 6)
            sp.dma_start(raw[:, 2, 0:ROPEW], w_rope[0]).then_inc(B.rope_in, 16)
            sp.dma_start(raw[:, 0, 0:HEADW], w_heads[0]).then_inc(B.head_in0, 16)
            sp.dma_start(raw[:, 1, 0:HEADW], w_heads[1]).then_inc(B.head_in1, 16)
            for g in range(GROUPS):
                if g + 1 < GROUPS:
                    sp.wait_ge(B.rw_lo, g + 1)
                    sp.dma_start(raw[:, 2, 0:ROPEW], w_rope[g + 1]).then_inc(B.rope_in, 16)
                for j in range(GH):
                    h = g * GH + j
                    if h + 2 < HEADS:
                        sp.wait_ge(B.hw_lo, h + 1)
                        sp.dma_start(raw[:, h % 2, 0:HEADW], w_heads[h + 2]).then_inc((B.head_in0, B.head_in1)[h % 2], 16)

        def aux_src(n):
            return ps[:, 6 + n % 2, :]

        def part_of(step, j, i):
            cut = slice(i * HALF, (i + 1) * HALF)
            if step == "q":
                return qn_h[j % 2][:, cut], qn_l[j % 2][:, cut]
            if step == "k":
                return kn_h[j % 2][:, cut], kn_l[j % 2][:, cut]
            return (v_h[:, 4 * i:4 * i + 4, :].rearrange("p a b -> p (a b)"), v_l[:, 4 * i:4 * i + 4, :].rearrange("p a b -> p (a b)"))

        def mla_scalar(act):
            def project(g, step, j, i):
                n = aux(step, j, i)
                act.wait_ge(B.projected, NPROJ * g + projections(step, j, i))
                act.activation(part_of(step, j, i)[0], aux_src(n), ACT.Copy).then_inc(B.aux_hi, 1)

            def head_weights(g, j):
                if j >= 2:
                    act.wait_ge(B.projected, NPROJ * g + projections("v", j - 2, 1))
                act.wait_ge((B.head_in0, B.head_in1)[j % 2], 32 * g + 16 * (j // 2 + 1))
                act.activation(hw_h[j % 2][:], raw[:, j % 2, 0:HEADW], ACT.Copy).then_inc(B.hw_hi, 1)

            act.wait_ge(A.product, 2 * TB)
            with act.Fori(0, GROUPS) as g:
                act.wait_ge(B.rope_in, 16 * g + 16)
                act.activation(flat(rw_h), raw[:, 2, 0:ROPEW], ACT.Copy).then_inc(B.rw_hi, 1)
                head_weights(g, 0)
                head_weights(g, 1)
                for t in range(4):
                    act.wait_ge(B.qr, 4 * g + t + 1)
                    if t > 0:
                        act.wait_ge(B.turned, TURNS * g + 2 * t)
                    hi = qsplit[:, :, :, 0, :].bitcast(F32R)
                    act.activation(hi, qr[:], ACT.Copy).then_inc(B.qsplit_hi, 1)
                for step, i in FIRST_HEAD:
                    project(g, step, 0, i)
                for j in range(GH):
                    for step, i in head_steps(j):
                        if step in "qkv":
                            project(g, step, j + 1, i)
                        elif step == "scores":
                            n = TB * j + i
                            nk = (i + 1) * P
                            act.wait_ge(B.neg_max, ROWSX * g + n + 1)
                            if i >= 4:
                                act.wait_ge(B.turned, TURNS * g + TB + 12 * j + i - 4 + 1)
                            elif j > 0:
                                act.wait_ge(B.turned, TURNS * g + TB + 12 * (j - 1) + 4 + 4 + i + 1)
                            col = slice(i, i + 1)
                            act.activation(probs[:, i % 4, 0:nk], psf[:, i % 2 * D:i % 2 * D + nk], ACT.Exp, bias=neg_max[:, col],
                                           scale=SCALE, accum_out=row_sum[:, col]).then_inc(B.exp, 1)
                        elif step == "turn":
                            half, kb, q0 = key_block(i)
                            n = TB + 12 * j + i
                            m = 12 * j + i
                            act.wait_ge(B.turned, TURNS * g + n + 1)
                            if m >= 2:
                                act.wait_ge(B.pv, PVS * g + m - 1)
                            act.activation(pt_h[:, m % 2, q0:HALF], ps[:, 4 + n % 2, q0:HALF], ACT.Copy).then_inc(B.turned_hi, 1)
                    if j + 2 < GH:
                        head_weights(g, j + 2)
                act.wait_ge(B.pv, PVS * g + PVS)

        def mla_vector(dve):
            def project(g, step, j, i):
                n = aux(step, j, i)
                m = proj_order.index((step, j, i))
                hi, lo = part_of(step, j, i)
                dve.wait_ge(B.aux_hi, len(proj_order) * g + m + 1)
                dve.tensor_tensor(lo, aux_src(n), f32(hi), ALU.subtract).then_inc(B.aux_free, 1)

            def head_weights(g, j):
                dve.wait_ge(B.hw_hi, GH * g + j + 1)
                dve.tensor_tensor(hw_l[j % 2][:], raw[:, j % 2, 0:HEADW], f32(hw_h[j % 2][:]), ALU.subtract).then_inc(B.hw_lo, 1)

            def normalise(g, j, i):
                n = TB * j + i
                nk = (i + 1) * P
                col = slice(i, i + 1)
                dve.wait_ge(B.exp, ROWSX * g + n + 1)
                dve.reciprocal(row_inv[:, col], row_sum[:, col]).then_inc(B.inv, 1)
                dve.wait_ge(B.inv, ROWSX * g + n + 1)
                dve.tensor_scalar(probs[:, i % 4, 0:nk], probs[:, i % 4, 0:nk], row_inv[:, col], None, ALU.mult).then_inc(B.probs, 1)

            with dve.Fori(0, GROUPS) as g:
                dve.wait_ge(B.rw_hi, g + 1)
                dve.tensor_tensor(flat(rw_l), raw[:, 2, 0:ROPEW], f32(flat(rw_h)), ALU.subtract).then_inc(B.rw_lo, 1)
                head_weights(g, 0)
                head_weights(g, 1)
                for t in range(4):
                    dve.wait_ge(B.projected, NPROJ * g + t + 1)
                    src = aux_src(t).rearrange("p (b h r) -> p b h r", b=2, h=GH)
                    for b in range(2):
                        tb = 2 * t + b
                        cos = cosine[:, tb:tb + 1, :].broadcast_to([P, GH, RH])
                        sin = sine[:, tb:tb + 1, :].broadcast_to([P, GH, RH])
                        q1, q2 = src[:, b, :, 0:RH], src[:, b, :, RH:ROPE]
                        dve.tensor_tensor(qtmp[:, 0, b, :, 0:RH], q1, cos, ALU.mult)
                        dve.tensor_tensor(qtmp[:, 0, b, :, RH:ROPE], q2, cos, ALU.mult)
                        dve.tensor_tensor(qtmp[:, 1, b, :, 0:RH], q2, sin, ALU.mult)
                        ins = dve.tensor_tensor(qtmp[:, 1, b, :, RH:ROPE], q1, sin, ALU.mult)
                    ins.then_inc(B.aux_free, 1)
                    dve.wait_ge(B.aux_free, AUX * g + t + 1)
                    if t > 0:
                        dve.wait_ge(B.qsplit_hi, 4 * g + t)
                    dve.tensor_tensor(qr[:, :, :, 0:RH], qtmp[:, 0, :, :, 0:RH], qtmp[:, 1, :, :, 0:RH], ALU.subtract)
                    dve.tensor_tensor(qr[:, :, :, RH:ROPE], qtmp[:, 0, :, :, RH:ROPE], qtmp[:, 1, :, :, RH:ROPE], ALU.add).then_inc(B.qr, 1)
                    dve.wait_ge(B.qsplit_hi, 4 * g + t + 1)
                    dve.tensor_tensor(qsplit[:, :, :, 1, :], qr[:], qsplit[:, :, :, 0, :], ALU.subtract).then_inc(B.qsplit, 1)
                    for b in range(2):
                        n = 2 * t + b
                        dve.wait_ge(B.turned, TURNS * g + n + 1)
                        src = ps[:, 4 + n % 2, :].rearrange("p (h t) -> p h t", h=GH)
                        dve.tensor_copy(qrot[:, :, n * P:(n + 1) * P], src).then_inc(B.turned_free, 1)
                for step, i in FIRST_HEAD:
                    project(g, step, 0, i)
                for j in range(GH):
                    pending = None
                    for step, i in head_steps(j):
                        if step in "qkv":
                            if pending is not None:
                                normalise(g, j, pending)
                                pending = None
                            project(g, step, j + 1, i)
                        elif step == "scores":
                            n = TB * j + i
                            nk = (i + 1) * P
                            dve.wait_ge(B.scores, ROWSX * g + n + 1)
                            col = slice(i, i + 1)
                            dve.tensor_reduce(row_max[:, col], psf[:, i % 2 * D:i % 2 * D + nk], AX.X, ALU.max).then_inc(B.max, 1)
                            dve.wait_ge(B.max, ROWSX * g + n + 1)
                            dve.tensor_scalar(neg_max[:, col], row_max[:, col], -SCALE, None, ALU.mult).then_inc(B.neg_max, 1)
                            if pending is not None:
                                normalise(g, j, pending)
                            pending = i
                        elif step == "turn":
                            if pending == TB - 1:
                                normalise(g, j, pending)
                                pending = None
                            half, kb, q0 = key_block(i)
                            n = TB + 12 * j + i
                            m = 12 * j + i
                            dve.wait_ge(B.turned_hi, PVS * g + m + 1)
                            dve.tensor_tensor(pt_l[:, m % 2, q0:HALF], ps[:, 4 + n % 2, q0:HALF], f32(pt_h[:, m % 2, q0:HALF]),
                                              ALU.subtract).then_inc(B.turned_free, 1)
                        elif step == "pv" and i in (3, 11):
                            n = aux("out", j, i // 8)
                            dve.wait_ge(B.pv, PVS * g + 12 * j + i + 1)
                            dve.tensor_copy(aT[:, bass.ds(g * (GH * SEQ) + j * SEQ + i // 8 * HALF, HALF)], aux_src(n)).then_inc(B.aux_free, 1)
                    if j + 2 < GH:
                        head_weights(g, j + 2)

        def mla_tensor(pe):
            def bank_wait(g, n):
                if n >= 2:
                    pe.wait_ge(B.aux_free, AUX * g + n - 1)

            def project(g, step, j, i):
                n = aux(step, j, i)
                bank_wait(g, n)
                hh, hl = hw_h[j % 2], hw_l[j % 2]
                pe.wait_ge(B.hw_lo, GH * g + j + 1)
                cut = slice(i * HALF, (i + 1) * HALF)
                if step == "q":
                    for k in range(QK):
                        w = slice(k * P, (k + 1) * P)
                        mm = three_passes(pe, aux_src(n), hh[:, w], hl[:, w], cq_h[:, k, cut], cq_l[:, k, cut], k == 0, k == QK - 1)
                elif step == "k":
                    for k in range(KK):
                        w = slice((QK + k) * P, (QK + k + 1) * P)
                        mm = three_passes(pe, aux_src(n), hh[:, w], hl[:, w], ckv_h[:, k, cut], ckv_l[:, k, cut], k == 0, k == KK - 1)
                else:
                    for t in range(4):
                        blk = slice((4 * i + t) * P, (4 * i + t + 1) * P)
                        for k in range(KK):
                            w = slice((QK + KK + k) * P, (QK + KK + k + 1) * P)
                            mm = three_passes(pe, aux_src(n)[:, t * P:(t + 1) * P], ckv_h[:, k, blk], ckv_l[:, k, blk],
                                              hh[:, w], hl[:, w], k == 0, k == KK - 1)
                mm.then_inc(B.projected, 1)

            pe.wait_ge(A.lo, 2 * TB)
            pe.wait_ge(A.k_lo, 2)
            with pe.Fori(0, GROUPS) as g:
                pe.wait_ge(B.rw_lo, g + 1)

                def rope_product(t):
                    bank_wait(g, t)
                    for b in range(2):
                        blk = slice((2 * t + b) * P, (2 * t + b + 1) * P)
                        for k in range(QK):
                            mm = three_passes(pe, aux_src(t)[:, b * 256:(b + 1) * 256], cq_h[:, k, blk], cq_l[:, k, blk],
                                              rw_h[:, k, :], rw_l[:, k, :], k == 0, k == QK - 1)
                    mm.then_inc(B.projected, 1)

                rope_product(0)
                for t in range(4):
                    if t < 3:
                        rope_product(t + 1)
                    pe.wait_ge(B.qsplit, 4 * g + t + 1)
                    for b in range(2):
                        n = 2 * t + b
                        if n >= 2:
                            pe.wait_ge(B.turned_free, TURNS * g + n - 1)
                        for h in range(GH):
                            mm = pe.transpose(ps[:, 4 + n % 2, h * P:(h + 1) * P], qsplit[:, b, h].rearrange("p a b -> p (a b)"), ident[:])
                        mm.then_inc(B.turned, 1)
                for step, i in FIRST_HEAD:
                    project(g, step, 0, i)
                pe.wait_ge(B.turned_free, TURNS * g + TB)
                for j in range(GH):
                    qh, ql, kh, kl = qn_h[j % 2], qn_l[j % 2], kn_h[j % 2], kn_l[j % 2]
                    pe.wait_ge(B.aux_free, AUX * g + aux("k", j, 1) + 1)
                    for step, i in head_steps(j):
                        if step in "qkv":
                            project(g, step, j + 1, i)
                        elif step == "scores":
                            n = TB * j + i
                            blk = slice(i * P, (i + 1) * P)
                            if n >= 2:
                                pe.wait_ge(B.exp, ROWSX * g + n - 1)
                            for c in range(i // 4 + 1):
                                width = min(HALF, (i + 1) * P - c * HALF)
                                dst = ps[:, i % 2 * 2 + c, 0:width]
                                keys = slice(c * HALF, c * HALF + width)
                                three_passes(pe, dst, qh[:, blk], ql[:, blk], kh[:, keys], kl[:, keys], True, False)
                                pe.matmul(dst, qrot[:, j, blk], krot_h[:, keys], start=False, stop=False)
                                mm = pe.matmul(dst, qrot[:, j, blk], krot_l[:, keys], start=False, stop=c < i // 4)
                            mm = pe.matmul(ps[:, i % 2 * 2 + c, width - P:width], identr[:], maskr[:], start=False, stop=True)
                            mm.then_inc(B.scores, 1)
                        elif step == "turn":
                            half, kb, q0 = key_block(i)
                            n = TB + 12 * j + i
                            pe.wait_ge(B.probs, ROWSX * g + TB * j + 4 * half + 4)
                            pe.wait_ge(B.turned_free, TURNS * g + n - 1)
                            for q in range(q0 // P, 4):
                                mm = pe.transpose(ps[:, 4 + n % 2, q * P:(q + 1) * P], probs[:, q, kb * P:(kb + 1) * P], ident[:])
                            mm.then_inc(B.turned, 1)
                        else:
                            half, kb, q0 = key_block(i)
                            m = 12 * j + i
                            n = aux("out", j, half)
                            if kb == 0:
                                bank_wait(g, n)
                                pe.wait_ge(B.aux_free, AUX * g + aux("v", j, 1) + 1)
                            pe.wait_ge(B.turned_free, TURNS * g + TB + m + 1)
                            mm = three_passes(pe, aux_src(n)[:, q0:HALF], v_h[:, kb, :], v_l[:, kb, :], pt_h[:, m % 2, q0:HALF],
                                              pt_l[:, m % 2, q0:HALF], kb == 0, i in (3, 11))
                            mm.then_inc(B.pv, 1)
                pe.wait_ge(B.aux_free, AUX * g + AUX)

        rec_h = at("rec_h", [KT, P], F32R, AT_W + 72 * KB)
        rec_l = at("rec_l", [KT, P], F32R, AT_W + 76 * KB)
        gw_h = at("gw_h", [KT, P], F32R, AT_W + 64 * KB)
        gw_l = at("gw_l", [KT, P], F32R, AT_W + 68 * KB)
        ax_h = at("ax_h", [2, P], F32R, AT_W + 8 * KB)
        ax_l = at("ax_l", [2, P], F32R, AT_W + 9 * KB)
        xc_h = at("xc_h", [SEQ], F32R, AT_W + 10 * KB)
        xc_l = at("xc_l", [SEQ], F32R, AT_W + 14 * KB)
        PAD = CONV - 1
        rec = at("rec", [SEQ + 8], F32, AT_W + 18 * KB)
        o = AT_W + 23 * KB
        xc = at("xc", [SEQ], F32, o)
        gate = at("gate", [SEQ], F32, o + 4 * KB)
        rgate = at("rgate", [SEQ], F32, o + 8 * KB)
        igate = at("igate", [SEQ], F32, o + 12 * KB)
        tanh = at("tanh", [SEQ], F32, o + 16 * KB)
        root = at("root", [SEQ], F32, o + 20 * KB)
        winv = at("winv", [SEQ], F32, o + 24 * KB)
        wtmp = at("wtmp", [SEQ], F32, o + 28 * KB)
        agate = at("agate", [SEQ], F32, o + 32 * KB)
        bgate = at("bgate", [SEQ], F32, o + 36 * KB)
        vec = at("vec", [CH, VEC], F32, 6304)
        tilev = at("tilev", [VEC], F32, 6624)
        dtmp = at("dtmp", [5, CH], F32, 6688)
        V_CONV_B, V_B_A, V_B_X, V_LAM, V_DECAY, V_DECAY2 = range(CONV, VEC)
        L = sems("lru", "vec_in", "raw_in0", "raw_in1", "raw_in2", "w_hi", "w_lo", "setup", "padded", "tile_vec", "rec_done", "gate_done",
                 "ax_done", "rec_copied", "gated", "conv", "xc_hi", "xc_lo", "sigmoid", "tanh", "estimate", "root", "inv", "decay", "u",
                 "ix", "b", "scan", "out")

        def lru_loads_first(sp, kinds):
            if "rec" in kinds:
                sp.dma_start(raw[:, 0, :], w_rec[0]).then_inc(L.raw_in0, 16)
            if "gate" in kinds:
                sp.dma_start(raw[:, 1, :], w_gate[0]).then_inc(L.raw_in1, 16)
            if "ax" in kinds:
                sp.dma_start(raw[:, 2, 0:2 * P], w_ax[0]).then_inc(L.raw_in2, 16)

        def lru_sync(sp):
            with sp.Fori(0, CH - 1) as n:
                row = sp.snap(n + 1)
                sp.wait_ge(L.w_lo, 3 * n + 1)
                sp.dma_start(raw[:, 0, :], w_rec[row]).then_inc(L.raw_in0, 16)
                sp.wait_ge(L.w_lo, 3 * n + 2)
                sp.dma_start(raw[:, 1, :], w_gate[row]).then_inc(L.raw_in1, 16)
                sp.wait_ge(L.w_lo, 3 * n + 3)
                sp.dma_start(raw[:, 2, 0:2 * P], w_ax[row]).then_inc(L.raw_in2, 16)

        LRU_WEIGHTS = {"rec": (0, rec_h, rec_l), "gate": (1, gw_h, gw_l), "ax": (2, ax_h, ax_l)}

        def lru_split_hi(act, n, which):
            slot, hi, lo = LRU_WEIGHTS[which]
            act.wait_ge((L.raw_in0, L.raw_in1, L.raw_in2)[slot], 16 * n + 16)
            act.activation(flat(hi), raw[:, slot, 0:flat(hi).shape[1]], ACT.Copy).then_inc(L.w_hi, 1)

        def lru_split_lo(dve, n, which):
            slot, hi, lo = LRU_WEIGHTS[which]
            dve.wait_ge(L.w_hi, 3 * n + slot + 1)
            dve.tensor_tensor(flat(lo), raw[:, slot, 0:flat(hi).shape[1]], f32(flat(hi)), ALU.subtract).then_inc(L.w_lo, 1)

        BANKS_REC, BANKS_GATE, BANKS_R, BANKS_I = 0, 2, 4, 6

        def pair(b):
            return psf[:, b * HALF:b * HALF + D]

        def tile_vec(k):
            return tilev[:, k:k + 1]

        def lru_scalar(act):
            act.wait_ge(L.vec_in, 16)
            act.activation(dtmp[:, 0, :], vec[:, :, V_LAM], ACT.Abs).then_inc(L.setup, 1)
            act.wait_ge(L.setup, 1)
            act.activation(dtmp[:, 1, :], dtmp[:, 0, :], ACT.Exp, scale=-1.0).then_inc(L.setup, 1)
            lru_split_hi(act, 0, "ax")

            def tile(n, last):
                act.wait_ge(L.rec_done, n + 1)
                act.activation(rec[:, PAD:PAD + SEQ], pair(BANKS_REC), ACT.Copy).then_inc(L.rec_copied, 1)
                if not last:
                    lru_split_hi(act, n + 1, "rec")
                act.wait_ge(L.conv, CONV * n + CONV)
                act.activation(xc_h[:], xc[:], ACT.Copy).then_inc(L.xc_hi, 1)
                act.wait_ge(L.gate_done, n + 1)
                act.activation(gate[:], pair(BANKS_GATE), ACT.Gelu_apprx_tanh).then_inc(L.gated, 1)
                if not last:
                    lru_split_hi(act, n + 1, "gate")
                act.wait_ge(L.ax_done, n + 1)
                act.activation(rgate[:], pair(BANKS_R), ACT.Sigmoid, bias=tile_vec(V_B_A)).then_inc(L.sigmoid, 1)
                act.activation(igate[:], pair(BANKS_I), ACT.Sigmoid, bias=tile_vec(V_B_X)).then_inc(L.sigmoid, 1)
                act.wait_ge(L.sigmoid, 2 * n + 1)
                act.activation(tanh[:], rgate[:], ACT.Tanh, scale=tile_vec(V_DECAY)).then_inc(L.tanh, 1)
                act.activation(winv[:], rgate[:], ACT.Exp, scale=tile_vec(V_DECAY2)).then_inc(L.estimate, 1)
                act.wait_ge(L.tanh, n + 1)
                act.activation(root[:], tanh[:], ACT.Sqrt, scale=4.0).then_inc(L.root, 1)
                if not last:
                    lru_split_hi(act, n + 1, "ax")

            with act.Fori(0, CH - 1) as n:
                tile(n, False)
            tile(CH - 1, True)

        def lru_setup_vector(dve):
            chain = 2

            def after(ins):
                nonlocal chain
                ins.then_inc(L.setup, 1)
                chain += 1
                dve.wait_ge(L.setup, chain)

            e, s, s2, p = dtmp[:, 1, :], dtmp[:, 2, :], dtmp[:, 3, :], dtmp[:, 4, :]
            dve.wait_ge(L.setup, 2)
            after(dve.tensor_scalar(p, e, 2.0, None, ALU.add))
            after(dve.reciprocal(s, p))
            after(dve.tensor_tensor(s, s, e, ALU.mult))
            after(dve.tensor_tensor(s2, s, s, ALU.mult))
            after(dve.tensor_scalar(p, s2, 1.0 / 17, None, ALU.mult))
            for k in range(15, 1, -2):
                after(dve.scalar_tensor_tensor(out=p, in0=p, scalar=1.0 / k, in1=s2, op0=ALU.add, op1=ALU.mult))
            after(dve.scalar_tensor_tensor(out=p, in0=p, scalar=1.0, in1=s, op0=ALU.add, op1=ALU.mult))
            after(dve.tensor_scalar(s, vec[:, :, V_LAM], -1.0, 0.0, ALU.mult, ALU.max))
            after(dve.scalar_tensor_tensor(out=p, in0=p, scalar=2.0, in1=s, op0=ALU.mult, op1=ALU.add))
            after(dve.tensor_scalar(vec[:, :, V_DECAY], p, LRU_C / 2, None, ALU.mult))
            after(dve.tensor_scalar(vec[:, :, V_DECAY2], p, -LRU_C, None, ALU.mult))

        vec_flat = vec[:].rearrange("p a b -> p (a b)")

        def lru_vector(dve):
            lru_setup_vector(dve)
            lru_split_lo(dve, 0, "ax")
            dve.wait_ge(L.padded, 1)

            def tile(n, last):
                dve.tensor_copy(tilev[:], vec_flat[:, bass.ds(n * VEC, VEC)] if not last else vec_flat[:, n * VEC:(n + 1) * VEC]).then_inc(L.tile_vec, 1)
                dve.wait_ge(L.tile_vec, n + 1)
                dve.wait_ge(L.rec_copied, n + 1)
                dve.tensor_scalar(xc[:], rec[:, PAD:PAD + SEQ], tile_vec(CONV - 1), tile_vec(V_CONV_B), ALU.mult, ALU.add).then_inc(L.conv, 1)
                for k in range(CONV - 1):
                    dve.wait_ge(L.conv, CONV * n + k + 1)
                    dve.scalar_tensor_tensor(out=xc[:], in0=rec[:, k:k + SEQ], scalar=tile_vec(k), in1=xc[:], op0=ALU.mult,
                                             op1=ALU.add).then_inc(L.conv, 1)
                if not last:
                    lru_split_lo(dve, n + 1, "rec")
                dve.wait_ge(L.xc_hi, n + 1)
                dve.tensor_tensor(xc_l[:], xc[:], f32(xc_h[:]), ALU.subtract).then_inc(L.xc_lo, 1)
                if not last:
                    lru_split_lo(dve, n + 1, "gate")
                dve.wait_ge(L.estimate, n + 1)
                dve.tensor_scalar(winv[:], winv[:], 0.5, 0.5, ALU.mult, ALU.add).then_inc(L.inv, 1)
                dve.wait_ge(L.inv, 3 * n + 1)
                dve.wait_ge(L.tanh, n + 1)
                dve.scalar_tensor_tensor(out=wtmp[:], in0=tanh[:], scalar=1.0, in1=winv[:], op0=ALU.add, op1=ALU.mult).then_inc(L.inv, 1)
                dve.wait_ge(L.inv, 3 * n + 2)
                dve.scalar_tensor_tensor(out=winv[:], in0=wtmp[:], scalar=2.0, in1=winv[:], op0=ALU.subtract, op1=ALU.mult).then_inc(L.inv, 1)
                dve.wait_ge(L.inv, 3 * n + 3)
                dve.wait_ge(L.root, n + 1)
                dve.scalar_tensor_tensor(out=bgate[:], in0=root[:], scalar=-1.0, in1=winv[:], op0=ALU.mult, op1=ALU.mult).then_inc(L.u, 1)
                dve.tensor_tensor(agate[:], tanh[:], winv[:], ALU.mult).then_inc(L.decay, 1)
                dve.wait_ge(L.decay, 2 * n + 1)
                dve.tensor_scalar(agate[:], agate[:], 2.0, 1.0, ALU.mult, ALU.add).then_inc(L.decay, 1)
                if not last:
                    lru_split_lo(dve, n + 1, "ax")
                dve.wait_ge(L.decay, 2 * n + 2)
                dve.wait_ge(L.b, n + 1)
                dve.tensor_tensor_scan(rgate[:], agate[:], bgate[:], 0.0, ALU.mult, ALU.add).then_inc(L.scan, 1)
                dve.wait_ge(L.scan, n + 1)
                dve.wait_ge(L.gated, n + 1)
                dst = aT[:, n * SEQ:(n + 1) * SEQ] if last else aT[:, bass.ds(n * SEQ, SEQ)]
                dve.tensor_tensor(dst, gate[:], rgate[:], ALU.mult).then_inc(L.out, 1)

            with dve.Fori(0, CH - 1) as n:
                tile(n, False)
            tile(CH - 1, True)

        def lru_gpsimd(pool):
            pool.wait_ge(MLP[2].down_done, TB * MLP_GROUPS)
            pool.memset(rec[:, 0:PAD], 0.0).then_inc(L.padded, 1)

            def tile(n):
                pool.wait_ge(L.sigmoid, 2 * n + 2)
                pool.tensor_tensor(igate[:], igate[:], xc[:], ALU.mult).then_inc(L.ix, 1)
                pool.wait_ge(L.u, n + 1)
                pool.wait_ge(L.ix, n + 1)
                pool.tensor_tensor(bgate[:], bgate[:], igate[:], ALU.mult).then_inc(L.b, 1)

            with pool.Fori(0, CH) as n:
                tile(n)

        def lru_tensor(pe):
            def project(n, which, halves):
                slot, wh, wl = LRU_WEIGHTS[which]
                banks, done = ((BANKS_REC, L.rec_done), (BANKS_GATE, L.gate_done))[slot]
                pe.wait_ge(L.w_lo, 3 * n + slot + 1)
                for half in halves:
                    cut = slice(half * HALF, (half + 1) * HALF)
                    for k in range(KT):
                        mm = three_passes(pe, ps[:, banks + half, :], wh[:, k, :], wl[:, k, :], hth[:, k, cut], htl[:, k, cut],
                                          k == 0, k == KT - 1)
                if 1 in halves:
                    mm.then_inc(done, 1)

            def gates(n):
                pe.wait_ge(L.w_lo, 3 * n + 3)
                pe.wait_ge(L.xc_lo, n + 1)
                for g, banks in ((0, BANKS_R), (1, BANKS_I)):
                    for half in range(2):
                        cut = slice(half * HALF, (half + 1) * HALF)
                        mm = three_passes(pe, ps[:, banks + half, :], ax_h[:, g, :], ax_l[:, g, :], xc_h[:, cut], xc_l[:, cut], True, True)
                mm.then_inc(L.ax_done, 1)

            pe.wait_ge(E.ht_lo, pre(2, TB // 2))
            project(0, "rec", (0,))
            project(0, "gate", (0,))
            pe.wait_ge(E.ht_lo, pre(2, TB))
            project(0, "rec", (1,))
            project(0, "gate", (1,))
            gates(0)
            with pe.Fori(1, CH) as n:
                project(n, "rec", (0, 1))
                project(n, "gate", (0, 1))
                gates(n)

        C = sems("const", "zeroed", "ident", "mask", "power", "rounded")
        block = ctx.enter_context(nc.Block())

        @block.sync
        def _(sp):
            end_loads(sp, 0)
            mla_in_small(sp)
            mla_in_loads(sp, range(4))
            mla_in_loads(sp, range(4, 6))
            sp.dma_start(vec[:, :, 0:VEC_IN], lru_vec).then_inc(L.vec_in, 16)
            mla_loads(sp)
            sp.wait_ge(B.hw_lo, HEADS)
            sp.wait_ge(B.pv, PVS * GROUPS)
            proj_loads(sp, 1, w_o, range(2))
            proj_loads(sp, 1, w_o, range(2, KT))
            sp.wait_ge(PROJ[1].w_lo, KT)
            end_loads(sp, 1)
            mlp_loads_first(sp, 2, 0, ("up",))
            end_sync(sp, 1)
            mlp_loads_first(sp, 2, 0, ("down",))
            mlp_sync(sp, 2, 0)
            sp.wait_ge(MLP[2].w_lo, 8 * MLP_GROUPS)
            sp.wait_ge(MLP[2].u_lo, 8 * MLP_GROUPS)
            end_loads(sp, 2)
            lru_loads_first(sp, ("rec", "gate"))
            end_sync(sp, 2)
            lru_loads_first(sp, ("ax",))
            lru_sync(sp)
            sp.wait_ge(L.w_lo, 3 * CH)
            proj_loads(sp, 3, w_out, range(4))
            proj_loads(sp, 3, w_out, range(4, KT))
            sp.wait_ge(PROJ[3].w_lo, KT)
            end_loads(sp, 3)
            mlp_loads_first(sp, 4, 1, ("up",))
            end_sync(sp, 3)
            mlp_loads_first(sp, 4, 1, ("down",))
            mlp_sync(sp, 4, 1)
            sp.wait_ge(MLP[4].w_lo, 8 * MLP_GROUPS)
            sp.wait_ge(MLP[4].u_lo, 8 * MLP_GROUPS)
            end_loads(sp, 4)
            end_sync(sp, 4)

        @block.scalar
        def _(act):
            for step in range(STEPS):
                end_scalar(act, 0, step, None)
                if step in (3, 5, 7):
                    mla_in_split_hi(act, [(step - 3) // 2])
            act.wait_ge(C.mask, 1)
            act.activation(identr[:], ident[:], ACT.Copy).then_inc(C.rounded, 1)
            act.activation(maskr[:], mask[:], ACT.Copy).then_inc(C.rounded, 1)
            mla_in_split_hi(act, range(3, 6))
            mla_in_scalar(act)
            mla_scalar(act)
            proj_scalar(act, 1, B.pv, PVS * GROUPS, B.aux_free, AUX * GROUPS)
            for step in range(STEPS):
                end_scalar(act, 1, step, PROJ[1].y_done)
                if step in EARLY:
                    split_hi(act, MLP[2], mlp_first_up(2, EARLY.index(step)))
            mlp_scalar(act, 2)
            for step in range(STEPS):
                end_scalar(act, 2, step, None)
                if step in EARLY:
                    lru_split_hi(act, 0, ("rec", "gate")[EARLY.index(step)])
            lru_scalar(act)
            proj_scalar(act, 3, L.out, CH, L.out, CH)
            for step in range(STEPS):
                end_scalar(act, 3, step, PROJ[3].y_done)
                if step in EARLY:
                    split_hi(act, MLP[4], mlp_first_up(4, EARLY.index(step)))
            mlp_scalar(act, 4)
            for step in range(STEPS):
                end_scalar(act, 4, step, None)

        @block.vector
        def _(dve):
            for step in range(STEPS):
                end_vector(dve, 0, step)
                if step in (3, 5, 7):
                    mla_in_split_lo(dve, [(step - 3) // 2])
            mla_in_split_lo(dve, range(3, 6))
            mla_in_vector(dve)
            mla_vector(dve)
            proj_vector(dve, 1)
            for step in range(STEPS):
                end_vector(dve, 1, step)
                if step in EARLY:
                    split_lo(dve, MLP[2], mlp_first_up(2, EARLY.index(step)), EARLY.index(step) + 1)
            mlp_vector(dve, 2, lambda i: lru_split_lo(dve, 0, ("rec", "gate")[i]))
            lru_vector(dve)
            proj_vector(dve, 3)
            for step in range(STEPS):
                end_vector(dve, 3, step)
                if step in EARLY:
                    split_lo(dve, MLP[4], mlp_first_up(4, EARLY.index(step)), EARLY.index(step) + 1)
            mlp_vector(dve, 4, lambda i: None)

        @block.gpsimd
        def _(pool):
            pool.memset(ident[:], 0.0).then_inc(C.zeroed, 1)
            pool.memset(mask[:], 0.0).then_inc(C.zeroed, 1)
            pool.memset(power[:], -0.5).then_inc(C.power, 1)
            pool.wait_ge(C.zeroed, 2)
            pool.affine_select(out=ident[:], in_=ident[:], compare_op=ALU.not_equal, fill=1.0, base=0, pattern=[[-1, P]],
                               channel_multiplier=1).then_inc(C.ident, 1)
            pool.affine_select(out=mask[:], in_=mask[:], compare_op=ALU.is_ge, fill=MASKED, base=0, pattern=[[-1, P]],
                               channel_multiplier=1).then_inc(C.mask, 1)
            pool.wait_ge(C.power, 1)
            for step in range(STEPS):
                end_gpsimd(pool, 0, step)
            mla_in_gpsimd(pool)
            for step in range(STEPS):
                end_gpsimd(pool, 1, step)
            mlp_gpsimd(pool, 2)
            for step in range(STEPS):
                end_gpsimd(pool, 2, step)
            lru_gpsimd(pool)
            for step in range(STEPS):
                end_gpsimd(pool, 3, step)
            mlp_gpsimd(pool, 4)
            for step in range(STEPS):
                end_gpsimd(pool, 4, step)

        @block.tensor
        def _(pe):
            pe.wait_ge(C.ident, 1)
            for step in range(STEPS):
                end_tensor(pe, 0, step - 3)
            mla_in_tensor(pe)
            pe.wait_ge(C.rounded, 2)
            mla_tensor(pe)
            proj_tensor(pe, 1)
            mlp_tensor(pe, 2)
            lru_tensor(pe)
            proj_tensor(pe, 3)
            mlp_tensor(pe, 4)


def packed(inputs):
    f = lambda name: np.asarray(inputs[name])

    def by_partition(w):
        return w.reshape(-1, P, w.shape[1]).transpose(1, 0, 2).reshape(P, -1)

    w_in = f("mla_w_in")[0]
    uq = f("mla_w_uq")[0].reshape(QK, P, HEADS, NOPE + ROPE)
    ukv = f("mla_w_ukv")[0].reshape(KK, P, HEADS, NOPE + VDIM)
    heads = np.concatenate([
        uq[..., :NOPE].transpose(2, 1, 0, 3).reshape(HEADS, P, QK * NOPE),
        ukv[..., :NOPE].transpose(2, 1, 0, 3).reshape(HEADS, P, KK * NOPE),
        ukv[..., NOPE:].transpose(2, 1, 0, 3).reshape(HEADS, P, KK * VDIM)], axis=2)
    rope = uq[..., NOPE:].reshape(QK, P, GROUPS, GH, ROPE).transpose(2, 1, 0, 3, 4).reshape(GROUPS, P, ROPEW)
    lru_in = f("lru_w_in")[0].reshape(KT, P, 2, CH, P).transpose(2, 3, 1, 0, 4).reshape(2, CH, P, KT * P)
    ax = np.stack([f("lru_w_a")[0], f("lru_w_x")[0]], axis=2).reshape(CH, P, 2 * P)
    vec = np.concatenate([f("lru_conv_w")[0], f("lru_conv_b"), f("lru_b_a"), f("lru_b_x"), f("lru_lambda")])
    gains = np.stack([f(k)[layer] for layer in range(2)
                      for k in ("mix_pre_norm", "mix_post_norm", "ffn_pre_norm", "ffn_post_norm")])
    up = f("ffn_w_up").reshape(2, KT, P, FFN // P, P).transpose(0, 3, 2, 1, 4).reshape(2, FFN // P, P, KT * P)
    return {
        "x": f("x").reshape(TB, P, D),
        "positions": f("positions").reshape(TB, P).T,
        "inv_freq": inverse_frequencies()[None],
        "gains": gains,
        "qkv_gain": np.concatenate([f("mla_q_norm"), f("mla_kv_norm")], axis=1),
        "w_in_q": by_partition(w_in[:, :QRANK]),
        "w_in_kv": by_partition(w_in[:, QRANK:]),
        "w_heads": heads,
        "w_rope": rope,
        "w_o": f("mla_w_o")[0].reshape(KT, P, D),
        "w_rec": lru_in[1],
        "w_gate": lru_in[0],
        "w_ax": ax,
        "lru_vec": vec.reshape(VEC_IN, CH, P).transpose(2, 1, 0),
        "w_out": f("lru_w_out")[0].reshape(KT, P, D),
        "w_up": up,
        "w_down": f("ffn_w_down").reshape(2, FFN // P, P, D),
    }


def kernel(**inputs):
    import concourse.bacc as bacc
    from concourse.bass_utils import run_bass_kernel_spmd

    nc = bacc.Bacc("TRN2", target_bir_lowering=False, num_devices=1)
    arrays = {k: np.ascontiguousarray(v) for k, v in packed(inputs).items()}
    args = [nc.dram_tensor(k, a.shape, mybir.dt.from_np(a.dtype), kind="ExternalInput").ap() for k, a in arrays.items()]
    out = nc.dram_tensor("out", (TB, P, D), F32, kind="ExternalOutput").ap()
    trunk(nc, *args, out)
    r = run_bass_kernel_spmd(nc, [arrays], core_ids=[0])
    return r.results[0]["out"].reshape(1, SEQ, D)
```

```python
from collections import namedtuple
from contextlib import ExitStack

import numpy as np

import concourse.bass as bass
from concourse import mybir

F32 = mybir.dt.float32
F32R = mybir.dt.float32r
BF16 = mybir.dt.bfloat16
I32 = mybir.dt.int32
ACT = mybir.ActivationFunctionType
ALU = mybir.AluOpType
AX = mybir.AxisListType

P = 128
D = 1024
SEQ = 1024
TB = SEQ // P
KT = D // P
HALF = 512
NORM_EPS = 1e-6

HEADS = 8
NOPE, ROPE, VDIM = 128, 64, 128
QRANK, KVRANK = 384, 256
QK, KK = QRANK // P, KVRANK // P
RH = ROPE // 2
SCALE = float(1.0 / np.sqrt(NOPE + ROPE))
ROPE_THETA = 10000.0
GH = 4
GROUPS = HEADS // GH
HEADW = (QK + 2 * KK) * P
ROPEW = QK * GH * ROPE
MASKED = -float(2.0 ** 100)

FFN = 4 * D
FG = 4
MLP_GROUPS = FFN // P // FG
CONV = 4
CH = D // P
LRU_C = 8.0
VEC_IN = CONV + 4
VEC = VEC_IN + 2

KB = 1024
AT_HT = 7 * KB
AT_S = AT_HT + 64 * KB
AT_RAW = AT_S + 32 * KB
AT_W = AT_RAW + 16 * KB


def inverse_frequencies():
    return (ROPE_THETA ** (-np.arange(0, ROPE, 2) / ROPE)).astype(np.float32)


def trunk(nc, x, positions, inv_freq, gains, qkv_gain, w_in_q, w_in_kv, w_heads, w_rope, w_o,
          w_rec, w_gate, w_ax, lru_vec, w_out, w_up, w_down, out):
    base = (nc.sbuf_base + 31) // 32 * 32

    def at(name, shape, dtype, offset):
        return nc.alloc_sbuf_tensor_at(name, [P, *shape], dtype, offset=base + offset)

    with ExitStack() as ctx:
        def sems(stage, *names):
            return namedtuple(stage, names)(*(ctx.enter_context(nc.semaphore(f"{stage}_{n}")) for n in names))

        xs = [nc.dram_tensor(f"x_after_{n}", (TB, P, D), F32, kind="Internal").ap() for n in range(3)]

        ps = ctx.enter_context(nc.psum_tensor("ps", [P, 8, HALF], F32))
        psf = ps[:].rearrange("p b n -> p (b n)")

        ident = at("ident", [P], F32, 0)
        identr = at("identr", [P], F32R, 512)
        mask = at("mask", [P], F32, 1024)
        maskr = at("maskr", [P], F32R, 1536)
        junk = at("junk", [D], BF16, 2048)
        stat = at("stat", [6, 6, TB], F32, 4096)
        power = at("power", [1], F32, 5248)
        neg_max = at("neg_max", [TB], F32, 5280)
        row_sum = at("row_sum", [TB], F32, 5312)
        row_inv = at("row_inv", [TB], F32, 5344)
        row_max = at("row_max", [TB], F32, 5376)
        stat1 = at("stat1", [3, 2 * TB], F32, 5856)

        hth = at("hth", [KT, SEQ], F32R, AT_HT)
        htl = at("htl", [KT, SEQ], F32R, AT_HT + 32 * KB)
        raw = at("raw", [4, D], F32, AT_RAW)
        rows = at("rows", [TB, D], F32, AT_S)
        gain0 = at("gain0", [D], F32, AT_W + 82 * KB)
        GAIN = 2
        xt = at("xt", [2, D], F32, AT_W + 80 * KB)

        def f32(ap):
            return ap.bitcast(F32)

        def three_passes(pe, dst, wh, wl, xh, xl, first, last):
            pe.matmul(dst, wh, xh, start=first, stop=False)
            pe.matmul(dst, wh, xl, start=False, stop=False)
            return pe.matmul(dst, wl, xh, start=False, stop=last)

        E = sems("end", "x_in0", "x_in1", "gain_in", "y_ready", "ss_y", "var_y", "rstd_y", "scaled", "x_new", "ss_x", "var_x",
                 "rstd_x", "hn", "turned", "ht_hi", "ht_lo", "x_out0", "x_out1")

        X_IN = sems("input", *(f"block{tb}" for tb in range(TB)))

        def pre(n, k):
            return TB * n + k

        def post(n, k):
            return TB * (n - 1) + k

        def x_loaded(n, tb):
            if n == 0:
                return X_IN[tb], 16
            return (E.x_in0, E.x_in1)[tb % 2], 16 * (TB // 2 * (n - 1) + tb // 2 + 1)

        def x_stored(n, tb):
            return (E.x_out0, E.x_out1)[tb % 2], 16 * (TB // 2 * (n - 1) + tb // 2 + 1)

        def x_block(n, tb):
            return rows[:, tb, :] if n == 0 else xt[:, tb % 2, :]

        def gains_loaded(n):
            return 16 * (2 * n + 1 if n < 4 else 2 * n)

        x_src = [x, x, *xs]
        x_dst = [None, *xs, out]

        def end_loads(sp, n):
            if n == 0:
                sp.dma_start(rows[:, 0, :], x_src[0][0]).then_inc(x_loaded(0, 0)[0], 16)
                sp.dma_start(gain0[:], gains[0:1, :].partition_broadcast(P)).then_inc(E.gain_in, 16)
                for tb in range(1, TB):
                    if tb <= 3:
                        mla_in_loads(sp, [tb - 1])
                    sp.dma_start(rows[:, tb, :], x_src[0][tb]).then_inc(x_loaded(0, tb)[0], 16)
                    if tb == 3:
                        mla_in_small(sp)
                        mla_in_loads(sp, [3])
                return
            sp.dma_start(raw[:, GAIN, :], gains[2 * n - 1:2 * n, :].partition_broadcast(P)).then_inc(E.gain_in, 16)
            if n < 4:
                sp.dma_start(raw[:, GAIN + 1, :], gains[2 * n:2 * n + 1, :].partition_broadcast(P)).then_inc(E.gain_in, 16)
            sp.dma_start(xt[:, 0, :], x_src[n][0]).then_inc(E.x_in0, 16)
            sp.dma_start(xt[:, 1, :], x_src[n][1]).then_inc(E.x_in1, 16)

        def end_sync(sp, n):
            for tb in range(TB):
                sp.wait_ge(E.x_new, post(n, tb + 1))
                sp.dma_start(x_dst[n][tb], xt[:, tb % 2, :]).then_inc(x_stored(n, tb)[0], 16)
                if tb + 2 < TB:
                    sp.wait_ge(*x_stored(n, tb))
                    if n < 4:
                        sp.wait_ge(E.hn, pre(n, tb + 1))
                    sp.dma_start(xt[:, tb % 2, :], x_src[n][tb + 2]).then_inc(x_loaded(n, tb + 2)[0], 16)
            sp.wait_ge(*x_stored(n, TB - 2))
            sp.wait_ge(*x_stored(n, TB - 1))
            if n < 4:
                sp.wait_ge(E.hn, pre(n, TB))

        DVE_SUMS = 6

        def turned_banks(n, tb):
            bank = tb % 2 * 2 + (0 if n > 0 and tb >= TB - 2 else 4)
            return psf[:, bank * HALF:bank * HALF + D]

        def end_scalar(act, n, step, copies):
            if step < TB and n > 0:
                if copies:
                    act.wait_ge(copies, step + 1)
                    act.activation(rows[:, step, :], psf[:, step % 2 * D:step % 2 * D + D], ACT.Copy).then_inc(E.y_ready, 1)
                act.wait_ge(E.y_ready, post(n, step + 1))
                act.wait_ge(E.ss_x, pre(min(n, 3), max(0, step - 1)) if n < 4 else pre(3, TB))
                act.wait_ge(E.ss_y, post(n, step))
                act.activation(junk[:], rows[:, step, :], ACT.Square,
                               accum_out=stat[:, 0, n, step:step + 1]).then_inc(E.ss_y, 1)
            tb = step - 1
            if 0 <= tb < TB and n < 4:
                if n > 0:
                    act.wait_ge(E.x_new, post(n, tb + 1))
                else:
                    act.wait_ge(*x_loaded(n, tb))
                    if tb > LATENT_LAG - 1:
                        act.wait_ge(A.ss, tb - LATENT_LAG + 1)
                act.wait_ge(E.ss_x, pre(n, tb))
                if n > 0:
                    act.wait_ge(E.ss_y, post(n, min(step + 1, TB)))
                act.activation(junk[:], x_block(n, tb), ACT.Square,
                               accum_out=stat[:, 3, n, tb:tb + 1]).then_inc(E.ss_x, 1)
            tb = step - 2
            if 0 <= tb < TB and n < 4:
                act.wait_ge(E.turned, pre(n, tb + 1))
                src = turned_banks(n, tb).rearrange("p (f t) -> p f t", f=KT)
                act.activation(hth[:, :, tb * P:(tb + 1) * P], src, ACT.Copy).then_inc(E.ht_hi, 1)

        def end_gpsimd(pool, n, step):
            if step < TB and n > 0:
                col = slice(step, step + 1)
                pool.wait_ge(E.ss_y, post(n, step + 1))
                pool.tensor_scalar(stat[:, 1, n, col], stat[:, 0, n, col], 1.0 / D, NORM_EPS, ALU.mult, ALU.add).then_inc(E.var_y, 1)
                pool.wait_ge(E.var_y, post(n, step + 1))
                pool.tensor_tensor(stat[:, 2, n, col], stat[:, 1, n, col], power[:], ALU.pow).then_inc(E.rstd_y, 1)
            tb = step - 1
            if 0 <= tb < TB:
                col = slice(tb, tb + 1)
                if n < 4:
                    pool.wait_ge(E.ss_x, pre(n, tb + 1))
                    pool.tensor_scalar(stat[:, 4, n, col], stat[:, 3, n, col], 1.0 / D, NORM_EPS, ALU.mult, ALU.add).then_inc(E.var_x, 1)
                    pool.wait_ge(E.var_x, pre(n, tb + 1))
                    pool.tensor_tensor(stat[:, 5, n, col], stat[:, 4, n, col], power[:], ALU.pow).then_inc(E.rstd_x, 1)
            tb = step
            if n > 0 and tb < DVE_SUMS:
                pool.wait_ge(*x_loaded(n, tb))
                pool.wait_ge(E.scaled, post(n, tb + 1))
                pool.tensor_tensor(xt[:, tb % 2, :], xt[:, tb % 2, :], rows[:, tb, :], ALU.add).then_inc(E.x_new, 1)

        def end_vector(dve, n, step):
            tb = step
            if tb < TB and n > 0:
                if tb == 0:
                    dve.wait_ge(E.gain_in, gains_loaded(n))
                dve.wait_ge(E.rstd_y, post(n, tb + 1))
                dve.scalar_tensor_tensor(out=rows[:, tb, :], in0=rows[:, tb, :], scalar=stat[:, 2, n, tb:tb + 1],
                                         in1=raw[:, GAIN, :], op0=ALU.mult, op1=ALU.mult).then_inc(E.scaled, 1)
                if tb >= DVE_SUMS:
                    dve.wait_ge(*x_loaded(n, tb))
                    dve.wait_ge(E.scaled, post(n, tb + 1))
                    dve.wait_ge(E.x_new, post(n, tb))
                    dve.tensor_tensor(xt[:, tb % 2, :], xt[:, tb % 2, :], rows[:, tb, :], ALU.add).then_inc(E.x_new, 1)
            tb = step - 1
            if 0 <= tb < TB and n < 4:
                if n == 0 and tb == 0:
                    dve.wait_ge(E.gain_in, gains_loaded(n))
                if n == 0:
                    dve.wait_ge(*x_loaded(n, tb))
                else:
                    dve.wait_ge(E.x_new, post(n, tb + 1))
                dve.wait_ge(E.rstd_x, pre(n, tb + 1))
                dve.scalar_tensor_tensor(out=rows[:, tb, :], in0=x_block(n, tb), scalar=stat[:, 5, n, tb:tb + 1],
                                         in1=gain0[:] if n == 0 else raw[:, GAIN + 1, :], op0=ALU.mult, op1=ALU.mult).then_inc(E.hn, 1)
            tb = step - 2
            if 0 <= tb < TB and n < 4:
                dve.wait_ge(E.ht_hi, pre(n, tb + 1))
                src = turned_banks(n, tb).rearrange("p (f t) -> p f t", f=KT)
                dst = slice(tb * P, (tb + 1) * P)
                dve.tensor_tensor(htl[:, :, dst], src, f32(hth[:, :, dst]), ALU.subtract).then_inc(E.ht_lo, 1)

        def end_tensor(pe, n, tb):
            if not 0 <= tb < TB or n == 4:
                return
            pe.wait_ge(E.hn, pre(n, tb + 1))
            if n > 0 and tb >= TB - 2:
                pe.wait_ge(E.y_ready, post(n, tb + 1))
            elif tb >= 2:
                pe.wait_ge(E.ht_lo, pre(n, tb - 1))
            dst = turned_banks(n, tb)
            for f in range(KT):
                mm = pe.transpose(dst[:, f * P:(f + 1) * P], rows[:, tb, f * P:(f + 1) * P], ident[:])
            mm.then_inc(E.turned, 1)

        def end_tensor_step(pe, n, step, fills):
            end_tensor(pe, n, step - 2)
            if step in FILL_STEPS and fills:
                fills[FILL_STEPS.index(step)]()

        STEPS = TB + 2
        FILL_STEPS = (TB - 1, TB + 1)
        LATENT_LAG = 3
        EARLY = (5, 7)

        aT = at("aT", [KT * SEQ], F32, AT_S)
        wo_h = [at(f"wo_h{k}", [D], F32R, AT_W + 8 * KB * k) for k in range(KT)]
        wo_l = [at(f"wo_l{k}", [D], F32R, AT_W + 8 * KB * k + 4 * KB) for k in range(KT)]
        PROJ = {n: sems(f"proj{n}", "raw_in0", "raw_in1", "raw_in2", "raw_in3", "w_hi", "w_lo", "a_hi", "a_lo", "y_done")
                for n in (1, 3)}

        def proj_loads(sp, n, w, chunks):
            q = PROJ[n]
            for k in chunks:
                if k >= 4:
                    sp.wait_ge(q.w_lo, k - 3)
                sp.dma_start(raw[:, k % 4, :], w[k]).then_inc((q.raw_in0, q.raw_in1, q.raw_in2, q.raw_in3)[k % 4], 16)

        def proj_scalar(act, n, w_free, w_free_count, a_done, a_count):
            q = PROJ[n]
            act.wait_ge(w_free, w_free_count)
            for k in range(KT):
                act.wait_ge((q.raw_in0, q.raw_in1, q.raw_in2, q.raw_in3)[k % 4], 16 * (k // 4 + 1))
                act.activation(wo_h[k][:], raw[:, k % 4, :], ACT.Copy).then_inc(q.w_hi, 1)
                if k == 0:
                    act.wait_ge(a_done, a_count)
                act.activation(hth[:, k, :], aT[:, k * SEQ:(k + 1) * SEQ], ACT.Copy).then_inc(q.a_hi, 1)
            act.wait_ge(q.a_lo, KT)

        def proj_vector(dve, n):
            q = PROJ[n]
            for k in range(KT):
                dve.wait_ge(q.w_hi, k + 1)
                dve.tensor_tensor(wo_l[k][:], raw[:, k % 4, :], f32(wo_h[k][:]), ALU.subtract).then_inc(q.w_lo, 1)
                dve.wait_ge(q.a_hi, k + 1)
                dve.tensor_tensor(htl[:, k, :], aT[:, k * SEQ:(k + 1) * SEQ], f32(hth[:, k, :]), ALU.subtract).then_inc(q.a_lo, 1)

        def proj_tensor(pe, n, fills):
            q = PROJ[n]
            for step in range(STEPS):
                if step < TB:
                    tb = step
                    if tb >= 2:
                        pe.wait_ge(E.y_ready, post(n, tb - 1))
                    for k in range(KT):
                        if tb == 0:
                            pe.wait_ge(q.w_lo, k + 1)
                            pe.wait_ge(q.a_lo, k + 1)
                        blk = slice(tb * P, (tb + 1) * P)
                        for c in range(D // HALF):
                            dst = ps[:, tb % 2 * 2 + c, :]
                            cut = slice(c * HALF, (c + 1) * HALF)
                            mm = three_passes(pe, dst, hth[:, k, blk], htl[:, k, blk], wo_h[k][:, cut], wo_l[k][:, cut],
                                              k == 0, k == KT - 1)
                    mm.then_inc(q.y_done, 1)
                end_tensor_step(pe, n, step, fills)

        u_h = at("u_h", [FG, SEQ], F32R, AT_W)
        u_l = at("u_l", [FG, SEQ], F32R, AT_W + 16 * KB)
        dn_h = at("dn_h", [FG, D], F32R, AT_W + 32 * KB)
        dn_l = at("dn_l", [FG, D], F32R, AT_W + 48 * KB)
        up_h = [at(f"up_h{s}", [KT, P], F32R, AT_W + (72 - 8 * s) * KB) for s in range(2)]
        up_l = [at(f"up_l{s}", [KT, P], F32R, AT_W + (76 - 8 * s) * KB) for s in range(2)]
        relu = at("relu", [2, HALF], F32, AT_W + 80 * KB)
        squared = at("squared", [2, HALF], F32, AT_W + 84 * KB)
        MLP = {n: sems(f"mlp{n}", "raw_in0", "raw_in1", "raw_in2", "raw_in3", "w_hi", "w_lo", "up_done", "relu", "sq",
                       "u_hi", "u_lo", "down_done", "y_sum") for n in (2, 4)}
        SLOT = {("up", 0): 0, ("up", 1): 1, ("down", 0): 2, ("down", 1): 3,
                ("up", 2): 0, ("down", 2): 1, ("up", 3): 2, ("down", 3): 3}

        def mlp_loads_first(sp, n, layer, kinds):
            q = MLP[n]
            if "up" in kinds:
                sp.dma_start(raw[:, 0, :], w_up[layer, 0]).then_inc(q.raw_in0, 16)
                sp.dma_start(raw[:, 1, :], w_up[layer, 1]).then_inc(q.raw_in1, 16)
            if "down" in kinds:
                sp.dma_start(raw[:, 2, :], w_down[layer, 0]).then_inc(q.raw_in2, 16)
                sp.dma_start(raw[:, 3, :], w_down[layer, 1]).then_inc(q.raw_in3, 16)

        SPLITS = [("down", 0), ("down", 1), ("up", 2), ("down", 2), ("up", 3), ("down", 3), ("up", 4), ("up", 5)]

        UP_ORDER = [(0, 0), (1, 0), (0, 1), (1, 1), (2, 0), (2, 1), (3, 0), (3, 1)]

        def mlp_sync(sp, n, layer):
            q = MLP[n]
            ins = (q.raw_in0, q.raw_in1, q.raw_in2, q.raw_in3)

            def load(src, row, slot, split_before):
                sp.wait_ge(q.w_lo, split_before)
                sp.dma_start(raw[:, slot, :], src[layer, row]).then_inc(ins[slot], 16)

            def group(g, last):
                rows_ = [sp.snap(g * FG + i) for i in range(2, FG + 2)] if not isinstance(g, int) else [g * FG + i for i in range(2, FG + 2)]
                load(w_up, rows_[0], 0, 8 * g + 1)
                load(w_down, rows_[0], 1, 8 * g + 2)
                load(w_up, rows_[1], 2, 8 * g + 3)
                load(w_down, rows_[1], 3, 8 * g + 4)
                if not last:
                    load(w_up, rows_[2], 0, 8 * g + 5)
                    load(w_up, rows_[3], 1, 8 * g + 6)
                    load(w_down, rows_[2], 2, 8 * g + 7)
                    load(w_down, rows_[3], 3, 8 * g + 8)

            with sp.Fori(0, MLP_GROUPS - 1) as g:
                group(g, False)
            group(MLP_GROUPS - 1, True)

        def mlp_chunk(n, g, kind, i):
            slot = SLOT[kind, i % FG]
            early = (kind, i) in (("down", 0), ("down", 1))
            arrived = 32 * g + (16 if early else 32 if i < FG else 48)
            if kind == "up":
                return slot, arrived, up_h[i % 2][:].rearrange("p a b -> p (a b)"), up_l[i % 2][:].rearrange("p a b -> p (a b)")
            return slot, arrived, dn_h[:, i, :], dn_l[:, i, :]

        def mlp_first_up(n, i):
            return i, 16, up_h[i][:].rearrange("p a b -> p (a b)"), up_l[i][:].rearrange("p a b -> p (a b)")

        def split_hi(act, q, chunk):
            slot, arrived, hi, lo = chunk
            act.wait_ge((q.raw_in0, q.raw_in1, q.raw_in2, q.raw_in3)[slot], arrived)
            act.activation(hi, raw[:, slot, 0:hi.shape[1]], ACT.Copy).then_inc(q.w_hi, 1)

        def split_lo(dve, q, chunk, count):
            slot, arrived, hi, lo = chunk
            dve.wait_ge(q.w_hi, count)
            dve.tensor_tensor(lo, raw[:, slot, 0:hi.shape[1]], f32(hi), ALU.subtract).then_inc(q.w_lo, 1)

        def mlp_scalar(act, n):
            q = MLP[n]

            def evacuate(g, *numbers):
                for i in numbers:
                    ft, half = UP_ORDER[i]
                    act.wait_ge(q.up_done, 8 * g + i + 1)
                    if i >= 2:
                        act.wait_ge(q.sq, 8 * g + i - 1)
                    act.activation(relu[:, i % 2, :], ps[:, 4 + i % 4, :], ACT.Relu).then_inc(q.relu, 1)
                    act.wait_ge(q.relu, 8 * g + i + 1)
                    act.activation(u_h[:, ft, half * HALF:(half + 1) * HALF], relu[:, i % 2, :], ACT.Square).then_inc(q.u_hi, 1)

            def group(g, last):
                split_hi(act, q, mlp_chunk(n, g, *SPLITS[0]))
                split_hi(act, q, mlp_chunk(n, g, *SPLITS[1]))
                evacuate(g, 0, 1, 2)
                split_hi(act, q, mlp_chunk(n, g, *SPLITS[2]))
                split_hi(act, q, mlp_chunk(n, g, *SPLITS[3]))
                evacuate(g, 3)
                split_hi(act, q, mlp_chunk(n, g, *SPLITS[4]))
                split_hi(act, q, mlp_chunk(n, g, *SPLITS[5]))
                evacuate(g, 4, 5)
                if not last:
                    split_hi(act, q, mlp_chunk(n, g, *SPLITS[6]))
                evacuate(g, 6, 7)
                if not last:
                    split_hi(act, q, mlp_chunk(n, g, *SPLITS[7]))

            act.wait_ge(*x_stored(n - 1, TB - 2))
            act.wait_ge(*x_stored(n - 1, TB - 1))
            with act.Fori(0, MLP_GROUPS - 1) as g:
                group(g, False)
                act.wait_ge(q.down_done, 8 * g + 8)
            group(MLP_GROUPS - 1, True)

        def mlp_vector(dve, n, early):
            q = MLP[n]

            def evacuate(g, *numbers):
                for i in numbers:
                    ft, half = UP_ORDER[i]
                    cut = slice(half * HALF, (half + 1) * HALF)
                    dve.wait_ge(q.sq, 8 * g + i + 1)
                    dve.wait_ge(q.u_hi, 8 * g + i + 1)
                    dve.tensor_tensor(u_l[:, ft, cut], squared[:, i % 2, :], f32(u_h[:, ft, cut]), ALU.subtract).then_inc(q.u_lo, 1)

            def group(g, last):
                split_lo(dve, q, mlp_chunk(n, g, *SPLITS[0]), 8 * g + 3)
                split_lo(dve, q, mlp_chunk(n, g, *SPLITS[1]), 8 * g + 4)
                evacuate(g, 0, 1, 2)
                split_lo(dve, q, mlp_chunk(n, g, *SPLITS[2]), 8 * g + 5)
                split_lo(dve, q, mlp_chunk(n, g, *SPLITS[3]), 8 * g + 6)
                evacuate(g, 3)
                split_lo(dve, q, mlp_chunk(n, g, *SPLITS[4]), 8 * g + 7)
                split_lo(dve, q, mlp_chunk(n, g, *SPLITS[5]), 8 * g + 8)
                evacuate(g, 4, 5)
                if not last:
                    split_lo(dve, q, mlp_chunk(n, g, *SPLITS[6]), 8 * g + 9)
                evacuate(g, 6, 7)
                if not last:
                    split_lo(dve, q, mlp_chunk(n, g, *SPLITS[7]), 8 * g + 10)

            def add(g, tb, signal):
                dve.wait_ge(q.down_done, 8 * g + tb + 1)
                ins = dve.tensor_tensor(rows[:, tb, :], psf[:, tb % 2 * D:tb % 2 * D + D], rows[:, tb, :], ALU.add)
                ins.then_inc(signal, 1)

            dve.wait_ge(q.y_sum, 1)
            with dve.Fori(0, MLP_GROUPS - 1) as g:
                group(g, False)
                for tb in range(TB):
                    add(g, tb, q.y_sum)
            group(MLP_GROUPS - 1, True)
            dve.wait_ge(q.y_sum, 1 + TB * (MLP_GROUPS - 1))
            for step in range(STEPS):
                if step < TB:
                    add(MLP_GROUPS - 1, step, E.y_ready)
                end_vector(dve, n, step)
                if step in EARLY:
                    early(EARLY.index(step))

        def mlp_gpsimd(pool, n):
            q = MLP[n]
            pool.wait_ge(E.turned, pre(n - 1, TB))
            pool.memset(rows[:], 0.0).then_inc(q.y_sum, 1)

            def group(g):
                for i in range(2 * FG):
                    pool.wait_ge(q.relu, 8 * g + i + 1)
                    if i >= 2:
                        pool.wait_ge(q.u_lo, 8 * g + i - 1)
                    pool.tensor_tensor(squared[:, i % 2, :], relu[:, i % 2, :], relu[:, i % 2, :], ALU.mult).then_inc(q.sq, 1)

            with pool.Fori(0, MLP_GROUPS - 1) as g:
                group(g)
            group(MLP_GROUPS - 1)

        def mlp_up(pe, n, g, i):
            q = MLP[n]
            ft, half = UP_ORDER[i]
            if i < 2:
                pe.wait_ge(E.ht_lo, pre(n - 1, TB // 2 + 1))
            elif i == 2:
                pe.wait_ge(E.ht_lo, pre(n - 1, TB))
            pe.wait_ge(q.w_lo, 8 * g + (1, 2, 5, 7)[ft])
            if i >= 4:
                pe.wait_ge(q.relu, 8 * g + i - 3)
            for k in range(KT):
                mm = three_passes(pe, ps[:, 4 + i % 4, :], up_h[ft % 2][:, k, :], up_l[ft % 2][:, k, :],
                                  hth[:, k, half * HALF:(half + 1) * HALF], htl[:, k, half * HALF:(half + 1) * HALF],
                                  k == 0, k == KT - 1)
            mm.then_inc(q.up_done, 1)

        UP_AHEAD = 2

        def mlp_tensor(pe, n, fills):
            q = MLP[n]

            def down(g, tb, bank_free):
                blk = slice(tb * P, (tb + 1) * P)
                if tb == 0:
                    pe.wait_ge(q.w_lo, 8 * g + 8)
                bank_free(tb)
                for ft in range(FG):
                    if tb == 0:
                        pe.wait_ge(q.u_lo, 8 * g + UP_ORDER.index((ft, 1)) + 1)
                    for c in range(D // HALF):
                        cut = slice(c * HALF, (c + 1) * HALF)
                        mm = three_passes(pe, ps[:, tb % 2 * 2 + c, :], u_h[:, ft, blk], u_l[:, ft, blk],
                                          dn_h[:, ft, cut], dn_l[:, ft, cut], ft == 0, ft == FG - 1)
                mm.then_inc(q.down_done, 1)

            with pe.Fori(0, MLP_GROUPS - 1) as g:
                for i in range(UP_AHEAD, 2 * FG):
                    mlp_up(pe, n, g, i)

                def bank_free(tb):
                    pe.wait_ge(q.y_sum, 8 * g + tb if tb >= 2 else 8 * g + 1)

                for tb in range(TB):
                    down(g, tb, bank_free)
                for i in range(UP_AHEAD):
                    mlp_up(pe, n, g + 1, i)
            for i in range(UP_AHEAD, 2 * FG):
                mlp_up(pe, n, MLP_GROUPS - 1, i)

            def last_bank_free(tb):
                if tb < 2:
                    pe.wait_ge(q.y_sum, 1 + TB * (MLP_GROUPS - 1))
                else:
                    pe.wait_ge(E.y_ready, post(n, tb - 1))

            for step in range(STEPS):
                if step < TB:
                    down(MLP_GROUPS - 1, step, last_bank_free)
                if step == 0:
                    pe.wait_ge(q.relu, 8 * MLP_GROUPS)
                end_tensor_step(pe, n, step, fills)

        wq_h = at("wq_h", [KT, QRANK], F32R, AT_W)
        wq_l = at("wq_l", [KT, QRANK], F32R, AT_W + 12 * KB)
        KVW = KVRANK + ROPE
        wkv_h = at("wkv_h", [KT, KVW], F32R, AT_W + 24 * KB)
        wkv_l = at("wkv_l", [KT, KVW], F32R, AT_W + 34 * KB)
        cq_h = at("cq_h", [QK, SEQ], F32R, AT_W + 44 * KB)
        cq_l = at("cq_l", [QK, SEQ], F32R, AT_W + 56 * KB)
        ckv_h = at("ckv_h", [KK, SEQ], F32R, AT_W)
        ckv_l = at("ckv_l", [KK, SEQ], F32R, AT_W + 8 * KB)
        krot_h = at("krot_h", [SEQ], F32R, AT_W + 16 * KB)
        krot_l = at("krot_l", [SEQ], F32R, AT_W + 20 * KB)
        o = AT_W + 68 * KB
        latent = at("latent", [2, QRANK], F32, o)
        krope = at("krope", [TB, ROPE], F32, o + 3 * KB)
        kturn = at("kturn", [TB, 2, ROPE], F32, o + 5 * KB)
        lgain = at("lgain", [QRANK + KVRANK], F32, o + 9 * KB)
        angle = at("angle", [TB, RH], F32, o + 12 * KB)
        turns = at("turns", [TB, RH], F32, o + 13 * KB)
        ktmp = at("ktmp", [4, TB, RH], F32, o + 14 * KB)
        sine = at("sine", [TB, RH], F32, o + 18 * KB)
        cosine = at("cosine", [TB, RH], F32, o + 19 * KB)
        pos_i = at("pos_i", [TB], I32, 6112)
        pos_f = at("pos_f", [TB], F32, 6144)
        freq = at("freq", [RH], F32, 6176)

        A = sems("mla_in", "raw_in0", "raw_in1", "raw_in2", "raw_in3", "w_hi", "w_lo", "small_in", "lgain_in", "product", "ss", "var",
                 "rstd", "normed", "krope", "turned", "hi", "lo", "trig", "reduced", "half_sine", "krot", "kturned", "k_hi", "k_lo")
        IN_CHUNKS = [(w_in_q, wq_h, wq_l, 0), (w_in_q, wq_h, wq_l, 1), (w_in_q, wq_h, wq_l, 2),
                     (w_in_kv, wkv_h, wkv_l, 0), (w_in_kv, wkv_h, wkv_l, 1), (w_in_kv, wkv_h, wkv_l, 2)]

        def flat(t):
            return t[:].rearrange("p a b -> p (a b)")

        def in_cut(c):
            w, hi, lo, i = IN_CHUNKS[c]
            return slice(i * D, min((i + 1) * D, w.shape[1]))

        def mla_in_loads(sp, chunks):
            for c in chunks:
                w, cut = IN_CHUNKS[c][0], in_cut(c)
                if c >= 4:
                    sp.wait_ge(A.w_lo, c - 3)
                sp.dma_start(raw[:, c % 4, 0:cut.stop - cut.start], w[:, cut]).then_inc((A.raw_in0, A.raw_in1, A.raw_in2, A.raw_in3)[c % 4], 16)

        def mla_in_small(sp):
            with nc.allow_non_contiguous_dma(reason="1024 positions, 4 bytes each"):
                sp.dma_start(pos_i[:], positions).then_inc(A.small_in, 16)
            sp.dma_start(freq[:], inv_freq[0:1, :].partition_broadcast(P)).then_inc(A.small_in, 16)
            sp.dma_start(lgain[:], qkv_gain[0:1, :].partition_broadcast(P)).then_inc(A.lgain_in, 16)

        def mla_in_split_hi(act, chunks):
            for c in chunks:
                w, hi, lo, i = IN_CHUNKS[c]
                cut = in_cut(c)
                act.wait_ge((A.raw_in0, A.raw_in1, A.raw_in2, A.raw_in3)[c % 4], 16 * (c // 4 + 1))
                act.activation(flat(hi)[:, cut], raw[:, c % 4, 0:cut.stop - cut.start], ACT.Copy).then_inc(A.w_hi, 1)

        def mla_in_split_lo(dve, chunks):
            for c in chunks:
                w, hi, lo, i = IN_CHUNKS[c]
                cut = in_cut(c)
                dve.wait_ge(A.w_hi, c + 1)
                dve.tensor_tensor(flat(lo)[:, cut], raw[:, c % 4, 0:cut.stop - cut.start], f32(flat(hi)[:, cut]),
                                  ALU.subtract).then_inc(A.w_lo, 1)

        IN_SPLITS = {0: [0], 1: [1], 2: [2], 5: [3], 7: [4], 9: [5]}

        def latent_of(i):
            return (QRANK, 0, QK, cq_h, cq_l) if i < TB else (KVRANK, QRANK, KK, ckv_h, ckv_l)

        def mla_in_scalar(act):
            for step in range(LATENT_LAG + 2 * TB + 1):
                if step < STEPS:
                    end_scalar(act, 0, step, None)
                if step in IN_SPLITS:
                    mla_in_split_hi(act, IN_SPLITS[step])
                i = step - LATENT_LAG
                if i < 0:
                    continue
                if i < 2 * TB:
                    rank = latent_of(i)[0]
                    act.wait_ge(A.product, i + 1)
                    act.wait_ge(E.ss_x, pre(0, min(step, TB)))
                    if i > 0:
                        act.wait_ge(A.ss, i)
                    act.activation(junk[:, 0:rank], ps[:, i % 2, 0:rank], ACT.Square,
                                   accum_out=stat1[:, 0, i:i + 1]).then_inc(A.ss, 1)
                if i >= 1:
                    tb, (rank, _, tiles, hi, lo) = (i - 1) % TB, latent_of(i - 1)
                    act.wait_ge(A.turned, i)
                    if i - 1 == TB:
                        act.wait_ge(A.product, TB)
                    src = ps[:, 2 + (i - 1) % 2, 0:tiles * P].rearrange("p (f t) -> p f t", f=tiles)
                    act.activation(hi[:, :, tb * P:(tb + 1) * P], src, ACT.Copy).then_inc(A.hi, 1)
                if i == 4:
                    act.wait_ge(A.trig, 6)
                    act.activation(sine[:], angle[:], ACT.Sin).then_inc(A.half_sine, 1)
                    act.activation(cosine[:], angle[:], ACT.Sin, scale=0.5).then_inc(A.half_sine, 1)
            act.wait_ge(A.ss, 2 * TB)
            for c in range(2):
                act.wait_ge(A.kturned, c + 1)
                act.activation(krot_h[:, c * HALF:(c + 1) * HALF], ps[:, 4 + c, :], ACT.Copy).then_inc(A.k_hi, 1)

        def mla_in_gpsimd(pool):
            for step in range(LATENT_LAG + 2 * TB):
                if step < STEPS:
                    end_gpsimd(pool, 0, step)
                i = step - LATENT_LAG
                if i < 0:
                    continue
                rank = latent_of(i)[0]
                col = slice(i, i + 1)
                pool.wait_ge(A.ss, i + 1)
                pool.tensor_scalar(stat1[:, 1, col], stat1[:, 0, col], 1.0 / rank, NORM_EPS, ALU.mult, ALU.add).then_inc(A.var, 1)
                pool.wait_ge(A.var, i + 1)
                pool.tensor_tensor(stat1[:, 2, col], stat1[:, 1, col], power[:], ALU.pow).then_inc(A.rstd, 1)

        def mla_angles(dve):
            two_pi = 2 * np.pi
            parts, rest = [], two_pi
            for _ in range(3):
                e = np.floor(np.log2(rest)) - 7
                part = np.floor(rest / 2.0 ** e) * 2.0 ** e
                parts.append(float(part))
                rest -= part
            parts.append(float(np.float32(rest)))
            dve.wait_ge(A.small_in, 32)
            dve.tensor_copy(pos_f[:], pos_i[:]).then_inc(A.trig, 1)
            dve.wait_ge(A.trig, 1)
            for tb in range(TB):
                ins = dve.tensor_scalar(angle[:, tb, :], freq[:], pos_f[:, tb:tb + 1], None, ALU.mult)
            ins.then_inc(A.trig, 1)
            dve.wait_ge(A.trig, 2)
            half_ulp = float(1.5 * 2 ** 23)
            dve.tensor_scalar(turns[:], angle[:], float(1 / two_pi), half_ulp, ALU.mult, ALU.add).then_inc(A.trig, 1)
            dve.wait_ge(A.trig, 3)
            dve.tensor_scalar(turns[:], turns[:], half_ulp, None, ALU.subtract).then_inc(A.trig, 1)
            dve.wait_ge(A.trig, 4)
            for i, part in enumerate(parts):
                ins = dve.scalar_tensor_tensor(out=angle[:], in0=turns[:], scalar=-part, in1=angle[:], op0=ALU.mult, op1=ALU.add)
                if i < 3:
                    ins.then_inc(A.reduced, 1)
                    dve.wait_ge(A.reduced, i + 1)
            ins.then_inc(A.trig, 1)
            dve.wait_ge(A.trig, 5)
            pi = float(np.nextafter(np.float32(np.pi), np.float32(0)))
            dve.tensor_scalar(angle[:], angle[:], pi, -pi, ALU.min, ALU.max).then_inc(A.trig, 1)

        def mla_in_vector(dve):
            for step in range(LATENT_LAG + 2 * TB + 1):
                if step < STEPS:
                    end_vector(dve, 0, step)
                if step in IN_SPLITS:
                    mla_in_split_lo(dve, IN_SPLITS[step])
                i = step - LATENT_LAG
                if i < 0:
                    continue
                if i < 2 * TB:
                    tb, (rank, off, tiles, hi, lo) = i % TB, latent_of(i)
                    if i == 0:
                        dve.wait_ge(A.lgain_in, 16)
                    dve.wait_ge(A.rstd, i + 1)
                    if i >= 2:
                        dve.wait_ge(A.turned, i - 1)
                    dve.scalar_tensor_tensor(out=latent[:, i % 2, 0:rank], in0=ps[:, i % 2, 0:rank], scalar=stat1[:, 2, i:i + 1],
                                             in1=lgain[:, off:off + rank], op0=ALU.mult, op1=ALU.mult).then_inc(A.normed, 1)
                    if i >= TB:
                        dve.tensor_copy(krope[:, tb, :], ps[:, i % 2, KVRANK:KVW]).then_inc(A.krope, 1)
                if i >= 1:
                    tb, (rank, _, tiles, hi, lo) = (i - 1) % TB, latent_of(i - 1)
                    dst = slice(tb * P, (tb + 1) * P)
                    dve.wait_ge(A.hi, i)
                    src = ps[:, 2 + (i - 1) % 2, 0:tiles * P].rearrange("p (f t) -> p f t", f=tiles)
                    dve.tensor_tensor(lo[:, :, dst], src, f32(hi[:, :, dst]), ALU.subtract).then_inc(A.lo, 1)
                if i == 3:
                    mla_angles(dve)
                if i == 6:
                    dve.wait_ge(A.half_sine, 2)
                    dve.tensor_tensor(cosine[:], cosine[:], cosine[:], ALU.mult).then_inc(A.trig, 1)
                    dve.wait_ge(A.trig, 7)
                    dve.tensor_scalar(cosine[:], cosine[:], -2.0, 1.0, ALU.mult, ALU.add).then_inc(A.trig, 1)
                    dve.wait_ge(A.trig, 8)
            dve.wait_ge(A.krope, TB)
            dve.wait_ge(E.hn, pre(0, TB))
            k1, k2 = krope[:, :, 0:RH], krope[:, :, RH:ROPE]
            dve.tensor_tensor(ktmp[:, 0], k1, cosine[:], ALU.mult)
            dve.tensor_tensor(ktmp[:, 1], k2, sine[:], ALU.mult)
            dve.tensor_tensor(ktmp[:, 2], k2, cosine[:], ALU.mult)
            dve.tensor_tensor(ktmp[:, 3], k1, sine[:], ALU.mult).then_inc(A.krot, 1)
            dve.wait_ge(A.krot, 1)
            for c in range(2):
                dve.tensor_tensor(kturn[:, :, c, 0:RH], ktmp[:, 0], ktmp[:, 1], ALU.subtract)
                ins = dve.tensor_tensor(kturn[:, :, c, RH:ROPE], ktmp[:, 2], ktmp[:, 3], ALU.add)
            ins.then_inc(A.krot, 1)
            for c in range(2):
                cut = slice(c * HALF, (c + 1) * HALF)
                dve.wait_ge(A.k_hi, c + 1)
                dve.tensor_tensor(krot_l[:, cut], ps[:, 4 + c, :], f32(krot_h[:, cut]), ALU.subtract).then_inc(A.k_lo, 1)

        def mla_in_tensor(pe):
            def turn(i):
                tiles = latent_of(i)[2]
                pe.wait_ge(A.normed, i + 1)
                if i >= 2:
                    pe.wait_ge(A.lo, i - 1)
                for f in range(tiles):
                    mm = pe.transpose(ps[:, 2 + i % 2, f * P:(f + 1) * P], latent[:, i % 2, f * P:(f + 1) * P], ident[:])
                mm.then_inc(A.turned, 1)

            for step in range(LATENT_LAG + 2 * TB):
                end_tensor(pe, 0, step - 2)
                i = step - LATENT_LAG
                if i < 0:
                    continue
                tb = i % TB
                blk = slice(tb * P, (tb + 1) * P)
                if i < TB:
                    pe.wait_ge(E.ht_lo, pre(0, i + 1))
                    width, wh, wl = QRANK, wq_h, wq_l
                else:
                    width, wh, wl = KVW, wkv_h, wkv_l
                if i == TB:
                    pe.wait_ge(A.w_lo, 6)
                if i >= 2:
                    pe.wait_ge(A.normed, i - 1)
                    if i - 2 >= TB:
                        pe.wait_ge(A.krope, i - 2 - TB + 1)
                for k in range(KT):
                    if i == 0:
                        pe.wait_ge(A.w_lo, ((k + 1) * QRANK - 1) // D + 1)
                    mm = three_passes(pe, ps[:, i % 2, 0:width], hth[:, k, blk], htl[:, k, blk], wh[:, k, :], wl[:, k, :],
                                      k == 0, k == KT - 1)
                mm.then_inc(A.product, 1)
                if i >= 1:
                    turn(i - 1)
            turn(2 * TB - 1)
            pe.wait_ge(A.krot, 2)
            for c in range(2):
                for t in range(4):
                    tb = 4 * c + t
                    mm = pe.transpose(ps[:, 4 + c, t * P:(t + 1) * P], kturn[:, tb].rearrange("p a b -> p (a b)"), ident[:])
                mm.then_inc(A.kturned, 1)

        qn_h = [at(f"qn_h{s}", [SEQ], F32R, AT_HT + (16 * s + 0) * KB) for s in range(2)]
        qn_l = [at(f"qn_l{s}", [SEQ], F32R, AT_HT + (16 * s + 4) * KB) for s in range(2)]
        kn_h = [at(f"kn_h{s}", [SEQ], F32R, AT_HT + (16 * s + 8) * KB) for s in range(2)]
        kn_l = [at(f"kn_l{s}", [SEQ], F32R, AT_HT + (16 * s + 12) * KB) for s in range(2)]
        v_h = at("v_h", [TB, VDIM], F32R, AT_HT + 32 * KB)
        v_l = at("v_l", [TB, VDIM], F32R, AT_HT + 36 * KB)
        pt_h = at("pt_h", [2, HALF], F32R, AT_HT + 40 * KB)
        pt_l = at("pt_l", [2, HALF], F32R, AT_HT + 44 * KB)
        qrot = at("qrot", [GH, SEQ], F32R, AT_HT + 48 * KB)
        hw_h = [at(f"hw_h{s}", [HEADW], F32R, AT_W + (24 + 7 * s) * KB) for s in range(2)]
        hw_l = [at(f"hw_l{s}", [HEADW], F32R, AT_W + (24 + 7 * s) * KB + 4 * HEADW) for s in range(2)]
        rw_h = at("rw_h", [QK, GH * ROPE], F32R, AT_W + 38 * KB)
        rw_l = at("rw_l", [QK, GH * ROPE], F32R, AT_W + 41 * KB)
        probs_first = at("probs_first", [10 * P], F32, AT_W + 38 * KB)
        probs_second = at("probs_second", [26 * P], F32, AT_W + 68 * KB)
        qr = [at("qr0", [2, GH, ROPE], F32, AT_W + 84 * KB), at("qr1", [2, GH, ROPE], F32, AT_HT + 44 * KB)]
        qsplit = [at("qsplit0", [2, GH, 2, ROPE], F32, AT_RAW + 12 * KB), at("qsplit1", [2, GH, 2, ROPE], F32, AT_HT + 40 * KB)]
        qtmp = at("qtmp", [2, 2, GH, ROPE], F32, AT_W + 68 * KB)

        B = sems("mla", "head_in0", "head_in1", "rope_in", "hw_hi", "hw_lo", "rw_hi", "rw_lo",
                 "rope_done", "rope_read", "qr", "qsplit_hi", "qsplit_lo", "rope_turned", "rope_copied",
                 "projected", "part_hi", "part_lo", "scores", "max", "neg_max", "exp", "inv", "probs",
                 "turned", "turned_hi", "turned_lo", "pv", "out_copied")

        def tensor_steps():
            steps = [("rope", 0), ("rope", 1), ("q", 0, 0), ("q", 0, 1), ("rope_turn", 0), ("rope", 2), ("k", 0, 0),
                     ("rope_turn", 1), ("rope", 3), ("k", 0, 1), ("rope_turn", 2), ("v", 0, 0), ("rope_turn", 3),
                     ("scores", 0, 0), ("scores", 0, 1), ("v", 0, 1), ("scores", 0, 2), ("scores", 0, 3)]
            for j in range(GH - 1):
                n = j + 1
                steps += [("scores", j, 4), ("turn", j, 0), ("q", n, 0), ("scores", j, 5), ("turn", j, 1), ("pv", j, 0),
                          ("scores", j, 6), ("turn", j, 2), ("k", n, 0), ("turn", j, 3), ("scores", j, 7), ("pv", j, 1),
                          ("pv", j, 2), ("q", n, 1), ("pv", j, 3), ("scores", n, 0), ("turn", j, 4), ("turn", j, 5),
                          ("k", n, 1), ("pv", j, 4), ("turn", j, 6), ("scores", n, 1), ("pv", j, 5),
                          ("turn", j, 7), ("scores", n, 2), ("pv", j, 6), ("turn", j, 8), ("scores", n, 3), ("pv", j, 7),
                          ("turn", j, 9), ("v", n, 0), ("pv", j, 8), ("turn", j, 10), ("pv", j, 9),
                          ("turn", j, 11), ("v", n, 1), ("pv", j, 10), ("pv", j, 11)]
            j = GH - 1
            steps += [("scores", j, 4), ("turn", j, 0), ("scores", j, 5), ("turn", j, 1), ("scores", j, 6), ("pv", j, 0),
                      ("turn", j, 2), ("scores", j, 7), ("pv", j, 1), ("turn", j, 3), ("pv", j, 2), ("pv", j, 3), ("turn", j, 4)]
            for m in range(5, 12):
                steps += [("turn", j, m), ("pv", j, m - 1)]
            return steps + [("pv", j, 11)]

        def other_steps():
            steps = [("rope", 0), ("rope_lo", 0), ("rope", 1), ("q", 0, 0), ("rope_lo", 1), ("q", 0, 1), ("rope_turn", 0),
                     ("rope", 2), ("rope_lo", 2), ("k", 0, 0), ("rope_turn", 1),
                     ("rope", 3), ("rope_lo", 3), ("k", 0, 1), ("rope_turn", 2), ("v", 0, 0), ("rope_turn", 3),
                     ("weights", 1), ("max", 0, 0), ("exp", 0, 0), ("max", 0, 1), ("exp", 0, 1), ("norm", 0, 0), ("v", 0, 1),
                     ("max", 0, 2), ("exp", 0, 2), ("norm", 0, 1), ("max", 0, 3), ("exp", 0, 3), ("norm", 0, 2), ("norm", 0, 3)]
            for j in range(GH):
                n = j + 1
                steps += [("max", j, 4), ("exp", j, 4), ("turn", j, 0), ("q", n, 0), ("max", j, 5), ("exp", j, 5), ("norm", j, 4),
                          ("turn", j, 1), ("max", j, 6), ("exp", j, 6), ("norm", j, 5), ("turn", j, 2), ("k", n, 0),
                          ("max", j, 7), ("turn", j, 3), ("exp", j, 7), ("norm", j, 6), ("norm", j, 7), ("q", n, 1), ("out", j, 0),
                          ("turn", j, 4), ("turn", j, 5), ("max", n, 0), ("exp", n, 0), ("k", n, 1),
                          ("turn", j, 6), ("max", n, 1), ("exp", n, 1), ("norm", n, 0),
                          ("turn", j, 7), ("max", n, 2), ("exp", n, 2), ("norm", n, 1),
                          ("turn", j, 8), ("max", n, 3), ("exp", n, 3), ("norm", n, 2), ("turn", j, 9), ("norm", n, 3), ("v", n, 0),
                          ("turn", j, 10), ("weights", j + 2), ("turn", j, 11), ("out", j, 1), ("v", n, 1)]
            return [s for s in steps if s[0][:4] == "rope" or s[1] < GH]

        TENSOR_STEPS, OTHER_STEPS = tensor_steps(), other_steps()
        PROJ_ORDER = [s for s in TENSOR_STEPS if s[0] in "qkv"]
        NPROJ, FIRST_PROJ = len(PROJ_ORDER), 6
        TURNS = 12 * GH
        SCORES = TB * GH
        OUTS = 2 * GH

        def projections(step, j, i):
            return PROJ_ORDER.index((step, j, i)) + 1

        def proj_bank(n):
            return ps[:, 7 - n % 2, :] if n < FIRST_PROJ else ps[:, 7, :]

        def out_bank():
            return ps[:, 6, :]

        def key_block(m):
            half, kb = (0, m) if m < 4 else (1, m - 4)
            return half, kb, max(0, kb - 4 * half) * P

        def probs_of(i, keys):
            if i < 4:
                start = i * (i + 1) // 2 * P
                return probs_first[:, start + keys.start:start + keys.stop]
            start = (i * (i + 1) // 2 - 10) * P
            return probs_second[:, start + keys.start:start + keys.stop]

        def mla_loads(sp):
            sp.wait_ge(A.w_lo, 6)
            sp.dma_start(raw[:, 2, 0:ROPEW], w_rope[0]).then_inc(B.rope_in, 16)
            sp.dma_start(raw[:, 0, 0:HEADW], w_heads[0]).then_inc(B.head_in0, 16)
            sp.dma_start(raw[:, 1, 0:HEADW], w_heads[1]).then_inc(B.head_in1, 16)
            for g in range(GROUPS):
                if g + 1 < GROUPS:
                    sp.wait_ge(B.rw_lo, g + 1)
                    sp.dma_start(raw[:, 2, 0:ROPEW], w_rope[g + 1]).then_inc(B.rope_in, 16)
                for j in range(GH):
                    h = g * GH + j
                    if h + 2 < HEADS:
                        sp.wait_ge(B.hw_lo, h + 1)
                        sp.dma_start(raw[:, h % 2, 0:HEADW], w_heads[h + 2]).then_inc((B.head_in0, B.head_in1)[h % 2], 16)

        def part_of(step, j, i):
            cut = slice(i * HALF, (i + 1) * HALF)
            if step == "q":
                return qn_h[j % 2][:, cut], qn_l[j % 2][:, cut]
            if step == "k":
                return kn_h[j % 2][:, cut], kn_l[j % 2][:, cut]
            return (v_h[:, 4 * i:4 * i + 4, :].rearrange("p a b -> p (a b)"), v_l[:, 4 * i:4 * i + 4, :].rearrange("p a b -> p (a b)"))

        def mla_scalar(act):
            def rope_hi(g, t):
                act.wait_ge(B.qr, 4 * g + t + 1)
                if t >= 2:
                    act.wait_ge(B.rope_turned, TB * g + 2 * t - 2)
                act.activation(qsplit[t % 2][:, :, :, 0, :].bitcast(F32R), qr[t % 2][:], ACT.Copy).then_inc(B.qsplit_hi, 1)

            def rope_copy(g, t):
                for n in (2 * t, 2 * t + 1):
                    act.wait_ge(B.rope_turned, TB * g + n + 1)
                    src = ps[:, 4 + n % 2, :].rearrange("p (h t) -> p h t", h=GH)
                    act.activation(qrot[:, :, n * P:(n + 1) * P], src, ACT.Copy).then_inc(B.rope_copied, 1)

            def weights(g, j):
                if j >= 2:
                    act.wait_ge(B.projected, NPROJ * g + projections("v", j - 2, 1))
                act.wait_ge((B.head_in0, B.head_in1)[j % 2], 32 * g + 16 * (j // 2 + 1))
                act.activation(hw_h[j % 2][:], raw[:, j % 2, 0:HEADW], ACT.Copy).then_inc(B.hw_hi, 1)

            def project(g, step, j, i):
                n = projections(step, j, i)
                act.wait_ge(B.projected, NPROJ * g + n)
                if step == "v" and j > 0:
                    act.wait_ge(B.pv, TURNS * g + 12 * (j - 1) + (8, 12)[i])
                act.activation(part_of(step, j, i)[0], proj_bank(n - 1), ACT.Copy).then_inc(B.part_hi, 1)

            def exponentiate(g, j, i):
                act.wait_ge(B.neg_max, SCORES * g + TB * j + i + 1)
                if j > 0:
                    act.wait_ge(B.turned, TURNS * g + 12 * (j - 1) + (i + 1 if i < 4 else 4 + i + 1))
                col = slice(i, i + 1)
                nk = (i + 1) * P
                act.activation(probs_of(i, slice(0, nk)), psf[:, i % 2 * D:i % 2 * D + nk], ACT.Exp, bias=neg_max[:, col],
                               scale=SCALE, accum_out=row_sum[:, col]).then_inc(B.exp, 1)

            def turned_hi(g, j, m):
                q0, n = key_block(m)[2], 12 * j + m
                act.wait_ge(B.turned, TURNS * g + n + 1)
                if n >= 2:
                    act.wait_ge(B.pv, TURNS * g + n - 1)
                act.activation(pt_h[:, n % 2, q0:HALF], ps[:, 4 + n % 2, q0:HALF], ACT.Copy).then_inc(B.turned_hi, 1)

            act.wait_ge(A.product, 2 * TB)
            with act.Fori(0, GROUPS) as g:
                act.wait_ge(B.rope_in, 16 * g + 16)
                act.activation(flat(rw_h), raw[:, 2, 0:ROPEW], ACT.Copy).then_inc(B.rw_hi, 1)
                weights(g, 0)
                for step in OTHER_STEPS:
                    kind, of = step[0], step[1:]
                    if kind == "rope":
                        rope_hi(g, *of)
                    elif kind == "rope_turn":
                        rope_copy(g, *of)
                    elif kind == "weights":
                        weights(g, *of)
                    elif kind in "qkv":
                        project(g, *step)
                    elif kind == "exp":
                        exponentiate(g, *of)
                    elif kind == "turn":
                        turned_hi(g, *of)
                act.wait_ge(B.pv, TURNS * g + TURNS)

        def mla_vector(dve):
            def rotate(g, t):
                dve.wait_ge(B.rope_done, 4 * g + t + 1)
                src = ps[:, 2 * (t % 2), :].rearrange("p (b h r) -> p b h r", b=2, h=GH)
                cos = cosine[:, 2 * t:2 * t + 2, :].unsqueeze(2).broadcast_to([P, 2, GH, RH])
                sin = sine[:, 2 * t:2 * t + 2, :].unsqueeze(2).broadcast_to([P, 2, GH, RH])
                q1, q2 = src[:, :, :, 0:RH], src[:, :, :, RH:ROPE]
                if t > 0:
                    dve.wait_ge(B.qr, 4 * g + t)
                dve.tensor_tensor(qtmp[:, 0, :, :, 0:RH], q1, cos, ALU.mult)
                dve.tensor_tensor(qtmp[:, 0, :, :, RH:ROPE], q2, cos, ALU.mult)
                dve.tensor_tensor(qtmp[:, 1, :, :, 0:RH], q2, sin, ALU.mult)
                dve.tensor_tensor(qtmp[:, 1, :, :, RH:ROPE], q1, sin, ALU.mult).then_inc(B.rope_read, 1)
                dve.wait_ge(B.rope_read, 4 * g + t + 1)
                if t >= 2:
                    dve.wait_ge(B.qsplit_hi, 4 * g + t - 1)
                dve.tensor_tensor(qr[t % 2][:, :, :, 0:RH], qtmp[:, 0, :, :, 0:RH], qtmp[:, 1, :, :, 0:RH], ALU.subtract)
                dve.tensor_tensor(qr[t % 2][:, :, :, RH:ROPE], qtmp[:, 0, :, :, RH:ROPE], qtmp[:, 1, :, :, RH:ROPE],
                                  ALU.add).then_inc(B.qr, 1)

            def rope_lo(g, t):
                dve.wait_ge(B.qsplit_hi, 4 * g + t + 1)
                dve.tensor_tensor(qsplit[t % 2][:, :, :, 1, :], qr[t % 2][:], qsplit[t % 2][:, :, :, 0, :],
                                  ALU.subtract).then_inc(B.qsplit_lo, 1)

            def weights(g, j):
                dve.wait_ge(B.hw_hi, GH * g + j + 1)
                dve.tensor_tensor(hw_l[j % 2][:], raw[:, j % 2, 0:HEADW], f32(hw_h[j % 2][:]), ALU.subtract).then_inc(B.hw_lo, 1)

            def project(g, step, j, i):
                n = projections(step, j, i)
                hi, lo = part_of(step, j, i)
                dve.wait_ge(B.part_hi, NPROJ * g + n)
                dve.tensor_tensor(lo, proj_bank(n - 1), f32(hi), ALU.subtract).then_inc(B.part_lo, 1)

            def maximum(g, j, i):
                n = TB * j + i
                col = slice(i, i + 1)
                dve.wait_ge(B.scores, SCORES * g + n + 1)
                dve.tensor_reduce(row_max[:, col], psf[:, i % 2 * D:i % 2 * D + (i + 1) * P], AX.X, ALU.max).then_inc(B.max, 1)
                dve.wait_ge(B.max, SCORES * g + n + 1)
                dve.tensor_scalar(neg_max[:, col], row_max[:, col], -SCALE, None, ALU.mult).then_inc(B.neg_max, 1)

            def normalise(g, j, i):
                n = TB * j + i
                col = slice(i, i + 1)
                row = probs_of(i, slice(0, (i + 1) * P))
                dve.wait_ge(B.exp, SCORES * g + n + 1)
                dve.reciprocal(row_inv[:, col], row_sum[:, col]).then_inc(B.inv, 1)
                dve.wait_ge(B.inv, SCORES * g + n + 1)
                dve.tensor_scalar(row, row, row_inv[:, col], None, ALU.mult).then_inc(B.probs, 1)

            def turned_lo(g, j, m):
                q0, n = key_block(m)[2], 12 * j + m
                dve.wait_ge(B.turned_hi, TURNS * g + n + 1)
                dve.tensor_tensor(pt_l[:, n % 2, q0:HALF], ps[:, 4 + n % 2, q0:HALF], f32(pt_h[:, n % 2, q0:HALF]),
                                  ALU.subtract).then_inc(B.turned_lo, 1)

            def copy_out(g, j, half):
                dve.wait_ge(B.pv, TURNS * g + 12 * j + (4, 12)[half])
                dve.tensor_copy(aT[:, bass.ds(g * (GH * SEQ) + j * SEQ + half * HALF, HALF)], out_bank()).then_inc(B.out_copied, 1)

            with dve.Fori(0, GROUPS) as g:
                dve.wait_ge(B.rw_hi, g + 1)
                dve.tensor_tensor(flat(rw_l), raw[:, 2, 0:ROPEW], f32(flat(rw_h)), ALU.subtract).then_inc(B.rw_lo, 1)
                weights(g, 0)
                for step in OTHER_STEPS:
                    kind, of = step[0], step[1:]
                    if kind == "rope":
                        rotate(g, *of)
                    elif kind == "rope_lo":
                        rope_lo(g, *of)
                    elif kind == "weights":
                        weights(g, *of)
                    elif kind in "qkv":
                        project(g, *step)
                    elif kind == "max":
                        maximum(g, *of)
                    elif kind == "norm":
                        normalise(g, *of)
                    elif kind == "turn":
                        turned_lo(g, *of)
                    elif kind == "out":
                        copy_out(g, *of)

        def mla_tensor(pe):
            def rope_product(g, t):
                if t >= 2:
                    pe.wait_ge(B.rope_read, 4 * g + t - 1)
                for b in range(2):
                    blk = slice((2 * t + b) * P, (2 * t + b + 1) * P)
                    for k in range(QK):
                        mm = three_passes(pe, ps[:, 2 * (t % 2), b * 256:(b + 1) * 256], cq_h[:, k, blk], cq_l[:, k, blk],
                                          rw_h[:, k, :], rw_l[:, k, :], k == 0, k == QK - 1)
                mm.then_inc(B.rope_done, 1)

            def rope_turn(g, t):
                pe.wait_ge(B.qsplit_lo, 4 * g + t + 1)
                for b in range(2):
                    n = 2 * t + b
                    if n >= 2:
                        pe.wait_ge(B.rope_copied, TB * g + n - 1)
                    for h in range(GH):
                        mm = pe.transpose(ps[:, 4 + n % 2, h * P:(h + 1) * P], qsplit[t % 2][:, b, h].rearrange("p a b -> p (a b)"), ident[:])
                    mm.then_inc(B.rope_turned, 1)

            def project(g, step, j, i):
                n = projections(step, j, i)
                dst = proj_bank(n - 1)
                if n > 2:
                    pe.wait_ge(B.part_lo, NPROJ * g + (n - 2 if n <= FIRST_PROJ else n - 1))
                if step == "q" and i == 0:
                    pe.wait_ge(B.hw_lo, GH * g + j + 1)
                hh, hl = hw_h[j % 2], hw_l[j % 2]
                cut = slice(i * HALF, (i + 1) * HALF)
                if step == "q":
                    for k in range(QK):
                        w = slice(k * P, (k + 1) * P)
                        mm = three_passes(pe, dst, hh[:, w], hl[:, w], cq_h[:, k, cut], cq_l[:, k, cut], k == 0, k == QK - 1)
                elif step == "k":
                    for k in range(KK):
                        w = slice((QK + k) * P, (QK + k + 1) * P)
                        mm = three_passes(pe, dst, hh[:, w], hl[:, w], ckv_h[:, k, cut], ckv_l[:, k, cut], k == 0, k == KK - 1)
                else:
                    for t in range(4):
                        blk = slice((4 * i + t) * P, (4 * i + t + 1) * P)
                        for k in range(KK):
                            w = slice((QK + KK + k) * P, (QK + KK + k + 1) * P)
                            mm = three_passes(pe, dst[:, t * P:(t + 1) * P], ckv_h[:, k, blk], ckv_l[:, k, blk],
                                              hh[:, w], hl[:, w], k == 0, k == KK - 1)
                mm.then_inc(B.projected, 1)

            def scores(g, j, i):
                qh, ql, kh, kl = qn_h[j % 2], qn_l[j % 2], kn_h[j % 2], kn_l[j % 2]
                n = TB * j + i
                blk = slice(i * P, (i + 1) * P)
                if i % 4 == 0:
                    pe.wait_ge(B.part_lo, NPROJ * g + max(projections(which, j, i // 4) for which in "qk"))
                if n >= 2:
                    pe.wait_ge(B.exp, SCORES * g + n - 1)
                if j == 0:
                    pe.wait_ge(B.rope_copied, TB * g + i + 1)
                for c in range(i // 4 + 1):
                    width = min(HALF, (i + 1) * P - c * HALF)
                    dst = ps[:, i % 2 * 2 + c, 0:width]
                    keys = slice(c * HALF, c * HALF + width)
                    three_passes(pe, dst, qh[:, blk], ql[:, blk], kh[:, keys], kl[:, keys], True, False)
                    pe.matmul(dst, qrot[:, j, blk], krot_h[:, keys], start=False, stop=False)
                    pe.matmul(dst, qrot[:, j, blk], krot_l[:, keys], start=False, stop=c < i // 4)
                mm = pe.matmul(ps[:, i % 2 * 2 + c, width - P:width], identr[:], maskr[:], start=False, stop=True)
                mm.then_inc(B.scores, 1)

            def turn(g, j, m):
                half, kb, q0 = key_block(m)
                n = 12 * j + m
                if m in (0, 4):
                    pe.wait_ge(B.probs, SCORES * g + TB * j + 4 * half + 4)
                if n >= 2:
                    pe.wait_ge(B.turned_lo, TURNS * g + n - 1)
                else:
                    pe.wait_ge(B.rope_copied, TB * g + TB)
                for q in range(q0 // P, 4):
                    mm = pe.transpose(ps[:, 4 + n % 2, q * P:(q + 1) * P], probs_of(4 * half + q, slice(kb * P, (kb + 1) * P)), ident[:])
                mm.then_inc(B.turned, 1)

            def pv(g, j, m):
                half, kb, q0 = key_block(m)
                n = 12 * j + m
                if kb == 0 and 2 * j + half > 0:
                    pe.wait_ge(B.out_copied, OUTS * g + 2 * j + half)
                if m == 0 and j > 0:
                    pe.wait_ge(B.part_lo, NPROJ * g + projections("v", j, 0))
                if m == 8 or n == 0:
                    pe.wait_ge(B.part_lo, NPROJ * g + projections("v", j, 1))
                pe.wait_ge(B.turned_lo, TURNS * g + n + 1)
                mm = three_passes(pe, out_bank()[:, q0:HALF], v_h[:, kb, :], v_l[:, kb, :], pt_h[:, n % 2, q0:HALF],
                                  pt_l[:, n % 2, q0:HALF], kb == 0, m in (3, 11))
                mm.then_inc(B.pv, 1)

            pe.wait_ge(A.lo, 2 * TB)
            pe.wait_ge(A.k_lo, 2)
            with pe.Fori(0, GROUPS) as g:
                pe.wait_ge(B.rw_lo, g + 1)
                for step in TENSOR_STEPS:
                    kind, of = step[0], step[1:]
                    if kind == "rope":
                        rope_product(g, *of)
                    elif kind == "rope_turn":
                        rope_turn(g, *of)
                    elif kind in "qkv":
                        project(g, *step)
                    elif kind == "scores":
                        scores(g, *of)
                    elif kind == "turn":
                        turn(g, *of)
                    elif kind == "pv":
                        pv(g, *of)
                pe.wait_ge(B.out_copied, OUTS * g + OUTS)

        rec_h = at("rec_h", [KT, P], F32R, AT_W + 72 * KB)
        rec_l = at("rec_l", [KT, P], F32R, AT_W + 76 * KB)
        gw_h = at("gw_h", [KT, P], F32R, AT_W + 64 * KB)
        gw_l = at("gw_l", [KT, P], F32R, AT_W + 68 * KB)
        ax_h = at("ax_h", [2, P], F32R, AT_W + 8 * KB)
        ax_l = at("ax_l", [2, P], F32R, AT_W + 9 * KB)
        xc_h = at("xc_h", [SEQ], F32R, AT_W + 10 * KB)
        xc_l = at("xc_l", [SEQ], F32R, AT_W + 14 * KB)
        PAD = CONV - 1
        rec = at("rec", [SEQ + 8], F32, AT_W + 18 * KB)
        o = AT_W + 23 * KB
        xc = at("xc", [SEQ], F32, o)
        gate = at("gate", [SEQ], F32, o + 4 * KB)
        rgate = at("rgate", [SEQ], F32, o + 8 * KB)
        igate = at("igate", [SEQ], F32, o + 12 * KB)
        tanh = at("tanh", [SEQ], F32, o + 16 * KB)
        root = at("root", [SEQ], F32, o + 20 * KB)
        winv = at("winv", [SEQ], F32, o + 24 * KB)
        wtmp = at("wtmp", [SEQ], F32, o + 28 * KB)
        agate = at("agate", [SEQ], F32, o + 32 * KB)
        bgate = at("bgate", [SEQ], F32, o + 36 * KB)
        vec = at("vec", [CH, VEC], F32, 6304)
        tilev = at("tilev", [VEC], F32, 6624)
        dtmp = at("dtmp", [5, CH], F32, 6688)
        V_CONV_B, V_B_A, V_B_X, V_LAM, V_DECAY, V_DECAY2 = range(CONV, VEC)
        L = sems("lru", "vec_in", "raw_in0", "raw_in1", "raw_in2", "w_hi", "w_lo", "setup", "padded", "tile_vec", "rec_done", "gate_done",
                 "ax_done", "rec_copied", "gated", "conv", "xc_hi", "xc_lo", "sigmoid", "tanh", "estimate", "root", "inv", "decay", "u",
                 "ix", "b", "scan", "out")

        def lru_loads_first(sp, kinds):
            if "rec" in kinds:
                sp.dma_start(raw[:, 0, :], w_rec[0]).then_inc(L.raw_in0, 16)
            if "gate" in kinds:
                sp.dma_start(raw[:, 1, :], w_gate[0]).then_inc(L.raw_in1, 16)
            if "ax" in kinds:
                sp.dma_start(raw[:, 2, 0:2 * P], w_ax[0]).then_inc(L.raw_in2, 16)

        def lru_sync(sp):
            with sp.Fori(0, CH - 1) as n:
                row = sp.snap(n + 1)
                sp.wait_ge(L.w_lo, 3 * n + 1)
                sp.dma_start(raw[:, 0, :], w_rec[row]).then_inc(L.raw_in0, 16)
                sp.wait_ge(L.w_lo, 3 * n + 2)
                sp.dma_start(raw[:, 1, :], w_gate[row]).then_inc(L.raw_in1, 16)
                sp.wait_ge(L.w_lo, 3 * n + 3)
                sp.dma_start(raw[:, 2, 0:2 * P], w_ax[row]).then_inc(L.raw_in2, 16)

        LRU_WEIGHTS = {"rec": (0, rec_h, rec_l), "gate": (1, gw_h, gw_l), "ax": (2, ax_h, ax_l)}

        def lru_split_hi(act, n, which):
            slot, hi, lo = LRU_WEIGHTS[which]
            act.wait_ge((L.raw_in0, L.raw_in1, L.raw_in2)[slot], 16 * n + 16)
            act.activation(flat(hi), raw[:, slot, 0:flat(hi).shape[1]], ACT.Copy).then_inc(L.w_hi, 1)

        def lru_split_lo(dve, n, which):
            slot, hi, lo = LRU_WEIGHTS[which]
            dve.wait_ge(L.w_hi, 3 * n + slot + 1)
            dve.tensor_tensor(flat(lo), raw[:, slot, 0:flat(hi).shape[1]], f32(flat(hi)), ALU.subtract).then_inc(L.w_lo, 1)

        BANKS_REC, BANKS_GATE, BANKS_R, BANKS_I = 4, 6, 0, 2

        def pair(b):
            return psf[:, b * HALF:b * HALF + D]

        def tile_vec(k):
            return tilev[:, k:k + 1]

        def lru_scalar(act):
            act.wait_ge(L.vec_in, 16)
            act.activation(dtmp[:, 0, :], vec[:, :, V_LAM], ACT.Abs).then_inc(L.setup, 1)
            act.wait_ge(L.setup, 1)
            act.activation(dtmp[:, 1, :], dtmp[:, 0, :], ACT.Exp, scale=-1.0).then_inc(L.setup, 1)
            lru_split_hi(act, 0, "ax")

            def tile(n, last):
                act.wait_ge(L.rec_done, n + 1)
                act.activation(rec[:, PAD:PAD + SEQ], pair(BANKS_REC), ACT.Copy).then_inc(L.rec_copied, 1)
                if not last:
                    lru_split_hi(act, n + 1, "rec")
                act.wait_ge(L.conv, CONV * n + CONV)
                act.activation(xc_h[:], xc[:], ACT.Copy).then_inc(L.xc_hi, 1)
                act.wait_ge(L.gate_done, n + 1)
                act.activation(gate[:], pair(BANKS_GATE), ACT.Gelu_apprx_tanh).then_inc(L.gated, 1)
                if not last:
                    lru_split_hi(act, n + 1, "gate")
                act.wait_ge(L.ax_done, n + 1)
                act.activation(rgate[:], pair(BANKS_R), ACT.Sigmoid, bias=tile_vec(V_B_A)).then_inc(L.sigmoid, 1)
                act.activation(igate[:], pair(BANKS_I), ACT.Sigmoid, bias=tile_vec(V_B_X)).then_inc(L.sigmoid, 1)
                act.wait_ge(L.sigmoid, 2 * n + 1)
                act.activation(tanh[:], rgate[:], ACT.Tanh, scale=tile_vec(V_DECAY)).then_inc(L.tanh, 1)
                act.activation(winv[:], rgate[:], ACT.Exp, scale=tile_vec(V_DECAY2)).then_inc(L.estimate, 1)
                act.wait_ge(L.tanh, n + 1)
                act.activation(root[:], tanh[:], ACT.Sqrt, scale=4.0).then_inc(L.root, 1)
                if not last:
                    lru_split_hi(act, n + 1, "ax")

            with act.Fori(0, CH - 1) as n:
                tile(n, False)
            tile(CH - 1, True)

        def lru_setup_vector(dve):
            chain = 2

            def after(ins):
                nonlocal chain
                ins.then_inc(L.setup, 1)
                chain += 1
                dve.wait_ge(L.setup, chain)

            e, s, s2, p = dtmp[:, 1, :], dtmp[:, 2, :], dtmp[:, 3, :], dtmp[:, 4, :]
            dve.wait_ge(L.setup, 2)
            after(dve.tensor_scalar(p, e, 2.0, None, ALU.add))
            after(dve.reciprocal(s, p))
            after(dve.tensor_tensor(s, s, e, ALU.mult))
            after(dve.tensor_tensor(s2, s, s, ALU.mult))
            after(dve.tensor_scalar(p, s2, 1.0 / 17, None, ALU.mult))
            for k in range(15, 1, -2):
                after(dve.scalar_tensor_tensor(out=p, in0=p, scalar=1.0 / k, in1=s2, op0=ALU.add, op1=ALU.mult))
            after(dve.scalar_tensor_tensor(out=p, in0=p, scalar=1.0, in1=s, op0=ALU.add, op1=ALU.mult))
            after(dve.tensor_scalar(s, vec[:, :, V_LAM], -1.0, 0.0, ALU.mult, ALU.max))
            after(dve.scalar_tensor_tensor(out=p, in0=p, scalar=2.0, in1=s, op0=ALU.mult, op1=ALU.add))
            after(dve.tensor_scalar(vec[:, :, V_DECAY], p, LRU_C / 2, None, ALU.mult))
            after(dve.tensor_scalar(vec[:, :, V_DECAY2], p, -LRU_C, None, ALU.mult))

        vec_flat = vec[:].rearrange("p a b -> p (a b)")

        def lru_vector(dve):
            lru_setup_vector(dve)
            lru_split_lo(dve, 0, "ax")
            dve.wait_ge(L.padded, 1)

            def tile(n, last):
                dve.tensor_copy(tilev[:], vec_flat[:, bass.ds(n * VEC, VEC)] if not last else vec_flat[:, n * VEC:(n + 1) * VEC]).then_inc(L.tile_vec, 1)
                dve.wait_ge(L.tile_vec, n + 1)
                dve.wait_ge(L.rec_copied, n + 1)
                dve.tensor_scalar(xc[:], rec[:, PAD:PAD + SEQ], tile_vec(CONV - 1), tile_vec(V_CONV_B), ALU.mult, ALU.add).then_inc(L.conv, 1)
                for k in range(CONV - 1):
                    dve.wait_ge(L.conv, CONV * n + k + 1)
                    dve.scalar_tensor_tensor(out=xc[:], in0=rec[:, k:k + SEQ], scalar=tile_vec(k), in1=xc[:], op0=ALU.mult,
                                             op1=ALU.add).then_inc(L.conv, 1)
                if not last:
                    lru_split_lo(dve, n + 1, "rec")
                dve.wait_ge(L.xc_hi, n + 1)
                dve.tensor_tensor(xc_l[:], xc[:], f32(xc_h[:]), ALU.subtract).then_inc(L.xc_lo, 1)
                if not last:
                    lru_split_lo(dve, n + 1, "gate")
                dve.wait_ge(L.estimate, n + 1)
                dve.tensor_scalar(winv[:], winv[:], 0.5, 0.5, ALU.mult, ALU.add).then_inc(L.inv, 1)
                dve.wait_ge(L.inv, 3 * n + 1)
                dve.wait_ge(L.tanh, n + 1)
                dve.scalar_tensor_tensor(out=wtmp[:], in0=tanh[:], scalar=1.0, in1=winv[:], op0=ALU.add, op1=ALU.mult).then_inc(L.inv, 1)
                dve.wait_ge(L.inv, 3 * n + 2)
                dve.scalar_tensor_tensor(out=winv[:], in0=wtmp[:], scalar=2.0, in1=winv[:], op0=ALU.subtract, op1=ALU.mult).then_inc(L.inv, 1)
                dve.wait_ge(L.inv, 3 * n + 3)
                dve.wait_ge(L.root, n + 1)
                dve.scalar_tensor_tensor(out=bgate[:], in0=root[:], scalar=-1.0, in1=winv[:], op0=ALU.mult, op1=ALU.mult).then_inc(L.u, 1)
                dve.tensor_tensor(agate[:], tanh[:], winv[:], ALU.mult).then_inc(L.decay, 1)
                dve.wait_ge(L.decay, 2 * n + 1)
                dve.tensor_scalar(agate[:], agate[:], 2.0, 1.0, ALU.mult, ALU.add).then_inc(L.decay, 1)
                if not last:
                    lru_split_lo(dve, n + 1, "ax")
                dve.wait_ge(L.decay, 2 * n + 2)
                dve.wait_ge(L.b, n + 1)
                dve.tensor_tensor_scan(rgate[:], agate[:], bgate[:], 0.0, ALU.mult, ALU.add).then_inc(L.scan, 1)
                dve.wait_ge(L.scan, n + 1)
                dve.wait_ge(L.gated, n + 1)
                dst = aT[:, n * SEQ:(n + 1) * SEQ] if last else aT[:, bass.ds(n * SEQ, SEQ)]
                dve.tensor_tensor(dst, gate[:], rgate[:], ALU.mult).then_inc(L.out, 1)

            with dve.Fori(0, CH - 1) as n:
                tile(n, False)
            tile(CH - 1, True)

        def lru_gpsimd(pool):
            pool.wait_ge(MLP[2].down_done, TB * MLP_GROUPS)
            pool.memset(rec[:, 0:PAD], 0.0).then_inc(L.padded, 1)

            def tile(n):
                pool.wait_ge(L.sigmoid, 2 * n + 2)
                pool.tensor_tensor(igate[:], igate[:], xc[:], ALU.mult).then_inc(L.ix, 1)
                pool.wait_ge(L.u, n + 1)
                pool.wait_ge(L.ix, n + 1)
                pool.tensor_tensor(bgate[:], bgate[:], igate[:], ALU.mult).then_inc(L.b, 1)

            with pool.Fori(0, CH) as n:
                tile(n)

        def lru_project(pe, n, which, halves):
            slot, wh, wl = LRU_WEIGHTS[which]
            banks, done = ((BANKS_REC, L.rec_done), (BANKS_GATE, L.gate_done))[slot]
            pe.wait_ge(L.w_lo, 3 * n + slot + 1)
            for half in halves:
                cut = slice(half * HALF, (half + 1) * HALF)
                for k in range(KT):
                    mm = three_passes(pe, ps[:, banks + half, :], wh[:, k, :], wl[:, k, :], hth[:, k, cut], htl[:, k, cut],
                                      k == 0, k == KT - 1)
            if 1 in halves:
                mm.then_inc(done, 1)

        def lru_first(pe, which):
            pe.wait_ge(E.ht_lo, pre(2, TB - 2))
            lru_project(pe, 0, which, (0,))

        def lru_tensor(pe):
            def gates(n):
                pe.wait_ge(L.w_lo, 3 * n + 3)
                pe.wait_ge(L.xc_lo, n + 1)
                for g, banks in ((0, BANKS_R), (1, BANKS_I)):
                    for half in range(2):
                        cut = slice(half * HALF, (half + 1) * HALF)
                        mm = three_passes(pe, ps[:, banks + half, :], ax_h[:, g, :], ax_l[:, g, :], xc_h[:, cut], xc_l[:, cut], True, True)
                mm.then_inc(L.ax_done, 1)

            pe.wait_ge(E.ht_lo, pre(2, TB))
            lru_project(pe, 0, "rec", (1,))
            lru_project(pe, 0, "gate", (1,))
            gates(0)
            with pe.Fori(1, CH) as n:
                lru_project(pe, n, "rec", (0, 1))
                lru_project(pe, n, "gate", (0, 1))
                gates(n)

        C = sems("const", "zeroed", "ident", "mask", "power", "rounded")
        block = ctx.enter_context(nc.Block())

        @block.sync
        def _(sp):
            end_loads(sp, 0)
            mla_in_loads(sp, range(4, 6))
            sp.dma_start(vec[:, :, 0:VEC_IN], lru_vec).then_inc(L.vec_in, 16)
            mla_loads(sp)
            sp.wait_ge(B.hw_lo, HEADS)
            sp.wait_ge(B.pv, TURNS * GROUPS)
            proj_loads(sp, 1, w_o, range(2))
            proj_loads(sp, 1, w_o, range(2, KT))
            sp.wait_ge(PROJ[1].w_lo, KT)
            end_loads(sp, 1)
            mlp_loads_first(sp, 2, 0, ("up",))
            end_sync(sp, 1)
            mlp_loads_first(sp, 2, 0, ("down",))
            mlp_sync(sp, 2, 0)
            sp.wait_ge(MLP[2].w_lo, 8 * MLP_GROUPS)
            sp.wait_ge(MLP[2].u_lo, 8 * MLP_GROUPS)
            end_loads(sp, 2)
            lru_loads_first(sp, ("rec", "gate"))
            end_sync(sp, 2)
            lru_loads_first(sp, ("ax",))
            lru_sync(sp)
            sp.wait_ge(L.w_lo, 3 * CH)
            proj_loads(sp, 3, w_out, range(4))
            proj_loads(sp, 3, w_out, range(4, KT))
            sp.wait_ge(PROJ[3].w_lo, KT)
            end_loads(sp, 3)
            mlp_loads_first(sp, 4, 1, ("up",))
            end_sync(sp, 3)
            mlp_loads_first(sp, 4, 1, ("down",))
            mlp_sync(sp, 4, 1)
            sp.wait_ge(MLP[4].w_lo, 8 * MLP_GROUPS)
            sp.wait_ge(MLP[4].u_lo, 8 * MLP_GROUPS)
            end_loads(sp, 4)
            end_sync(sp, 4)

        @block.scalar
        def _(act):
            mla_in_scalar(act)
            act.wait_ge(C.mask, 1)
            act.activation(identr[:], ident[:], ACT.Copy).then_inc(C.rounded, 1)
            act.activation(maskr[:], mask[:], ACT.Copy).then_inc(C.rounded, 1)
            mla_scalar(act)
            proj_scalar(act, 1, B.pv, TURNS * GROUPS, B.out_copied, OUTS * GROUPS)
            for step in range(STEPS):
                end_scalar(act, 1, step, PROJ[1].y_done)
                if step in EARLY:
                    split_hi(act, MLP[2], mlp_first_up(2, EARLY.index(step)))
            mlp_scalar(act, 2)
            for step in range(STEPS):
                end_scalar(act, 2, step, None)
                if step in EARLY:
                    lru_split_hi(act, 0, ("rec", "gate")[EARLY.index(step)])
            lru_scalar(act)
            proj_scalar(act, 3, L.out, CH, L.out, CH)
            for step in range(STEPS):
                end_scalar(act, 3, step, PROJ[3].y_done)
                if step in EARLY:
                    split_hi(act, MLP[4], mlp_first_up(4, EARLY.index(step)))
            mlp_scalar(act, 4)
            for step in range(STEPS):
                end_scalar(act, 4, step, None)

        @block.vector
        def _(dve):
            mla_in_vector(dve)
            mla_vector(dve)
            proj_vector(dve, 1)
            for step in range(STEPS):
                end_vector(dve, 1, step)
                if step in EARLY:
                    split_lo(dve, MLP[2], mlp_first_up(2, EARLY.index(step)), EARLY.index(step) + 1)
            mlp_vector(dve, 2, lambda i: lru_split_lo(dve, 0, ("rec", "gate")[i]))
            lru_vector(dve)
            proj_vector(dve, 3)
            for step in range(STEPS):
                end_vector(dve, 3, step)
                if step in EARLY:
                    split_lo(dve, MLP[4], mlp_first_up(4, EARLY.index(step)), EARLY.index(step) + 1)
            mlp_vector(dve, 4, lambda i: None)

        @block.gpsimd
        def _(pool):
            pool.memset(ident[:], 0.0).then_inc(C.zeroed, 1)
            pool.memset(mask[:], 0.0).then_inc(C.zeroed, 1)
            pool.memset(power[:], -0.5).then_inc(C.power, 1)
            pool.wait_ge(C.zeroed, 2)
            pool.affine_select(out=ident[:], in_=ident[:], compare_op=ALU.not_equal, fill=1.0, base=0, pattern=[[-1, P]],
                               channel_multiplier=1).then_inc(C.ident, 1)
            pool.affine_select(out=mask[:], in_=mask[:], compare_op=ALU.is_ge, fill=MASKED, base=0, pattern=[[-1, P]],
                               channel_multiplier=1).then_inc(C.mask, 1)
            pool.wait_ge(C.power, 1)
            mla_in_gpsimd(pool)
            for step in range(STEPS):
                end_gpsimd(pool, 1, step)
            mlp_gpsimd(pool, 2)
            for step in range(STEPS):
                end_gpsimd(pool, 2, step)
            lru_gpsimd(pool)
            for step in range(STEPS):
                end_gpsimd(pool, 3, step)
            mlp_gpsimd(pool, 4)
            for step in range(STEPS):
                end_gpsimd(pool, 4, step)

        @block.tensor
        def _(pe):
            pe.wait_ge(C.ident, 1)
            mla_in_tensor(pe)
            pe.wait_ge(C.rounded, 2)
            mla_tensor(pe)
            proj_tensor(pe, 1, [lambda: mlp_up(pe, 2, 0, 0), lambda: mlp_up(pe, 2, 0, 1)])
            mlp_tensor(pe, 2, [lambda: lru_first(pe, "rec"), lambda: lru_first(pe, "gate")])
            lru_tensor(pe)
            proj_tensor(pe, 3, [lambda: mlp_up(pe, 4, 0, 0), lambda: mlp_up(pe, 4, 0, 1)])
            mlp_tensor(pe, 4, [])


def packed(inputs):
    f = lambda name: np.asarray(inputs[name])

    def by_partition(w):
        return w.reshape(-1, P, w.shape[1]).transpose(1, 0, 2).reshape(P, -1)

    w_in = f("mla_w_in")[0]
    uq = f("mla_w_uq")[0].reshape(QK, P, HEADS, NOPE + ROPE)
    ukv = f("mla_w_ukv")[0].reshape(KK, P, HEADS, NOPE + VDIM)
    heads = np.concatenate([
        uq[..., :NOPE].transpose(2, 1, 0, 3).reshape(HEADS, P, QK * NOPE),
        ukv[..., :NOPE].transpose(2, 1, 0, 3).reshape(HEADS, P, KK * NOPE),
        ukv[..., NOPE:].transpose(2, 1, 0, 3).reshape(HEADS, P, KK * VDIM)], axis=2)
    rope = uq[..., NOPE:].reshape(QK, P, GROUPS, GH, ROPE).transpose(2, 1, 0, 3, 4).reshape(GROUPS, P, ROPEW)
    lru_in = f("lru_w_in")[0].reshape(KT, P, 2, CH, P).transpose(2, 3, 1, 0, 4).reshape(2, CH, P, KT * P)
    ax = np.stack([f("lru_w_a")[0], f("lru_w_x")[0]], axis=2).reshape(CH, P, 2 * P)
    vec = np.concatenate([f("lru_conv_w")[0], f("lru_conv_b"), f("lru_b_a"), f("lru_b_x"), f("lru_lambda")])
    gains = np.stack([f(k)[layer] for layer in range(2)
                      for k in ("mix_pre_norm", "mix_post_norm", "ffn_pre_norm", "ffn_post_norm")])
    up = f("ffn_w_up").reshape(2, KT, P, FFN // P, P).transpose(0, 3, 2, 1, 4).reshape(2, FFN // P, P, KT * P)
    return {
        "x": f("x").reshape(TB, P, D),
        "positions": f("positions").reshape(TB, P).T,
        "inv_freq": inverse_frequencies()[None],
        "gains": gains,
        "qkv_gain": np.concatenate([f("mla_q_norm"), f("mla_kv_norm")], axis=1),
        "w_in_q": by_partition(w_in[:, :QRANK]),
        "w_in_kv": by_partition(w_in[:, QRANK:]),
        "w_heads": heads,
        "w_rope": rope,
        "w_o": f("mla_w_o")[0].reshape(KT, P, D),
        "w_rec": lru_in[1],
        "w_gate": lru_in[0],
        "w_ax": ax,
        "lru_vec": vec.reshape(VEC_IN, CH, P).transpose(2, 1, 0),
        "w_out": f("lru_w_out")[0].reshape(KT, P, D),
        "w_up": up,
        "w_down": f("ffn_w_down").reshape(2, FFN // P, P, D),
    }


def kernel(**inputs):
    import concourse.bacc as bacc
    from concourse.bass_utils import run_bass_kernel_spmd

    nc = bacc.Bacc("TRN2", target_bir_lowering=False, num_devices=1)
    arrays = {k: np.ascontiguousarray(v) for k, v in packed(inputs).items()}
    args = [nc.dram_tensor(k, a.shape, mybir.dt.from_np(a.dtype), kind="ExternalInput").ap() for k, a in arrays.items()]
    out = nc.dram_tensor("out", (TB, P, D), F32, kind="ExternalOutput").ap()
    trunk(nc, *args, out)
    r = run_bass_kernel_spmd(nc, [arrays], core_ids=[0])
    return r.results[0]["out"].reshape(1, SEQ, D)
```

```python
from collections import namedtuple
from contextlib import ExitStack

import numpy as np

import concourse.bass as bass
from concourse import mybir

F32 = mybir.dt.float32
F32R = mybir.dt.float32r
BF16 = mybir.dt.bfloat16
I32 = mybir.dt.int32
ACT = mybir.ActivationFunctionType
ALU = mybir.AluOpType
AX = mybir.AxisListType

P = 128
D = 1024
SEQ = 1024
TB = SEQ // P
KT = D // P
HALF = 512
NORM_EPS = 1e-6

HEADS = 8
NOPE, ROPE, VDIM = 128, 64, 128
QRANK, KVRANK = 384, 256
QK, KK = QRANK // P, KVRANK // P
RH = ROPE // 2
SCALE = float(1.0 / np.sqrt(NOPE + ROPE))
ROPE_THETA = 10000.0
GH = 4
GROUPS = HEADS // GH
HEADW = (QK + KK) * P
PAIRW = KK * 2 * VDIM
ROPEW = QK * GH * ROPE
MASKED = -float(2.0 ** 100)

FFN = 4 * D
FG = 4
MLP_GROUPS = FFN // P // FG
CONV = 4
CH = D // P
LRU_C = 8.0
VEC_IN = CONV + 4
VEC = VEC_IN + 2

KB = 1024
AT_HT = 7 * KB
AT_S = AT_HT + 64 * KB
AT_RAW = AT_S + 32 * KB
AT_W = AT_RAW + 16 * KB


def inverse_frequencies():
    return (ROPE_THETA ** (-np.arange(0, ROPE, 2) / ROPE)).astype(np.float32)


def trunk(nc, x, positions, inv_freq, gains, qkv_gain, w_in_q, w_in_kv, w_heads, w_values, w_rope, w_o,
          w_rec, w_gate, w_ax, lru_vec, w_out, w_up, w_down, out):
    base = (nc.sbuf_base + 31) // 32 * 32

    def at(name, shape, dtype, offset):
        return nc.alloc_sbuf_tensor_at(name, [P, *shape], dtype, offset=base + offset)

    with ExitStack() as ctx:
        def sems(stage, *names):
            return namedtuple(stage, names)(*(ctx.enter_context(nc.semaphore(f"{stage}_{n}")) for n in names))

        xs = [nc.dram_tensor(f"x_after_{n}", (TB, P, D), F32, kind="Internal").ap() for n in range(3)]

        ps = ctx.enter_context(nc.psum_tensor("ps", [P, 8, HALF], F32))
        psf = ps[:].rearrange("p b n -> p (b n)")

        ident = at("ident", [P], F32, 0)
        identr = at("identr", [P], F32R, 512)
        mask = at("mask", [P], F32, 1024)
        maskr = at("maskr", [P], F32R, 1536)
        junk = at("junk", [D], BF16, 2048)
        stat = at("stat", [6, 6, TB], F32, 4096)
        power = at("power", [1], F32, 5248)
        neg_max = at("neg_max", [TB], F32, 5280)
        row_sum = at("row_sum", [TB], F32, 5312)
        row_inv = at("row_inv", [TB], F32, 5344)
        row_max = at("row_max", [TB], F32, 5376)
        stat1 = at("stat1", [3, 2 * TB], F32, 5856)

        hth = at("hth", [KT, SEQ], F32R, AT_HT)
        htl = at("htl", [KT, SEQ], F32R, AT_HT + 32 * KB)
        raw = at("raw", [4, D], F32, AT_RAW)
        rows = at("rows", [TB, D], F32, AT_S)
        gain0 = at("gain0", [D], F32, AT_W + 82 * KB)
        GAIN = 2
        xt = at("xt", [2, D], F32, AT_W + 80 * KB)

        def f32(ap):
            return ap.bitcast(F32)

        def three_passes(pe, dst, wh, wl, xh, xl, first, last):
            pe.matmul(dst, wh, xh, start=first, stop=False)
            pe.matmul(dst, wh, xl, start=False, stop=False)
            return pe.matmul(dst, wl, xh, start=False, stop=last)

        E = sems("end", "x_in0", "x_in1", "gain_in", "y_ready", "ss_y", "var_y", "rstd_y", "scaled", "x_new", "ss_x", "var_x",
                 "rstd_x", "hn", "turned", "ht_hi", "ht_lo", "x_out0", "x_out1")

        X_IN = sems("input", *(f"block{tb}" for tb in range(TB)))

        def pre(n, k):
            return TB * n + k

        def post(n, k):
            return TB * (n - 1) + k

        def x_loaded(n, tb):
            if n == 0:
                return X_IN[tb], 16
            return (E.x_in0, E.x_in1)[tb % 2], 16 * (TB // 2 * (n - 1) + tb // 2 + 1)

        def x_stored(n, tb):
            return (E.x_out0, E.x_out1)[tb % 2], 16 * (TB // 2 * (n - 1) + tb // 2 + 1)

        def x_block(n, tb):
            return rows[:, tb, :] if n == 0 else xt[:, tb % 2, :]

        def gains_loaded(n):
            return 16 * (2 * n + 1 if n < 4 else 2 * n)

        x_src = [x, x, *xs]
        x_dst = [None, *xs, out]

        def end_loads(sp, n):
            if n == 0:
                sp.dma_start(rows[:, 0, :], x_src[0][0]).then_inc(x_loaded(0, 0)[0], 16)
                sp.dma_start(gain0[:], gains[0:1, :].partition_broadcast(P)).then_inc(E.gain_in, 16)
                for tb in range(1, TB):
                    if tb <= 3:
                        mla_in_loads(sp, [tb - 1])
                    sp.dma_start(rows[:, tb, :], x_src[0][tb]).then_inc(x_loaded(0, tb)[0], 16)
                    if tb == 3:
                        mla_in_small(sp)
                        mla_in_loads(sp, [3])
                return
            sp.dma_start(raw[:, GAIN, :], gains[2 * n - 1:2 * n, :].partition_broadcast(P)).then_inc(E.gain_in, 16)
            if n < 4:
                sp.dma_start(raw[:, GAIN + 1, :], gains[2 * n:2 * n + 1, :].partition_broadcast(P)).then_inc(E.gain_in, 16)

        def end_x_loads(sp, n):
            sp.dma_start(xt[:, 0, :], x_src[n][0]).then_inc(E.x_in0, 16)
            sp.dma_start(xt[:, 1, :], x_src[n][1]).then_inc(E.x_in1, 16)

        def end_sync(sp, n):
            for tb in range(TB):
                sp.wait_ge(E.x_new, post(n, tb + 1))
                sp.dma_start(x_dst[n][tb], xt[:, tb % 2, :]).then_inc(x_stored(n, tb)[0], 16)
                if tb + 2 < TB:
                    sp.wait_ge(*x_stored(n, tb))
                    if n < 4:
                        sp.wait_ge(E.hn, pre(n, tb + 1))
                    sp.dma_start(xt[:, tb % 2, :], x_src[n][tb + 2]).then_inc(x_loaded(n, tb + 2)[0], 16)
            sp.wait_ge(*x_stored(n, TB - 2))
            sp.wait_ge(*x_stored(n, TB - 1))
            if n < 4:
                sp.wait_ge(E.hn, pre(n, TB))

        DVE_SUMS = 7

        def turned_banks(n, tb):
            bank = tb % 2 * 2 + (0 if n > 0 and tb >= TB - 2 else 4)
            return psf[:, bank * HALF:bank * HALF + D]

        def proj_banks(tb):
            bank = 4 + 2 * tb if tb < 2 else tb % 2 * 2
            return psf[:, bank * HALF:bank * HALF + D]

        def end_late(n, step):
            return n in (0, 1, 3) or step >= TB

        def end_scalar(act, n, step, copies):
            def hi(tb):
                if 0 <= tb < TB and n < 4:
                    act.wait_ge(E.turned, pre(n, tb + 1))
                    src = turned_banks(n, tb).rearrange("p (f t) -> p f t", f=KT)
                    act.activation(hth[:, :, tb * P:(tb + 1) * P], src, ACT.Copy).then_inc(E.ht_hi, 1)

            late = end_late(n, step)
            if step < TB and copies:
                act.wait_ge(copies, step + 1)
                act.activation(rows[:, step, :], proj_banks(step), ACT.Copy).then_inc(E.y_ready, 1)
            if not late:
                hi(step - 2)
            if step < TB and n > 0:
                act.wait_ge(E.y_ready, post(n, step + 1))
                act.wait_ge(E.ss_x, pre(min(n, 3), max(0, step - 1)) if n < 4 else pre(3, TB))
                act.wait_ge(E.ss_y, post(n, step))
                act.activation(junk[:], rows[:, step, :], ACT.Square,
                               accum_out=stat[:, 0, n, step:step + 1]).then_inc(E.ss_y, 1)
            tb = step - 1
            if 0 <= tb < TB and n < 4:
                if n > 0:
                    act.wait_ge(E.x_new, post(n, tb + 1))
                else:
                    act.wait_ge(*x_loaded(n, tb))
                    if tb > LATENT_LAG - 1:
                        act.wait_ge(A.ss, tb - LATENT_LAG + 1)
                act.wait_ge(E.ss_x, pre(n, tb))
                if n > 0:
                    act.wait_ge(E.ss_y, post(n, min(step + 1, TB)))
                act.activation(junk[:], x_block(n, tb), ACT.Square,
                               accum_out=stat[:, 3, n, tb:tb + 1]).then_inc(E.ss_x, 1)
            if late:
                hi(step - 2)

        def end_gpsimd(pool, n, step):
            if step < TB and n > 0:
                col = slice(step, step + 1)
                pool.wait_ge(E.ss_y, post(n, step + 1))
                pool.tensor_scalar(stat[:, 1, n, col], stat[:, 0, n, col], 1.0 / D, NORM_EPS, ALU.mult, ALU.add).then_inc(E.var_y, 1)
                pool.wait_ge(E.var_y, post(n, step + 1))
                pool.tensor_tensor(stat[:, 2, n, col], stat[:, 1, n, col], power[:], ALU.pow).then_inc(E.rstd_y, 1)
            tb = step - 1
            if 0 <= tb < TB:
                col = slice(tb, tb + 1)
                if n < 4:
                    pool.wait_ge(E.ss_x, pre(n, tb + 1))
                    pool.tensor_scalar(stat[:, 4, n, col], stat[:, 3, n, col], 1.0 / D, NORM_EPS, ALU.mult, ALU.add).then_inc(E.var_x, 1)
                    pool.wait_ge(E.var_x, pre(n, tb + 1))
                    pool.tensor_tensor(stat[:, 5, n, col], stat[:, 4, n, col], power[:], ALU.pow).then_inc(E.rstd_x, 1)
            tb = step
            if n > 0 and tb < DVE_SUMS:
                pool.wait_ge(*x_loaded(n, tb))
                pool.wait_ge(E.scaled, post(n, tb + 1))
                pool.tensor_tensor(xt[:, tb % 2, :], xt[:, tb % 2, :], rows[:, tb, :], ALU.add).then_inc(E.x_new, 1)

        def end_vector(dve, n, step):
            def lo(tb):
                if 0 <= tb < TB and n < 4:
                    dve.wait_ge(E.ht_hi, pre(n, tb + 1))
                    src = turned_banks(n, tb).rearrange("p (f t) -> p f t", f=KT)
                    dst = slice(tb * P, (tb + 1) * P)
                    dve.tensor_tensor(htl[:, :, dst], src, f32(hth[:, :, dst]), ALU.subtract).then_inc(E.ht_lo, 1)

            if not end_late(n, step):
                lo(step - 2)
            tb = step
            if tb < TB and n > 0:
                if tb == 0:
                    dve.wait_ge(E.gain_in, gains_loaded(n))
                dve.wait_ge(E.rstd_y, post(n, tb + 1))
                dve.scalar_tensor_tensor(out=rows[:, tb, :], in0=rows[:, tb, :], scalar=stat[:, 2, n, tb:tb + 1],
                                         in1=raw[:, GAIN, :], op0=ALU.mult, op1=ALU.mult).then_inc(E.scaled, 1)
                if tb >= DVE_SUMS:
                    dve.wait_ge(*x_loaded(n, tb))
                    dve.wait_ge(E.scaled, post(n, tb + 1))
                    dve.wait_ge(E.x_new, post(n, tb))
                    dve.tensor_tensor(xt[:, tb % 2, :], xt[:, tb % 2, :], rows[:, tb, :], ALU.add).then_inc(E.x_new, 1)
            tb = step - 1
            if 0 <= tb < TB and n < 4:
                if n == 0 and tb == 0:
                    dve.wait_ge(E.gain_in, gains_loaded(n))
                if n == 0:
                    dve.wait_ge(*x_loaded(n, tb))
                else:
                    dve.wait_ge(E.x_new, post(n, tb + 1))
                dve.wait_ge(E.rstd_x, pre(n, tb + 1))
                dve.scalar_tensor_tensor(out=rows[:, tb, :], in0=x_block(n, tb), scalar=stat[:, 5, n, tb:tb + 1],
                                         in1=gain0[:] if n == 0 else raw[:, GAIN + 1, :], op0=ALU.mult, op1=ALU.mult).then_inc(E.hn, 1)
            if end_late(n, step):
                lo(step - 2)

        def end_tensor(pe, n, tb):
            if not 0 <= tb < TB or n == 4:
                return
            pe.wait_ge(E.hn, pre(n, tb + 1))
            if n > 0 and tb >= TB - 2:
                pe.wait_ge(E.y_ready, post(n, tb + 1))
            elif tb >= 2:
                pe.wait_ge(E.ht_lo, pre(n, tb - 1))
            dst = turned_banks(n, tb)
            for f in range(KT):
                mm = pe.transpose(dst[:, f * P:(f + 1) * P], rows[:, tb, f * P:(f + 1) * P], ident[:])
            mm.then_inc(E.turned, 1)

        def end_tensor_step(pe, n, step, fills):
            end_tensor(pe, n, step - 2)
            if step in FILL_STEPS and fills:
                fills[FILL_STEPS.index(step)]()

        STEPS = TB + 2
        FILL_STEPS = (TB - 1, TB + 1)
        LATENT_LAG = 3
        EARLY = (5, 7)

        aT = at("aT", [KT * SEQ], F32, AT_S)
        wo_h = [at(f"wo_h{k}", [D], F32R, AT_W + 8 * KB * k) for k in range(KT)]
        wo_l = [at(f"wo_l{k}", [D], F32R, AT_W + 8 * KB * k + 4 * KB) for k in range(KT)]
        PROJ = {n: sems(f"proj{n}", "raw_in0", "raw_in1", "raw_in2", "raw_in3", "w_hi", "w_lo", "a_hi", "a_lo", "y_done")
                for n in (1, 3)}

        PROJ_SLOTS = {1: 4, 3: 3}

        def proj_arrival(n, k):
            q, slots = PROJ[n], PROJ_SLOTS[n]
            return (q.raw_in0, q.raw_in1, q.raw_in2, q.raw_in3)[k % slots], 16 * (k // slots + 1)

        def proj_loads(sp, n, w, slots_free):
            slots = PROJ_SLOTS[n]
            for k in range(KT):
                if k < slots:
                    sp.wait_ge(*slots_free[k])
                else:
                    sp.wait_ge(PROJ[n].w_lo, k - slots + 1)
                sp.dma_start(raw[:, k % slots, :], w[k]).then_inc(proj_arrival(n, k)[0], 16)

        def proj_w_hi(act, n, *ks):
            for k in ks:
                act.wait_ge(*proj_arrival(n, k))
                act.activation(wo_h[k][:], raw[:, k % PROJ_SLOTS[n], :], ACT.Copy).then_inc(PROJ[n].w_hi, 1)

        def proj_w_lo(dve, n, *ks):
            for k in ks:
                dve.wait_ge(PROJ[n].w_hi, k + 1)
                dve.tensor_tensor(wo_l[k][:], raw[:, k % PROJ_SLOTS[n], :], f32(wo_h[k][:]), ALU.subtract).then_inc(PROJ[n].w_lo, 1)

        def proj_a_hi(act, n, half, *ks):
            for k in ks:
                cut = slice(half * HALF, (half + 1) * HALF)
                act.activation(hth[:, k, cut], aT[:, k * SEQ + cut.start:k * SEQ + cut.stop], ACT.Copy).then_inc(PROJ[n].a_hi, 1)

        def proj_a_lo(dve, n, half, *ks):
            for k in ks:
                cut = slice(half * HALF, (half + 1) * HALF)
                dve.wait_ge(PROJ[n].a_hi, KT * half + k + 1)
                dve.tensor_tensor(htl[:, k, cut], aT[:, k * SEQ + cut.start:k * SEQ + cut.stop], f32(hth[:, k, cut]),
                                  ALU.subtract).then_inc(PROJ[n].a_lo, 1)

        def proj1_scalar(act):
            act.wait_ge(B.out_copied, OUTS * GROUPS - 2)
            for k in range(KT):
                proj_w_hi(act, 1, k)
                if k == KT - 1:
                    act.wait_ge(B.out_copied, OUTS * GROUPS)
                proj_a_hi(act, 1, 0, k)
            proj_a_hi(act, 1, 1, *range(KT))
            act.wait_ge(PROJ[1].a_lo, 2 * KT)

        def proj1_vector(dve):
            for k in range(KT):
                proj_w_lo(dve, 1, k)
                proj_a_lo(dve, 1, 0, k)
            proj_a_lo(dve, 1, 1, *range(KT))

        def proj3_scalar(act):
            proj_w_hi(act, 3, 3)
            proj_a_hi(act, 3, 0, 4, 5)
            act.wait_ge(L.ix, CH)
            proj_w_hi(act, 3, 4)
            act.wait_ge(L.out, CH)
            proj_a_hi(act, 3, 0, 6)
            act.wait_ge(L.b, CH)
            proj_w_hi(act, 3, 5)
            act.wait_ge(L.out, CH + 1)
            proj_w_hi(act, 3, 6)
            proj_a_hi(act, 3, 0, 7)
            proj_w_hi(act, 3, 7)
            proj_a_hi(act, 3, 1, *range(KT))
            act.wait_ge(PROJ[3].a_lo, 2 * KT)

        def proj3_vector(dve):
            for k in range(4, KT):
                proj_a_lo(dve, 3, 0, k)
                proj_w_lo(dve, 3, k)
            proj_a_lo(dve, 3, 1, *range(KT))

        TOGETHER = {1: 4, 3: 5}

        def proj_tensor(pe, n, fills):
            q = PROJ[n]

            def product(tb, k):
                blk = slice(tb * P, (tb + 1) * P)
                for c in range(D // HALF):
                    cut = slice(c * HALF, (c + 1) * HALF)
                    mm = three_passes(pe, proj_banks(tb)[:, cut], hth[:, k, blk], htl[:, k, blk], wo_h[k][:, cut], wo_l[k][:, cut],
                                      k == 0, k == KT - 1)
                if k == KT - 1:
                    mm.then_inc(q.y_done, 1)

            def parts_wait(k):
                pe.wait_ge(q.w_lo, k + 1)
                pe.wait_ge(q.a_lo, k + 1)

            for k in range(TOGETHER[n]):
                parts_wait(k)
                for tb in range(TB // 2):
                    if n == 3 and k == 0 and tb == 2:
                        pe.wait_ge(L.sigmoid, 2 * CH)
                    product(tb, k)
            for tb, turned in enumerate(((), (), (), (0,), (1, 2), (3,), (4,), (5,))):
                if tb >= TB // 2:
                    pe.wait_ge(E.y_ready, post(n, tb - 1))
                for k in range(TOGETHER[n] if tb < TB // 2 else 0, KT):
                    if tb == 0:
                        parts_wait(k)
                    if tb == TB // 2:
                        pe.wait_ge(q.a_lo, KT + k + 1)
                    product(tb, k)
                for t in turned:
                    end_tensor(pe, n, t)
            fills[0]()
            end_tensor(pe, n, TB - 2)
            end_tensor(pe, n, TB - 1)
            fills[1]()

        u_h = at("u_h", [FG, SEQ], F32R, AT_W)
        u_l = at("u_l", [FG, SEQ], F32R, AT_W + 16 * KB)
        dn_h = at("dn_h", [FG, D], F32R, AT_W + 32 * KB)
        dn_l = at("dn_l", [FG, D], F32R, AT_W + 48 * KB)
        up_h = [at(f"up_h{s}", [KT, P], F32R, AT_W + (72 - 8 * s) * KB) for s in range(2)]
        up_l = [at(f"up_l{s}", [KT, P], F32R, AT_W + (76 - 8 * s) * KB) for s in range(2)]
        relu = at("relu", [2, HALF], F32, AT_W + 80 * KB)
        squared = at("squared", [2, HALF], F32, AT_W + 84 * KB)
        MLP = {n: sems(f"mlp{n}", "raw_in0", "raw_in1", "raw_in2", "raw_in3", "w_hi", "w_lo", "up_done", "relu", "sq",
                       "u_hi", "u_lo", "down_done", "y_sum") for n in (2, 4)}
        SLOT = {("up", 0): 0, ("up", 1): 1, ("down", 0): 2, ("down", 1): 3,
                ("up", 2): 0, ("down", 2): 1, ("up", 3): 2, ("down", 3): 3}

        def mlp_loads_first(sp, n, layer, kinds):
            q = MLP[n]
            if "up" in kinds:
                sp.dma_start(raw[:, 0, :], w_up[layer, 0]).then_inc(q.raw_in0, 16)
                sp.dma_start(raw[:, 1, :], w_up[layer, 1]).then_inc(q.raw_in1, 16)
            if "down" in kinds:
                sp.dma_start(raw[:, 2, :], w_down[layer, 0]).then_inc(q.raw_in2, 16)
                sp.dma_start(raw[:, 3, :], w_down[layer, 1]).then_inc(q.raw_in3, 16)

        SPLITS = [("down", 0), ("down", 1), ("up", 2), ("down", 2), ("up", 3), ("down", 3), ("up", 4), ("up", 5)]

        UP_ORDER = [(0, 0), (1, 0), (0, 1), (1, 1), (2, 0), (2, 1), (3, 0), (3, 1)]

        def mlp_sync(sp, n, layer):
            q = MLP[n]
            ins = (q.raw_in0, q.raw_in1, q.raw_in2, q.raw_in3)

            def load(src, row, slot, split_before):
                sp.wait_ge(q.w_lo, split_before)
                sp.dma_start(raw[:, slot, :], src[layer, row]).then_inc(ins[slot], 16)

            def group(g, last):
                rows_ = [sp.snap(g * FG + i) for i in range(2, FG + 2)] if not isinstance(g, int) else [g * FG + i for i in range(2, FG + 2)]
                load(w_up, rows_[0], 0, 8 * g + 1)
                load(w_down, rows_[0], 1, 8 * g + 2)
                load(w_up, rows_[1], 2, 8 * g + 3)
                load(w_down, rows_[1], 3, 8 * g + 4)
                if not last:
                    load(w_up, rows_[2], 0, 8 * g + 5)
                    load(w_up, rows_[3], 1, 8 * g + 6)
                    load(w_down, rows_[2], 2, 8 * g + 7)
                    load(w_down, rows_[3], 3, 8 * g + 8)

            with sp.Fori(0, MLP_GROUPS - 1) as g:
                group(g, False)
            group(MLP_GROUPS - 1, True)

        def mlp_chunk(n, g, kind, i):
            slot = SLOT[kind, i % FG]
            early = (kind, i) in (("down", 0), ("down", 1))
            arrived = 32 * g + (16 if early else 32 if i < FG else 48)
            if kind == "up":
                return slot, arrived, up_h[i % 2][:].rearrange("p a b -> p (a b)"), up_l[i % 2][:].rearrange("p a b -> p (a b)")
            return slot, arrived, dn_h[:, i, :], dn_l[:, i, :]

        def mlp_first_up(n, i):
            return i, 16, up_h[i][:].rearrange("p a b -> p (a b)"), up_l[i][:].rearrange("p a b -> p (a b)")

        def split_hi(act, q, chunk):
            slot, arrived, hi, lo = chunk
            act.wait_ge((q.raw_in0, q.raw_in1, q.raw_in2, q.raw_in3)[slot], arrived)
            act.activation(hi, raw[:, slot, 0:hi.shape[1]], ACT.Copy).then_inc(q.w_hi, 1)

        def split_lo(dve, q, chunk, count):
            slot, arrived, hi, lo = chunk
            dve.wait_ge(q.w_hi, count)
            dve.tensor_tensor(lo, raw[:, slot, 0:hi.shape[1]], f32(hi), ALU.subtract).then_inc(q.w_lo, 1)

        def mlp_scalar(act, n):
            q = MLP[n]

            def evacuate(g, *numbers):
                for i in numbers:
                    ft, half = UP_ORDER[i]
                    act.wait_ge(q.up_done, 8 * g + i + 1)
                    if i >= 2:
                        act.wait_ge(q.sq, 8 * g + i - 1)
                    act.activation(relu[:, i % 2, :], ps[:, 4 + i % 4, :], ACT.Relu).then_inc(q.relu, 1)
                    act.wait_ge(q.relu, 8 * g + i + 1)
                    act.activation(u_h[:, ft, half * HALF:(half + 1) * HALF], relu[:, i % 2, :], ACT.Square).then_inc(q.u_hi, 1)

            def group(g, last):
                split_hi(act, q, mlp_chunk(n, g, *SPLITS[0]))
                split_hi(act, q, mlp_chunk(n, g, *SPLITS[1]))
                evacuate(g, 0, 1, 2)
                split_hi(act, q, mlp_chunk(n, g, *SPLITS[2]))
                split_hi(act, q, mlp_chunk(n, g, *SPLITS[3]))
                evacuate(g, 3)
                split_hi(act, q, mlp_chunk(n, g, *SPLITS[4]))
                split_hi(act, q, mlp_chunk(n, g, *SPLITS[5]))
                evacuate(g, 4, 5)
                if not last:
                    split_hi(act, q, mlp_chunk(n, g, *SPLITS[6]))
                evacuate(g, 6, 7)
                if not last:
                    split_hi(act, q, mlp_chunk(n, g, *SPLITS[7]))

            act.wait_ge(*x_stored(n - 1, TB - 2))
            act.wait_ge(*x_stored(n - 1, TB - 1))
            with act.Fori(0, MLP_GROUPS - 1) as g:
                group(g, False)
                act.wait_ge(q.down_done, 8 * g + 8)
            group(MLP_GROUPS - 1, True)

        def mlp_vector(dve, n, early):
            q = MLP[n]

            def evacuate(g, *numbers):
                for i in numbers:
                    ft, half = UP_ORDER[i]
                    cut = slice(half * HALF, (half + 1) * HALF)
                    dve.wait_ge(q.sq, 8 * g + i + 1)
                    dve.wait_ge(q.u_hi, 8 * g + i + 1)
                    dve.tensor_tensor(u_l[:, ft, cut], squared[:, i % 2, :], f32(u_h[:, ft, cut]), ALU.subtract).then_inc(q.u_lo, 1)

            def group(g, last):
                split_lo(dve, q, mlp_chunk(n, g, *SPLITS[0]), 8 * g + 3)
                split_lo(dve, q, mlp_chunk(n, g, *SPLITS[1]), 8 * g + 4)
                evacuate(g, 0, 1, 2)
                split_lo(dve, q, mlp_chunk(n, g, *SPLITS[2]), 8 * g + 5)
                split_lo(dve, q, mlp_chunk(n, g, *SPLITS[3]), 8 * g + 6)
                evacuate(g, 3)
                split_lo(dve, q, mlp_chunk(n, g, *SPLITS[4]), 8 * g + 7)
                split_lo(dve, q, mlp_chunk(n, g, *SPLITS[5]), 8 * g + 8)
                evacuate(g, 4, 5)
                if not last:
                    split_lo(dve, q, mlp_chunk(n, g, *SPLITS[6]), 8 * g + 9)
                evacuate(g, 6, 7)
                if not last:
                    split_lo(dve, q, mlp_chunk(n, g, *SPLITS[7]), 8 * g + 10)

            def add(g, tb, signal):
                dve.wait_ge(q.down_done, 8 * g + tb + 1)
                ins = dve.tensor_tensor(rows[:, tb, :], psf[:, tb % 2 * D:tb % 2 * D + D], rows[:, tb, :], ALU.add)
                ins.then_inc(signal, 1)

            dve.wait_ge(q.y_sum, 1)
            with dve.Fori(0, MLP_GROUPS - 1) as g:
                group(g, False)
                for tb in range(TB):
                    add(g, tb, q.y_sum)
            group(MLP_GROUPS - 1, True)
            dve.wait_ge(q.y_sum, 1 + TB * (MLP_GROUPS - 1))
            for step in range(STEPS):
                if step < TB:
                    add(MLP_GROUPS - 1, step, E.y_ready)
                end_vector(dve, n, step)
                if step in EARLY:
                    early(EARLY.index(step))

        def mlp_gpsimd(pool, n):
            q = MLP[n]
            pool.wait_ge(E.turned, pre(n - 1, TB))
            pool.memset(rows[:], 0.0).then_inc(q.y_sum, 1)

            def group(g):
                for i in range(2 * FG):
                    pool.wait_ge(q.relu, 8 * g + i + 1)
                    if i >= 2:
                        pool.wait_ge(q.u_lo, 8 * g + i - 1)
                    pool.tensor_tensor(squared[:, i % 2, :], relu[:, i % 2, :], relu[:, i % 2, :], ALU.mult).then_inc(q.sq, 1)

            with pool.Fori(0, MLP_GROUPS - 1) as g:
                group(g)
            group(MLP_GROUPS - 1)

        def mlp_up(pe, n, g, i):
            q = MLP[n]
            ft, half = UP_ORDER[i]
            if i < 2:
                pe.wait_ge(E.ht_lo, pre(n - 1, TB // 2 + 1))
            elif i == 2:
                pe.wait_ge(E.ht_lo, pre(n - 1, TB))
            pe.wait_ge(q.w_lo, 8 * g + (1, 2, 5, 7)[ft])
            if i >= 4:
                pe.wait_ge(q.relu, 8 * g + i - 3)
            for k in range(KT):
                mm = three_passes(pe, ps[:, 4 + i % 4, :], up_h[ft % 2][:, k, :], up_l[ft % 2][:, k, :],
                                  hth[:, k, half * HALF:(half + 1) * HALF], htl[:, k, half * HALF:(half + 1) * HALF],
                                  k == 0, k == KT - 1)
            mm.then_inc(q.up_done, 1)

        UP_AHEAD = 2

        def mlp_tensor(pe, n, fills):
            q = MLP[n]

            def down(g, tb, bank_free):
                blk = slice(tb * P, (tb + 1) * P)
                if tb == 0:
                    pe.wait_ge(q.w_lo, 8 * g + 8)
                bank_free(tb)
                for ft in range(FG):
                    if tb == 0:
                        pe.wait_ge(q.u_lo, 8 * g + UP_ORDER.index((ft, 1)) + 1)
                    for c in range(D // HALF):
                        cut = slice(c * HALF, (c + 1) * HALF)
                        mm = three_passes(pe, ps[:, tb % 2 * 2 + c, :], u_h[:, ft, blk], u_l[:, ft, blk],
                                          dn_h[:, ft, cut], dn_l[:, ft, cut], ft == 0, ft == FG - 1)
                mm.then_inc(q.down_done, 1)

            with pe.Fori(0, MLP_GROUPS - 1) as g:
                for i in range(UP_AHEAD, 2 * FG):
                    mlp_up(pe, n, g, i)

                def bank_free(tb):
                    pe.wait_ge(q.y_sum, 8 * g + tb if tb >= 2 else 8 * g + 1)

                for tb in range(TB):
                    down(g, tb, bank_free)
                for i in range(UP_AHEAD):
                    mlp_up(pe, n, g + 1, i)
            for i in range(UP_AHEAD, 2 * FG):
                mlp_up(pe, n, MLP_GROUPS - 1, i)

            def last_bank_free(tb):
                if tb < 2:
                    pe.wait_ge(q.y_sum, 1 + TB * (MLP_GROUPS - 1))
                else:
                    pe.wait_ge(E.y_ready, post(n, tb - 1))

            for step in range(STEPS):
                if step < TB:
                    down(MLP_GROUPS - 1, step, last_bank_free)
                if step == 0:
                    pe.wait_ge(q.relu, 8 * MLP_GROUPS)
                end_tensor_step(pe, n, step, fills)

        wq_h = at("wq_h", [KT, QRANK], F32R, AT_S)
        wq_l = at("wq_l", [KT, QRANK], F32R, AT_S + 12 * KB)
        KVW = KVRANK + ROPE
        wkv_h = at("wkv_h", [KT, KVW], F32R, AT_W + 24 * KB)
        wkv_l = at("wkv_l", [KT, KVW], F32R, AT_W + 34 * KB)
        cq_h = at("cq_h", [QK, SEQ], F32R, AT_W + 44 * KB)
        cq_l = at("cq_l", [QK, SEQ], F32R, AT_W + 56 * KB)
        ckv_h = at("ckv_h", [KK, SEQ], F32R, AT_W)
        ckv_l = at("ckv_l", [KK, SEQ], F32R, AT_W + 8 * KB)
        krot_h = at("krot_h", [SEQ], F32R, AT_W + 16 * KB)
        krot_l = at("krot_l", [SEQ], F32R, AT_W + 20 * KB)
        o = AT_W + 68 * KB
        latent = at("latent", [2, QRANK], F32, o)
        krope = at("krope", [TB, ROPE], F32, o + 3 * KB)
        kturn = at("kturn", [TB, 2, ROPE], F32, o + 5 * KB)
        lgain = at("lgain", [QRANK + KVRANK], F32, o + 9 * KB)
        angle = at("angle", [TB, RH], F32, o + 12 * KB)
        turns = at("turns", [TB, RH], F32, o + 13 * KB)
        ktmp = at("ktmp", [4, TB, RH], F32, o + 14 * KB)
        sine = at("sine", [TB, RH], F32, o + 18 * KB)
        cosine = at("cosine", [TB, RH], F32, o + 19 * KB)
        pos_i = at("pos_i", [TB], I32, 6112)
        pos_f = at("pos_f", [TB], F32, 6144)
        freq = at("freq", [RH], F32, 6176)

        A = sems("mla_in", "raw_in0", "raw_in1", "raw_in2", "raw_in3", "w_hi", "w_lo", "small_in", "lgain_in", "product", "ss", "var",
                 "rstd", "normed", "krope", "turned", "hi", "lo", "trig", "reduced", "half_sine", "krot", "kturned", "k_hi", "k_lo")
        IN_CHUNKS = [(w_in_kv, wkv_h, wkv_l, 0), (w_in_kv, wkv_h, wkv_l, 1), (w_in_kv, wkv_h, wkv_l, 2),
                     (w_in_q, wq_h, wq_l, 0), (w_in_q, wq_h, wq_l, 1), (w_in_q, wq_h, wq_l, 2)]

        def flat(t):
            return t[:].rearrange("p a b -> p (a b)")

        def in_cut(c):
            w, hi, lo, i = IN_CHUNKS[c]
            return slice(i * D, min((i + 1) * D, w.shape[1]))

        def mla_in_loads(sp, chunks):
            for c in chunks:
                w, cut = IN_CHUNKS[c][0], in_cut(c)
                if c >= 4:
                    sp.wait_ge(A.w_lo, c - 3)
                sp.dma_start(raw[:, c % 4, 0:cut.stop - cut.start], w[:, cut]).then_inc((A.raw_in0, A.raw_in1, A.raw_in2, A.raw_in3)[c % 4], 16)

        def mla_in_small(sp):
            with nc.allow_non_contiguous_dma(reason="1024 positions, 4 bytes each"):
                sp.dma_start(pos_i[:], positions).then_inc(A.small_in, 16)
            sp.dma_start(freq[:], inv_freq[0:1, :].partition_broadcast(P)).then_inc(A.small_in, 16)
            sp.dma_start(lgain[:], qkv_gain[0:1, :].partition_broadcast(P)).then_inc(A.lgain_in, 16)

        def mla_in_split_hi(act, chunks):
            for c in chunks:
                w, hi, lo, i = IN_CHUNKS[c]
                cut = in_cut(c)
                if c == 3:
                    act.wait_ge(E.turned, pre(0, TB))
                act.wait_ge((A.raw_in0, A.raw_in1, A.raw_in2, A.raw_in3)[c % 4], 16 * (c // 4 + 1))
                act.activation(flat(hi)[:, cut], raw[:, c % 4, 0:cut.stop - cut.start], ACT.Copy).then_inc(A.w_hi, 1)

        def mla_in_split_lo(dve, chunks):
            for c in chunks:
                w, hi, lo, i = IN_CHUNKS[c]
                cut = in_cut(c)
                dve.wait_ge(A.w_hi, c + 1)
                dve.tensor_tensor(flat(lo)[:, cut], raw[:, c % 4, 0:cut.stop - cut.start], f32(flat(hi)[:, cut]),
                                  ALU.subtract).then_inc(A.w_lo, 1)

        IN_SPLITS = {1: [0], 2: [1, 2], 9: [3], 10: [4, 5]}

        def latent_of(i):
            return (KVRANK, QRANK, KK, ckv_h, ckv_l) if i < TB else (QRANK, 0, QK, cq_h, cq_l)

        def mla_in_scalar(act):
            for step in range(LATENT_LAG + 2 * TB + 1):
                if step < STEPS:
                    end_scalar(act, 0, step, None)
                if step in IN_SPLITS:
                    mla_in_split_hi(act, IN_SPLITS[step])
                i = step - LATENT_LAG
                if i < 0:
                    continue
                if i < 2 * TB:
                    rank = latent_of(i)[0]
                    act.wait_ge(A.product, i + 1)
                    act.wait_ge(E.ss_x, pre(0, min(step, TB)))
                    if i > 0:
                        act.wait_ge(A.ss, i)
                    act.activation(junk[:, 0:rank], ps[:, i % 2, 0:rank], ACT.Square,
                                   accum_out=stat1[:, 0, i:i + 1]).then_inc(A.ss, 1)
                if i >= 1:
                    tb, (rank, _, tiles, hi, lo) = (i - 1) % TB, latent_of(i - 1)
                    act.wait_ge(A.turned, i)
                    src = ps[:, 2 + (i - 1) % 2, 0:tiles * P].rearrange("p (f t) -> p f t", f=tiles)
                    act.activation(hi[:, :, tb * P:(tb + 1) * P], src, ACT.Copy).then_inc(A.hi, 1)
                if i == TB + 1:
                    act.wait_ge(A.trig, 6)
                    act.activation(sine[:], angle[:], ACT.Sin).then_inc(A.half_sine, 1)
                    act.activation(cosine[:], angle[:], ACT.Sin, scale=0.5).then_inc(A.half_sine, 1)
                if i == TB + 6:
                    for c in range(2):
                        act.wait_ge(A.kturned, c + 1)
                        act.activation(krot_h[:, c * HALF:(c + 1) * HALF], ps[:, 4 + c, :], ACT.Copy).then_inc(A.k_hi, 1)
            act.wait_ge(A.ss, 2 * TB)

        def mla_in_gpsimd(pool):
            for step in range(LATENT_LAG + 2 * TB):
                if step < STEPS:
                    end_gpsimd(pool, 0, step)
                i = step - LATENT_LAG
                if i < 0:
                    continue
                rank = latent_of(i)[0]
                col = slice(i, i + 1)
                pool.wait_ge(A.ss, i + 1)
                pool.tensor_scalar(stat1[:, 1, col], stat1[:, 0, col], 1.0 / rank, NORM_EPS, ALU.mult, ALU.add).then_inc(A.var, 1)
                pool.wait_ge(A.var, i + 1)
                pool.tensor_tensor(stat1[:, 2, col], stat1[:, 1, col], power[:], ALU.pow).then_inc(A.rstd, 1)

        def mla_angles(dve):
            two_pi = 2 * np.pi
            parts, rest = [], two_pi
            for _ in range(3):
                e = np.floor(np.log2(rest)) - 7
                part = np.floor(rest / 2.0 ** e) * 2.0 ** e
                parts.append(float(part))
                rest -= part
            parts.append(float(np.float32(rest)))
            dve.wait_ge(A.small_in, 32)
            dve.tensor_copy(pos_f[:], pos_i[:]).then_inc(A.trig, 1)
            dve.wait_ge(A.trig, 1)
            for tb in range(TB):
                ins = dve.tensor_scalar(angle[:, tb, :], freq[:], pos_f[:, tb:tb + 1], None, ALU.mult)
            ins.then_inc(A.trig, 1)
            dve.wait_ge(A.trig, 2)
            half_ulp = float(1.5 * 2 ** 23)
            dve.tensor_scalar(turns[:], angle[:], float(1 / two_pi), half_ulp, ALU.mult, ALU.add).then_inc(A.trig, 1)
            dve.wait_ge(A.trig, 3)
            dve.tensor_scalar(turns[:], turns[:], half_ulp, None, ALU.subtract).then_inc(A.trig, 1)
            dve.wait_ge(A.trig, 4)
            for i, part in enumerate(parts):
                ins = dve.scalar_tensor_tensor(out=angle[:], in0=turns[:], scalar=-part, in1=angle[:], op0=ALU.mult, op1=ALU.add)
                if i < 3:
                    ins.then_inc(A.reduced, 1)
                    dve.wait_ge(A.reduced, i + 1)
            ins.then_inc(A.trig, 1)
            dve.wait_ge(A.trig, 5)
            pi = float(np.nextafter(np.float32(np.pi), np.float32(0)))
            dve.tensor_scalar(angle[:], angle[:], pi, -pi, ALU.min, ALU.max).then_inc(A.trig, 1)

        def mla_in_vector(dve):
            for step in range(LATENT_LAG + 2 * TB + 1):
                if step < STEPS:
                    end_vector(dve, 0, step)
                if step in IN_SPLITS:
                    mla_in_split_lo(dve, IN_SPLITS[step])
                i = step - LATENT_LAG
                if i < 0:
                    continue
                if i < 2 * TB:
                    tb, (rank, off, tiles, hi, lo) = i % TB, latent_of(i)
                    if i == 0:
                        dve.wait_ge(A.lgain_in, 16)
                    dve.wait_ge(A.rstd, i + 1)
                    if i >= 2:
                        dve.wait_ge(A.turned, i - 1)
                    dve.scalar_tensor_tensor(out=latent[:, i % 2, 0:rank], in0=ps[:, i % 2, 0:rank], scalar=stat1[:, 2, i:i + 1],
                                             in1=lgain[:, off:off + rank], op0=ALU.mult, op1=ALU.mult).then_inc(A.normed, 1)
                    if i < TB:
                        dve.tensor_copy(krope[:, tb, :], ps[:, i % 2, KVRANK:KVW]).then_inc(A.krope, 1)
                if i >= 1:
                    tb, (rank, _, tiles, hi, lo) = (i - 1) % TB, latent_of(i - 1)
                    dst = slice(tb * P, (tb + 1) * P)
                    dve.wait_ge(A.hi, i)
                    src = ps[:, 2 + (i - 1) % 2, 0:tiles * P].rearrange("p (f t) -> p f t", f=tiles)
                    dve.tensor_tensor(lo[:, :, dst], src, f32(hi[:, :, dst]), ALU.subtract).then_inc(A.lo, 1)
                if i == TB:
                    mla_angles(dve)
                if i == TB + 2:
                    dve.wait_ge(A.half_sine, 2)
                    dve.tensor_tensor(cosine[:], cosine[:], cosine[:], ALU.mult).then_inc(A.trig, 1)
                    dve.wait_ge(A.trig, 7)
                    dve.tensor_scalar(cosine[:], cosine[:], -2.0, 1.0, ALU.mult, ALU.add).then_inc(A.trig, 1)
                    dve.wait_ge(A.trig, 8)
                if i == TB + 3:
                    dve.wait_ge(A.krope, TB)
                    dve.wait_ge(E.hn, pre(0, TB))
                    k1, k2 = krope[:, :, 0:RH], krope[:, :, RH:ROPE]
                    dve.tensor_tensor(ktmp[:, 0], k1, cosine[:], ALU.mult)
                    dve.tensor_tensor(ktmp[:, 1], k2, sine[:], ALU.mult)
                    dve.tensor_tensor(ktmp[:, 2], k2, cosine[:], ALU.mult)
                    dve.tensor_tensor(ktmp[:, 3], k1, sine[:], ALU.mult).then_inc(A.krot, 1)
                    dve.wait_ge(A.krot, 1)
                    for c in range(2):
                        dve.tensor_tensor(kturn[:, :, c, 0:RH], ktmp[:, 0], ktmp[:, 1], ALU.subtract)
                        ins = dve.tensor_tensor(kturn[:, :, c, RH:ROPE], ktmp[:, 2], ktmp[:, 3], ALU.add)
                    ins.then_inc(A.krot, 1)
                if i == TB + 6:
                    for c in range(2):
                        cut = slice(c * HALF, (c + 1) * HALF)
                        dve.wait_ge(A.k_hi, c + 1)
                        dve.tensor_tensor(krot_l[:, cut], ps[:, 4 + c, :], f32(krot_h[:, cut]), ALU.subtract).then_inc(A.k_lo, 1)

        def mla_in_tensor(pe):
            def turn(i):
                tiles = latent_of(i)[2]
                pe.wait_ge(A.normed, i + 1)
                if i >= 2:
                    pe.wait_ge(A.lo, i - 1)
                for f in range(tiles):
                    mm = pe.transpose(ps[:, 2 + i % 2, f * P:(f + 1) * P], latent[:, i % 2, f * P:(f + 1) * P], ident[:])
                mm.then_inc(A.turned, 1)

            for step in range(LATENT_LAG + 2 * TB):
                end_tensor(pe, 0, step - 2)
                i = step - LATENT_LAG
                if i < 0:
                    continue
                tb = i % TB
                blk = slice(tb * P, (tb + 1) * P)
                if i < TB:
                    pe.wait_ge(E.ht_lo, pre(0, i + 1))
                    width, wh, wl = KVW, wkv_h, wkv_l
                else:
                    width, wh, wl = QRANK, wq_h, wq_l
                if i >= 2:
                    pe.wait_ge(A.normed, i - 1)
                    if i - 2 < TB:
                        pe.wait_ge(A.krope, i - 1)
                for k in range(KT):
                    if i % TB == 0:
                        pe.wait_ge(A.w_lo, (0 if i < TB else 3) + ((k + 1) * width - 1) // D + 1)
                    mm = three_passes(pe, ps[:, i % 2, 0:width], hth[:, k, blk], htl[:, k, blk], wh[:, k, :], wl[:, k, :],
                                      k == 0, k == KT - 1)
                mm.then_inc(A.product, 1)
                if i >= 1:
                    turn(i - 1)
                if i == TB + 5:
                    pe.wait_ge(A.krot, 2)
                    for c in range(2):
                        for t in range(4):
                            tb = 4 * c + t
                            mm = pe.transpose(ps[:, 4 + c, t * P:(t + 1) * P], kturn[:, tb].rearrange("p a b -> p (a b)"), ident[:])
                        mm.then_inc(A.kturned, 1)
            turn(2 * TB - 1)

        qn_h = [at(f"qn_h{s}", [SEQ], F32R, AT_HT + (16 * s + 0) * KB) for s in range(2)]
        qn_l = [at(f"qn_l{s}", [SEQ], F32R, AT_HT + (16 * s + 4) * KB) for s in range(2)]
        kn_h = [at(f"kn_h{s}", [SEQ], F32R, AT_HT + (16 * s + 8) * KB) for s in range(2)]
        kn_l = [at(f"kn_l{s}", [SEQ], F32R, AT_HT + (16 * s + 12) * KB) for s in range(2)]
        v_h = at("v_h", [TB, 2, VDIM], F32R, AT_HT + 32 * KB)
        v_l = [at("v_l0", [4, 2, VDIM], F32R, AT_RAW + 12 * KB), at("v_l1", [4, 2, VDIM], F32R, AT_W + 81 * KB)]
        pt_h = at("pt_h", [2, HALF], F32R, AT_HT + 40 * KB)
        pt_l = at("pt_l", [2, HALF], F32R, AT_HT + 44 * KB)
        qrot = at("qrot", [GH, SEQ], F32R, AT_HT + 48 * KB)
        hw_h = [at(f"hw_h{s}", [HEADW], F32R, AT_W + (24 + 5 * s) * KB) for s in range(2)]
        hw_l = [at(f"hw_l{s}", [HEADW], F32R, AT_W + (24 + 5 * s) * KB + 4 * HEADW) for s in range(2)]
        vw_h = at("vw_h", [PAIRW], F32R, AT_W + 34 * KB)
        vw_l = at("vw_l", [PAIRW], F32R, AT_W + 36 * KB)
        rw_h = at("rw_h", [QK, GH * ROPE], F32R, AT_W + 38 * KB)
        rw_l = at("rw_l", [QK, GH * ROPE], F32R, AT_W + 41 * KB)
        probs_first = at("probs_first", [10 * P], F32, AT_W + 38 * KB)
        probs_second = at("probs_second", [26 * P], F32, AT_W + 68 * KB)
        qr = [at("qr0", [2, GH, ROPE], F32, AT_W + 84 * KB), at("qr1", [2, GH, ROPE], F32, AT_HT + 44 * KB)]
        qsplit = [at("qsplit0", [2, GH, 2, ROPE], F32, AT_RAW + 12 * KB), at("qsplit1", [2, GH, 2, ROPE], F32, AT_HT + 40 * KB)]
        qtmp = at("qtmp", [2, 2, GH, ROPE], F32, AT_W + 68 * KB)

        B = sems("mla", "head_in0", "head_in1", "slot2_in", "hw_hi", "hw_lo", "rw_hi", "rw_lo", "vw_hi", "vw_lo",
                 "rope_done", "rope_read", "qr", "qsplit_hi", "qsplit_lo", "rope_turned", "rope_copied",
                 "projected", "part_hi", "part_lo", "scores", "max", "neg_max", "exp", "inv", "probs",
                 "turned", "turned_hi", "turned_lo", "pv", "out_copied")

        def tensor_steps():
            steps = [("rope", 0), ("rope", 1), ("q", 0, 0), ("q", 0, 1), ("rope_turn", 0), ("rope", 2), ("k", 0, 0),
                     ("rope_turn", 1), ("rope", 3), ("k", 0, 1), ("rope_turn", 2), ("v", 0, 0), ("v", 0, 1), ("rope_turn", 3),
                     ("scores", 0, 0), ("scores", 0, 1), ("v", 0, 2), ("scores", 0, 2), ("scores", 0, 3), ("scores", 0, 4), ("v", 0, 3)]
            for j in range(GH - 1):
                n = j + 1
                steps += [("turn", j, 0), ("scores", j, 5), ("q", n, 0), ("turn", j, 1), ("pv", j, 0),
                          ("scores", j, 6), ("turn", j, 2), ("k", n, 0), ("turn", j, 3), ("scores", j, 7), ("pv", j, 1),
                          ("pv", j, 2), ("q", n, 1), ("pv", j, 3), ("scores", n, 0), ("turn", j, 4), ("turn", j, 5)]
                if j % 2 == 0:
                    steps += [("scores", n, 1), ("pv", j, 4), ("turn", j, 6), ("scores", n, 2), ("pv", j, 5),
                              ("turn", j, 7), ("scores", n, 3), ("pv", j, 6), ("turn", j, 8), ("pv", j, 7), ("turn", j, 9),
                              ("k", n, 1), ("pv", j, 8), ("turn", j, 10), ("pv", j, 9), ("turn", j, 11),
                              ("scores", n, 4), ("pv", j, 10), ("pv", j, 11)]
                else:
                    steps += [("k", n, 1), ("pv", j, 4), ("turn", j, 6), ("scores", n, 1), ("pv", j, 5),
                              ("turn", j, 7), ("v", n, 0), ("scores", n, 2), ("pv", j, 6), ("turn", j, 8), ("scores", n, 3), ("pv", j, 7),
                              ("turn", j, 9), ("v", n, 1), ("pv", j, 8), ("turn", j, 10), ("pv", j, 9),
                              ("turn", j, 11), ("v", n, 2), ("pv", j, 10), ("pv", j, 11), ("scores", n, 4), ("v", n, 3)]
            j = GH - 1
            steps += [("turn", j, 0), ("scores", j, 5), ("turn", j, 1), ("scores", j, 6), ("pv", j, 0),
                      ("turn", j, 2), ("scores", j, 7), ("pv", j, 1), ("turn", j, 3), ("pv", j, 2), ("pv", j, 3), ("turn", j, 4)]
            for m in range(5, 12):
                steps += [("turn", j, m), ("pv", j, m - 1)]
            return steps + [("pv", j, 11)]

        def other_steps():
            steps = [("rope", 0), ("rope_lo", 0), ("rope", 1), ("q", 0, 0), ("rope_lo", 1), ("q", 0, 1), ("rope_turn", 0),
                     ("rope", 2), ("rope_lo", 2), ("k", 0, 0), ("rope_turn", 1), ("value_weights", 0),
                     ("k", 0, 1), ("rope", 3), ("rope_lo", 3), ("rope_turn", 2), ("v", 0, 0), ("v", 0, 1), ("rope_turn", 3),
                     ("max", 0, 0), ("exp", 0, 0), ("max", 0, 1), ("exp", 0, 1), ("norm", 0, 0),
                     ("max", 0, 2), ("v", 0, 2), ("exp", 0, 2), ("norm", 0, 1), ("max", 0, 3), ("exp", 0, 3),
                     ("norm", 0, 2), ("norm", 0, 3), ("max", 0, 4), ("exp", 0, 4), ("v", 0, 3), ("weights", 1)]
            for j in range(GH):
                n = j + 1
                steps += [("turn", j, 0), ("max", j, 5), ("exp", j, 5), ("q", n, 0), ("norm", j, 4),
                          ("turn", j, 1), ("max", j, 6), ("exp", j, 6), ("norm", j, 5), ("turn", j, 2), ("k", n, 0),
                          ("max", j, 7), ("turn", j, 3), ("exp", j, 7), ("norm", j, 6), ("norm", j, 7), ("q", n, 1), ("out", j, 0),
                          ("max", n, 0), ("turn", j, 4), ("exp", n, 0), ("turn", j, 5)]
                if j % 2 == 0:
                    steps += [("max", n, 1), ("norm", n, 0), ("turn", j, 6), ("exp", n, 1), ("max", n, 2), ("turn", j, 7), ("norm", n, 1),
                              ("exp", n, 2), ("max", n, 3), ("turn", j, 8), ("exp", n, 3), ("turn", j, 9), ("norm", n, 2),
                              ("k", n, 1), ("turn", j, 10), ("weights", j + 2), ("norm", n, 3), ("turn", j, 11),
                              ("max", n, 4), ("exp", n, 4), ("out", j, 1), ("value_weights", j + 2)]
                else:
                    steps += [("k", n, 1), ("norm", n, 0), ("turn", j, 6), ("max", n, 1), ("exp", n, 1),
                              ("turn", j, 7), ("v", n, 0), ("norm", n, 1), ("max", n, 2), ("turn", j, 8), ("exp", n, 2),
                              ("max", n, 3), ("turn", j, 9), ("norm", n, 2), ("exp", n, 3),
                              ("v", n, 1), ("turn", j, 10), ("weights", j + 2), ("norm", n, 3), ("turn", j, 11), ("v", n, 2), ("out", j, 1),
                              ("max", n, 4), ("exp", n, 4), ("v", n, 3)]
            return [s for s in steps if s[0][:4] == "rope" or s[1] < GH]

        TENSOR_STEPS, OTHER_STEPS = tensor_steps(), other_steps()
        PROJ_ORDER = [s for s in TENSOR_STEPS if s[0] in "qkv"]
        NPROJ, FIRST_PROJ = len(PROJ_ORDER), 8
        TURNS = 12 * GH
        SCORES = TB * GH
        OUTS = 2 * GH

        def projections(step, j, i):
            return PROJ_ORDER.index((step, j, i)) + 1

        def proj_bank(n):
            return ps[:, 7 - n % 2, :] if n < FIRST_PROJ else ps[:, 7, :]

        def out_bank():
            return ps[:, 6, :]

        def key_block(m):
            half, kb = (0, m) if m < 4 else (1, m - 4)
            return half, kb, max(0, kb - 4 * half) * P

        def probs_of(i, keys):
            if i < 4:
                start = i * (i + 1) // 2 * P
                return probs_first[:, start + keys.start:start + keys.stop]
            start = (i * (i + 1) // 2 - 10) * P
            return probs_second[:, start + keys.start:start + keys.stop]

        def mla_loads(sp):
            sp.wait_ge(A.w_lo, 6)
            sp.dma_start(raw[:, 2, 0:ROPEW], w_rope[0]).then_inc(B.slot2_in, 16)
            sp.dma_start(raw[:, 0, 0:HEADW], w_heads[0]).then_inc(B.head_in0, 16)
            sp.dma_start(raw[:, 1, 0:HEADW], w_heads[1]).then_inc(B.head_in1, 16)
            for g in range(GROUPS):
                sp.wait_ge(B.rw_lo, g + 1)
                sp.dma_start(raw[:, 2, 0:PAIRW], w_values[2 * g]).then_inc(B.slot2_in, 16)
                for j in range(GH):
                    h = g * GH + j
                    if h + 2 < HEADS:
                        sp.wait_ge(B.hw_lo, h + 1)
                        sp.dma_start(raw[:, h % 2, 0:HEADW], w_heads[h + 2]).then_inc((B.head_in0, B.head_in1)[h % 2], 16)
                    if j == 0:
                        sp.wait_ge(B.vw_lo, 2 * g + 1)
                        sp.dma_start(raw[:, 2, 0:PAIRW], w_values[2 * g + 1]).then_inc(B.slot2_in, 16)
                    if j == 2 and g + 1 < GROUPS:
                        sp.wait_ge(B.vw_lo, 2 * g + 2)
                        sp.dma_start(raw[:, 2, 0:ROPEW], w_rope[g + 1]).then_inc(B.slot2_in, 16)

        def part_of(step, j, i):
            cut = slice(i * HALF, (i + 1) * HALF)
            if step == "q":
                return qn_h[j % 2][:, cut], qn_l[j % 2][:, cut]
            if step == "k":
                return kn_h[j % 2][:, cut], kn_l[j % 2][:, cut]
            return (v_h[:, 2 * i:2 * i + 2].rearrange("p a b c -> p (a b c)"),
                    v_l[i // 2][:, i % 2 * 2:i % 2 * 2 + 2].rearrange("p a b c -> p (a b c)"))

        def mla_scalar(act):
            def rope_hi(g, t):
                act.wait_ge(B.qr, 4 * g + t + 1)
                if t >= 2:
                    act.wait_ge(B.rope_turned, TB * g + 2 * t - 2)
                act.activation(qsplit[t % 2][:, :, :, 0, :].bitcast(F32R), qr[t % 2][:], ACT.Copy).then_inc(B.qsplit_hi, 1)

            def rope_copy(g, t):
                for n in (2 * t, 2 * t + 1):
                    act.wait_ge(B.rope_turned, TB * g + n + 1)
                    src = ps[:, 4 + n % 2, :].rearrange("p (h t) -> p h t", h=GH)
                    act.activation(qrot[:, :, n * P:(n + 1) * P], src, ACT.Copy).then_inc(B.rope_copied, 1)

            def weights(g, j):
                if j >= 2:
                    act.wait_ge(B.projected, NPROJ * g + projections("k", j - 2, 1))
                act.wait_ge((B.head_in0, B.head_in1)[j % 2], 32 * g + 16 * (j // 2 + 1))
                act.activation(hw_h[j % 2][:], raw[:, j % 2, 0:HEADW], ACT.Copy).then_inc(B.hw_hi, 1)

            def value_weights(g, j):
                if j > 0:
                    act.wait_ge(B.projected, NPROJ * g + projections("v", j - 2, 3))
                act.wait_ge(B.slot2_in, 48 * g + 16 * (j // 2 + 2))
                act.activation(vw_h[:], raw[:, 2, 0:PAIRW], ACT.Copy).then_inc(B.vw_hi, 1)

            def project(g, step, j, i):
                n = projections(step, j, i)
                act.wait_ge(B.projected, NPROJ * g + n)
                if step == "v" and j > 0:
                    act.wait_ge(B.pv, TURNS * g + 12 * (j - 1) + 4 + 2 * i + 2)
                act.activation(part_of(step, j, i)[0], proj_bank(n - 1), ACT.Copy).then_inc(B.part_hi, 1)

            def exponentiate(g, j, i):
                act.wait_ge(B.neg_max, SCORES * g + TB * j + i + 1)
                if j > 0:
                    act.wait_ge(B.turned, TURNS * g + 12 * (j - 1) + (i + 1 if i < 4 else 4 + i + 1))
                col = slice(i, i + 1)
                nk = (i + 1) * P
                act.activation(probs_of(i, slice(0, nk)), psf[:, i % 2 * D:i % 2 * D + nk], ACT.Exp, bias=neg_max[:, col],
                               scale=SCALE, accum_out=row_sum[:, col]).then_inc(B.exp, 1)

            def turned_hi(g, j, m):
                q0, n = key_block(m)[2], 12 * j + m
                act.wait_ge(B.turned, TURNS * g + n + 1)
                if n >= 2:
                    act.wait_ge(B.pv, TURNS * g + n - 1)
                act.activation(pt_h[:, n % 2, q0:HALF], ps[:, 4 + n % 2, q0:HALF], ACT.Copy).then_inc(B.turned_hi, 1)

            act.wait_ge(A.product, TB)
            with act.Fori(0, GROUPS) as g:
                act.wait_ge(B.slot2_in, 48 * g + 16)
                act.activation(flat(rw_h), raw[:, 2, 0:ROPEW], ACT.Copy).then_inc(B.rw_hi, 1)
                weights(g, 0)
                for step in OTHER_STEPS:
                    kind, of = step[0], step[1:]
                    if kind == "rope":
                        rope_hi(g, *of)
                    elif kind == "rope_turn":
                        rope_copy(g, *of)
                    elif kind == "weights":
                        weights(g, *of)
                    elif kind == "value_weights":
                        value_weights(g, *of)
                    elif kind in "qkv":
                        project(g, *step)
                    elif kind == "exp":
                        exponentiate(g, *of)
                    elif kind == "turn":
                        turned_hi(g, *of)

        def mla_vector(dve):
            def rotate(g, t):
                dve.wait_ge(B.rope_done, 4 * g + t + 1)
                src = ps[:, 2 * (t % 2), :].rearrange("p (b h r) -> p b h r", b=2, h=GH)
                cos = cosine[:, 2 * t:2 * t + 2, :].unsqueeze(2).broadcast_to([P, 2, GH, RH])
                sin = sine[:, 2 * t:2 * t + 2, :].unsqueeze(2).broadcast_to([P, 2, GH, RH])
                q1, q2 = src[:, :, :, 0:RH], src[:, :, :, RH:ROPE]
                if t > 0:
                    dve.wait_ge(B.qr, 4 * g + t)
                dve.tensor_tensor(qtmp[:, 0, :, :, 0:RH], q1, cos, ALU.mult)
                dve.tensor_tensor(qtmp[:, 0, :, :, RH:ROPE], q2, cos, ALU.mult)
                dve.tensor_tensor(qtmp[:, 1, :, :, 0:RH], q2, sin, ALU.mult)
                dve.tensor_tensor(qtmp[:, 1, :, :, RH:ROPE], q1, sin, ALU.mult).then_inc(B.rope_read, 1)
                dve.wait_ge(B.rope_read, 4 * g + t + 1)
                if t >= 2:
                    dve.wait_ge(B.qsplit_hi, 4 * g + t - 1)
                dve.tensor_tensor(qr[t % 2][:, :, :, 0:RH], qtmp[:, 0, :, :, 0:RH], qtmp[:, 1, :, :, 0:RH], ALU.subtract)
                dve.tensor_tensor(qr[t % 2][:, :, :, RH:ROPE], qtmp[:, 0, :, :, RH:ROPE], qtmp[:, 1, :, :, RH:ROPE],
                                  ALU.add).then_inc(B.qr, 1)

            def rope_lo(g, t):
                dve.wait_ge(B.qsplit_hi, 4 * g + t + 1)
                dve.tensor_tensor(qsplit[t % 2][:, :, :, 1, :], qr[t % 2][:], qsplit[t % 2][:, :, :, 0, :],
                                  ALU.subtract).then_inc(B.qsplit_lo, 1)

            def weights(g, j):
                dve.wait_ge(B.hw_hi, GH * g + j + 1)
                dve.tensor_tensor(hw_l[j % 2][:], raw[:, j % 2, 0:HEADW], f32(hw_h[j % 2][:]), ALU.subtract).then_inc(B.hw_lo, 1)

            def value_weights(g, j):
                dve.wait_ge(B.vw_hi, 2 * g + j // 2 + 1)
                dve.tensor_tensor(vw_l[:], raw[:, 2, 0:PAIRW], f32(vw_h[:]), ALU.subtract).then_inc(B.vw_lo, 1)

            def project(g, step, j, i):
                n = projections(step, j, i)
                hi, lo = part_of(step, j, i)
                dve.wait_ge(B.part_hi, NPROJ * g + n)
                dve.tensor_tensor(lo, proj_bank(n - 1), f32(hi), ALU.subtract).then_inc(B.part_lo, 1)

            def maximum(g, j, i):
                n = TB * j + i
                col = slice(i, i + 1)
                dve.wait_ge(B.scores, SCORES * g + n + 1)
                dve.tensor_reduce(row_max[:, col], psf[:, i % 2 * D:i % 2 * D + (i + 1) * P], AX.X, ALU.max).then_inc(B.max, 1)
                dve.wait_ge(B.max, SCORES * g + n + 1)
                dve.tensor_scalar(neg_max[:, col], row_max[:, col], -SCALE, None, ALU.mult).then_inc(B.neg_max, 1)

            def normalise(g, j, i):
                n = TB * j + i
                col = slice(i, i + 1)
                row = probs_of(i, slice(0, (i + 1) * P))
                dve.wait_ge(B.exp, SCORES * g + n + 1)
                dve.reciprocal(row_inv[:, col], row_sum[:, col]).then_inc(B.inv, 1)
                dve.wait_ge(B.inv, SCORES * g + n + 1)
                dve.tensor_scalar(row, row, row_inv[:, col], None, ALU.mult).then_inc(B.probs, 1)

            def turned_lo(g, j, m):
                q0, n = key_block(m)[2], 12 * j + m
                dve.wait_ge(B.turned_hi, TURNS * g + n + 1)
                dve.tensor_tensor(pt_l[:, n % 2, q0:HALF], ps[:, 4 + n % 2, q0:HALF], f32(pt_h[:, n % 2, q0:HALF]),
                                  ALU.subtract).then_inc(B.turned_lo, 1)

            def copy_out(g, j, half):
                dve.wait_ge(B.pv, TURNS * g + 12 * j + (4, 12)[half])
                dve.tensor_copy(aT[:, bass.ds(g * (GH * SEQ) + j * SEQ + half * HALF, HALF)], out_bank()).then_inc(B.out_copied, 1)

            with dve.Fori(0, GROUPS) as g:
                dve.wait_ge(B.rw_hi, g + 1)
                dve.tensor_tensor(flat(rw_l), raw[:, 2, 0:ROPEW], f32(flat(rw_h)), ALU.subtract).then_inc(B.rw_lo, 1)
                weights(g, 0)
                for step in OTHER_STEPS:
                    kind, of = step[0], step[1:]
                    if kind == "rope":
                        rotate(g, *of)
                    elif kind == "rope_lo":
                        rope_lo(g, *of)
                    elif kind == "weights":
                        weights(g, *of)
                    elif kind == "value_weights":
                        value_weights(g, *of)
                    elif kind in "qkv":
                        project(g, *step)
                    elif kind == "max":
                        maximum(g, *of)
                    elif kind == "norm":
                        normalise(g, *of)
                    elif kind == "turn":
                        turned_lo(g, *of)
                    elif kind == "out":
                        copy_out(g, *of)

        def mla_tensor(pe):
            def rope_product(g, t):
                if t >= 2:
                    pe.wait_ge(B.rope_read, 4 * g + t - 1)
                pe.wait_ge(A.lo, TB + 2 * t + 2)
                for b in range(2):
                    blk = slice((2 * t + b) * P, (2 * t + b + 1) * P)
                    for k in range(QK):
                        mm = three_passes(pe, ps[:, 2 * (t % 2), b * 256:(b + 1) * 256], cq_h[:, k, blk], cq_l[:, k, blk],
                                          rw_h[:, k, :], rw_l[:, k, :], k == 0, k == QK - 1)
                mm.then_inc(B.rope_done, 1)

            def rope_turn(g, t):
                pe.wait_ge(B.qsplit_lo, 4 * g + t + 1)
                for b in range(2):
                    n = 2 * t + b
                    if n >= 2:
                        pe.wait_ge(B.rope_copied, TB * g + n - 1)
                    for h in range(GH):
                        mm = pe.transpose(ps[:, 4 + n % 2, h * P:(h + 1) * P], qsplit[t % 2][:, b, h].rearrange("p a b -> p (a b)"), ident[:])
                    mm.then_inc(B.rope_turned, 1)

            def project(g, step, j, i):
                n = projections(step, j, i)
                dst = proj_bank(n - 1)
                if n > 2:
                    pe.wait_ge(B.part_lo, NPROJ * g + (n - 2 if n <= FIRST_PROJ + 1 else n - 1))
                if step == "q" and i == 0:
                    pe.wait_ge(B.hw_lo, GH * g + j + 1)
                if step == "q" and j == 0:
                    pe.wait_ge(A.lo, TB + TB // 2 * (i + 1))
                hh, hl = hw_h[j % 2], hw_l[j % 2]
                cut = slice(i * HALF, (i + 1) * HALF)
                if step == "q":
                    for k in range(QK):
                        w = slice(k * P, (k + 1) * P)
                        mm = three_passes(pe, dst, hh[:, w], hl[:, w], cq_h[:, k, cut], cq_l[:, k, cut], k == 0, k == QK - 1)
                elif step == "k":
                    for k in range(KK):
                        w = slice((QK + k) * P, (QK + k + 1) * P)
                        mm = three_passes(pe, dst, hh[:, w], hl[:, w], ckv_h[:, k, cut], ckv_l[:, k, cut], k == 0, k == KK - 1)
                else:
                    pe.wait_ge(B.vw_lo, 2 * g + j // 2 + 1)
                    for t in range(2):
                        blk = slice((2 * i + t) * P, (2 * i + t + 1) * P)
                        for k in range(KK):
                            w = slice(k * 2 * VDIM, (k + 1) * 2 * VDIM)
                            mm = three_passes(pe, dst[:, t * 2 * VDIM:(t + 1) * 2 * VDIM], ckv_h[:, k, blk], ckv_l[:, k, blk],
                                              vw_h[:, w], vw_l[:, w], k == 0, k == KK - 1)
                mm.then_inc(B.projected, 1)

            def scores(g, j, i):
                qh, ql, kh, kl = qn_h[j % 2], qn_l[j % 2], kn_h[j % 2], kn_l[j % 2]
                n = TB * j + i
                blk = slice(i * P, (i + 1) * P)
                if i % 4 == 0:
                    pe.wait_ge(B.part_lo, NPROJ * g + max(projections(which, j, i // 4) for which in "qk"))
                if n >= 2:
                    pe.wait_ge(B.exp, SCORES * g + n - 1)
                if j == 0:
                    pe.wait_ge(B.rope_copied, TB * g + i + 1)
                for c in range(i // 4 + 1):
                    width = min(HALF, (i + 1) * P - c * HALF)
                    dst = ps[:, i % 2 * 2 + c, 0:width]
                    keys = slice(c * HALF, c * HALF + width)
                    three_passes(pe, dst, qh[:, blk], ql[:, blk], kh[:, keys], kl[:, keys], True, False)
                    pe.matmul(dst, qrot[:, j, blk], krot_h[:, keys], start=False, stop=False)
                    pe.matmul(dst, qrot[:, j, blk], krot_l[:, keys], start=False, stop=c < i // 4)
                mm = pe.matmul(ps[:, i % 2 * 2 + c, width - P:width], identr[:], maskr[:], start=False, stop=True)
                mm.then_inc(B.scores, 1)

            def turn(g, j, m):
                half, kb, q0 = key_block(m)
                n = 12 * j + m
                if m in (0, 4):
                    pe.wait_ge(B.probs, SCORES * g + TB * j + 4 * half + 4)
                if n >= 2:
                    pe.wait_ge(B.turned_lo, TURNS * g + n - 1)
                else:
                    pe.wait_ge(B.rope_copied, TB * g + TB)
                for q in range(q0 // P, 4):
                    mm = pe.transpose(ps[:, 4 + n % 2, q * P:(q + 1) * P], probs_of(4 * half + q, slice(kb * P, (kb + 1) * P)), ident[:])
                mm.then_inc(B.turned, 1)

            def pv(g, j, m):
                half, kb, q0 = key_block(m)
                n = 12 * j + m
                if kb == 0 and 2 * j + half > 0:
                    pe.wait_ge(B.out_copied, OUTS * g + 2 * j + half)
                if n == 0:
                    pe.wait_ge(B.part_lo, NPROJ * g + FIRST_PROJ)
                elif j % 2 == 0 and m in (0, 2, 8, 10):
                    pe.wait_ge(B.part_lo, NPROJ * g + projections("v", j, kb // 2))
                pe.wait_ge(B.turned_lo, TURNS * g + n + 1)
                mm = three_passes(pe, out_bank()[:, q0:HALF], v_h[:, kb, j % 2, :], v_l[kb // 4][:, kb % 4, j % 2, :], pt_h[:, n % 2, q0:HALF],
                                  pt_l[:, n % 2, q0:HALF], kb == 0, m in (3, 11))
                mm.then_inc(B.pv, 1)

            pe.wait_ge(A.k_lo, 2)
            with pe.Fori(0, GROUPS) as g:
                pe.wait_ge(B.rw_lo, g + 1)
                for step in TENSOR_STEPS:
                    kind, of = step[0], step[1:]
                    if kind == "rope":
                        rope_product(g, *of)
                    elif kind == "rope_turn":
                        rope_turn(g, *of)
                    elif kind in "qkv":
                        project(g, *step)
                    elif kind == "scores":
                        scores(g, *of)
                    elif kind == "turn":
                        turn(g, *of)
                    elif kind == "pv":
                        pv(g, *of)
                pe.wait_ge(B.out_copied, OUTS * g + OUTS)

        rec_h = at("rec_h", [KT, P], F32R, AT_W + 72 * KB)
        rec_l = at("rec_l", [KT, P], F32R, AT_W + 76 * KB)
        gw_h = at("gw_h", [KT, P], F32R, AT_W + 64 * KB)
        gw_l = at("gw_l", [KT, P], F32R, AT_W + 68 * KB)
        ax_h = at("ax_h", [2, P], F32R, AT_W + 24 * KB)
        ax_l = at("ax_l", [2, P], F32R, AT_W + 25 * KB)
        xc_h = at("xc_h", [SEQ], F32R, AT_W + 26 * KB)
        xc_l = at("xc_l", [SEQ], F32R, AT_W + 30 * KB)
        PAD = CONV - 1
        rec = at("rec", [SEQ + 8], F32, AT_W + 34 * KB)
        xc = at("xc", [SEQ], F32, AT_W + 39 * KB)
        igate = at("igate", [SEQ], F32, AT_W + 43 * KB)
        tanh = at("tanh", [SEQ], F32, AT_W + 47 * KB)
        root = at("root", [SEQ], F32, AT_W + 51 * KB)
        winv = at("winv", [SEQ], F32, AT_W + 55 * KB)
        wtmp = at("wtmp", [SEQ], F32, AT_W + 59 * KB)
        rgate = at("rgate", [SEQ], F32, AT_W + 80 * KB)
        bgate = at("bgate", [SEQ], F32, AT_W + 84 * KB)
        agate = at("agate", [SEQ], F32, AT_RAW + 12 * KB)
        vec = at("vec", [CH, VEC], F32, 6304)
        tilev = at("tilev", [VEC], F32, 6624)
        dtmp = at("dtmp", [5, CH], F32, 6688)
        V_CONV_B, V_B_A, V_B_X, V_LAM, V_DECAY, V_DECAY2 = range(CONV, VEC)
        L = sems("lru", "vec_in", "raw_in0", "raw_in1", "raw_in2", "w_hi", "first_lo", "w_lo", "setup", "tile_vec", "rec_done", "gate_done",
                 "ax_done", "rec_copied", "gated", "conv", "xc_hi", "xc_lo", "sigmoid", "tanh", "estimate", "root", "inv", "decay", "u",
                 "ix", "b", "scan", "out")

        def lru_loads_first(sp, kinds):
            if "rec" in kinds:
                sp.dma_start(raw[:, 0, :], w_rec[0]).then_inc(L.raw_in0, 16)
            if "gate" in kinds:
                sp.dma_start(raw[:, 1, :], w_gate[0]).then_inc(L.raw_in1, 16)
            if "ax" in kinds:
                sp.dma_start(raw[:, 2, 0:2 * P], w_ax[0]).then_inc(L.raw_in2, 16)

        def lru_sync(sp):
            def next_tile(n, row):
                for slot, (src, width, arrived) in enumerate(((w_rec, D, L.raw_in0), (w_gate, D, L.raw_in1), (w_ax, 2 * P, L.raw_in2))):
                    sp.wait_ge(*lru_split(n, slot))
                    sp.dma_start(raw[:, slot, 0:width], src[row]).then_inc(arrived, 16)

            next_tile(0, 1)
            with sp.Fori(1, CH - 1) as n:
                next_tile(n, sp.snap(n + 1))

        def lru_split(n, slot):
            return (L.first_lo, slot + 1) if isinstance(n, int) and n == 0 else (L.w_lo, 3 * n + slot - 2)

        LRU_WEIGHTS = {"rec": (0, rec_h, rec_l), "gate": (1, gw_h, gw_l), "ax": (2, ax_h, ax_l)}

        def lru_split_hi(act, n, which):
            slot, hi, lo = LRU_WEIGHTS[which]
            act.wait_ge((L.raw_in0, L.raw_in1, L.raw_in2)[slot], 16 * n + 16)
            act.activation(flat(hi), raw[:, slot, 0:flat(hi).shape[1]], ACT.Copy).then_inc(L.w_hi, 1)

        def lru_split_lo(engine, n, which):
            slot, hi, lo = LRU_WEIGHTS[which]
            engine.wait_ge(L.w_hi, 3 * n + slot + 1)
            engine.tensor_tensor(flat(lo), raw[:, slot, 0:flat(hi).shape[1]], f32(flat(hi)),
                                 ALU.subtract).then_inc(lru_split(n, slot)[0], 1)

        BANKS_REC, BANKS_GATE, BANKS_R, BANKS_I = 4, 6, 0, 2

        def pair(b):
            return psf[:, b * HALF:b * HALF + D]

        def at_tile(n):
            return aT[:, n * SEQ:(n + 1) * SEQ] if isinstance(n, int) else aT[:, bass.ds(n * SEQ, SEQ)]

        def tile_vec(k):
            return tilev[:, k:k + 1]

        def lru_scalar(act):
            act.wait_ge(L.vec_in, 16)
            act.activation(dtmp[:, 0, :], vec[:, :, V_LAM], ACT.Abs).then_inc(L.setup, 1)
            act.wait_ge(L.setup, 1)
            act.activation(dtmp[:, 1, :], dtmp[:, 0, :], ACT.Exp, scale=-1.0).then_inc(L.setup, 1)
            lru_split_hi(act, 0, "ax")

            def tile(n, last):
                act.wait_ge(L.rec_done, n + 1)
                act.activation(rec[:, PAD:PAD + SEQ], pair(BANKS_REC), ACT.Copy).then_inc(L.rec_copied, 1)
                if not last:
                    lru_split_hi(act, n + 1, "rec")
                act.wait_ge(L.conv, CONV * n + CONV)
                act.activation(xc_h[:], xc[:], ACT.Copy).then_inc(L.xc_hi, 1)
                if last:
                    proj_w_hi(act, 3, 0, 1, 2)
                act.wait_ge(L.gate_done, n + 1)
                act.activation(at_tile(n), pair(BANKS_GATE), ACT.Gelu_apprx_tanh).then_inc(L.gated, 1)
                if not last:
                    lru_split_hi(act, n + 1, "gate")
                else:
                    act.wait_ge(L.out, CH - 1)
                    proj_a_hi(act, 3, 0, *range(4))
                act.wait_ge(L.ax_done, n + 1)
                act.wait_ge(L.out, n + 1)
                act.activation(rgate[:], pair(BANKS_R), ACT.Sigmoid, bias=tile_vec(V_B_A)).then_inc(L.sigmoid, 1)
                act.activation(igate[:], pair(BANKS_I), ACT.Sigmoid, bias=tile_vec(V_B_X)).then_inc(L.sigmoid, 1)
                act.wait_ge(L.sigmoid, 2 * n + 1)
                act.activation(tanh[:], rgate[:], ACT.Tanh, scale=tile_vec(V_DECAY)).then_inc(L.tanh, 1)
                act.activation(winv[:], rgate[:], ACT.Exp, scale=tile_vec(V_DECAY2)).then_inc(L.estimate, 1)
                act.wait_ge(L.tanh, n + 1)
                act.activation(root[:], tanh[:], ACT.Sqrt, scale=4.0).then_inc(L.root, 1)
                if not last:
                    lru_split_hi(act, n + 1, "ax")

            with act.Fori(0, CH - 1) as n:
                tile(n, False)
            tile(CH - 1, True)

        def lru_setup_vector(dve):
            chain = 2

            def after(ins):
                nonlocal chain
                ins.then_inc(L.setup, 1)
                chain += 1
                dve.wait_ge(L.setup, chain)

            e, s, s2, p = dtmp[:, 1, :], dtmp[:, 2, :], dtmp[:, 3, :], dtmp[:, 4, :]
            dve.wait_ge(L.setup, 2)
            after(dve.tensor_scalar(p, e, 2.0, None, ALU.add))
            after(dve.reciprocal(s, p))
            after(dve.tensor_tensor(s, s, e, ALU.mult))
            after(dve.tensor_tensor(s2, s, s, ALU.mult))
            after(dve.tensor_scalar(p, s2, 1.0 / 17, None, ALU.mult))
            for k in range(15, 1, -2):
                after(dve.scalar_tensor_tensor(out=p, in0=p, scalar=1.0 / k, in1=s2, op0=ALU.add, op1=ALU.mult))
            after(dve.scalar_tensor_tensor(out=p, in0=p, scalar=1.0, in1=s, op0=ALU.add, op1=ALU.mult))
            after(dve.tensor_scalar(s, vec[:, :, V_LAM], -1.0, 0.0, ALU.mult, ALU.max))
            after(dve.scalar_tensor_tensor(out=p, in0=p, scalar=2.0, in1=s, op0=ALU.mult, op1=ALU.add))
            after(dve.tensor_scalar(vec[:, :, V_DECAY], p, LRU_C / 2, None, ALU.mult))
            after(dve.tensor_scalar(vec[:, :, V_DECAY2], p, -LRU_C, None, ALU.mult))

        vec_flat = vec[:].rearrange("p a b -> p (a b)")

        def lru_vector(dve):
            lru_setup_vector(dve)
            lru_split_lo(dve, 0, "ax")
            dve.wait_ge(L.out, 1)

            def convolve(n):
                cols = slice(n * VEC, (n + 1) * VEC) if isinstance(n, int) else bass.ds(n * VEC, VEC)
                dve.tensor_copy(tilev[:], vec_flat[:, cols]).then_inc(L.tile_vec, 1)
                dve.wait_ge(L.tile_vec, n + 1)
                dve.wait_ge(L.rec_copied, n + 1)
                dve.tensor_scalar(xc[:], rec[:, PAD:PAD + SEQ], tile_vec(CONV - 1), tile_vec(V_CONV_B), ALU.mult, ALU.add).then_inc(L.conv, 1)
                for k in range(CONV - 1):
                    dve.wait_ge(L.conv, CONV * n + k + 1)
                    dve.scalar_tensor_tensor(out=xc[:], in0=rec[:, k:k + SEQ], scalar=tile_vec(k), in1=xc[:], op0=ALU.mult,
                                             op1=ALU.add).then_inc(L.conv, 1)

            def convolved_lo(n):
                dve.wait_ge(L.xc_hi, n + 1)
                dve.tensor_tensor(xc_l[:], xc[:], f32(xc_h[:]), ALU.subtract).then_inc(L.xc_lo, 1)

            def recur(n, last):
                dve.wait_ge(L.estimate, n + 1)
                dve.tensor_scalar(winv[:], winv[:], 0.5, 0.5, ALU.mult, ALU.add).then_inc(L.inv, 1)
                dve.wait_ge(L.inv, 3 * n + 1)
                dve.wait_ge(L.tanh, n + 1)
                dve.scalar_tensor_tensor(out=wtmp[:], in0=tanh[:], scalar=1.0, in1=winv[:], op0=ALU.add, op1=ALU.mult).then_inc(L.inv, 1)
                dve.wait_ge(L.inv, 3 * n + 2)
                dve.scalar_tensor_tensor(out=winv[:], in0=wtmp[:], scalar=2.0, in1=winv[:], op0=ALU.subtract, op1=ALU.mult).then_inc(L.inv, 1)
                dve.wait_ge(L.inv, 3 * n + 3)
                dve.wait_ge(L.root, n + 1)
                dve.scalar_tensor_tensor(out=bgate[:], in0=root[:], scalar=-1.0, in1=winv[:], op0=ALU.mult, op1=ALU.mult).then_inc(L.u, 1)
                if not last:
                    dve.wait_ge(L.ix, n + 1)
                    convolve(n + 1)
                dve.tensor_tensor(agate[:], tanh[:], winv[:], ALU.mult).then_inc(L.decay, 1)
                if not last:
                    convolved_lo(n + 1)
                dve.wait_ge(L.decay, 2 * n + 1)
                dve.tensor_scalar(agate[:], agate[:], 2.0, 1.0, ALU.mult, ALU.add).then_inc(L.decay, 1)
                if last:
                    proj_w_lo(dve, 3, 3)
                dve.wait_ge(L.decay, 2 * n + 2)
                dve.wait_ge(L.b, n + 1)
                dve.tensor_tensor_scan(rgate[:], agate[:], bgate[:], 0.0, ALU.mult, ALU.add).then_inc(L.scan, 1)
                dve.wait_ge(L.scan, n + 1)
                dve.wait_ge(L.gated, n + 1)
                dve.tensor_tensor(at_tile(n), at_tile(n), rgate[:], ALU.mult).then_inc(L.out, 1)

            convolve(0)
            convolved_lo(0)
            with dve.Fori(0, CH - 1) as n:
                recur(n, False)
            for k in range(3):
                proj_w_lo(dve, 3, k)
                proj_a_lo(dve, 3, 0, k)
            proj_a_lo(dve, 3, 0, 3)
            recur(CH - 1, True)

        def lru_gpsimd(pool):
            pool.wait_ge(MLP[2].down_done, TB * MLP_GROUPS)
            pool.memset(rec[:, 0:PAD], 0.0).then_inc(L.out, 1)

            def tile(n, last):
                if not last:
                    lru_split_lo(pool, n + 1, "rec")
                    lru_split_lo(pool, n + 1, "gate")
                pool.wait_ge(L.sigmoid, 2 * n + 2)
                pool.tensor_tensor(igate[:], igate[:], xc[:], ALU.mult).then_inc(L.ix, 1)
                pool.wait_ge(L.u, n + 1)
                pool.wait_ge(L.ix, n + 1)
                pool.tensor_tensor(bgate[:], bgate[:], igate[:], ALU.mult).then_inc(L.b, 1)
                if not last:
                    lru_split_lo(pool, n + 1, "ax")

            with pool.Fori(0, CH - 1) as n:
                tile(n, False)
            tile(CH - 1, True)

        def lru_project(pe, n, which, halves):
            slot, wh, wl = LRU_WEIGHTS[which]
            banks, done = ((BANKS_REC, L.rec_done), (BANKS_GATE, L.gate_done))[slot]
            pe.wait_ge(*lru_split(n, slot))
            for half in halves:
                cut = slice(half * HALF, (half + 1) * HALF)
                for k in range(KT):
                    mm = three_passes(pe, ps[:, banks + half, :], wh[:, k, :], wl[:, k, :], hth[:, k, cut], htl[:, k, cut],
                                      k == 0, k == KT - 1)
            if 1 in halves:
                mm.then_inc(done, 1)

        def lru_first(pe, which):
            pe.wait_ge(E.ht_lo, pre(2, TB // 2 + (1 if which == "rec" else 2)))
            lru_project(pe, 0, which, (0,))

        def lru_tensor(pe):
            def gates(n):
                pe.wait_ge(*lru_split(n, 2))
                pe.wait_ge(L.xc_lo, n + 1)
                for g, banks in ((0, BANKS_R), (1, BANKS_I)):
                    for half in range(2):
                        cut = slice(half * HALF, (half + 1) * HALF)
                        mm = three_passes(pe, ps[:, banks + half, :], ax_h[:, g, :], ax_l[:, g, :], xc_h[:, cut], xc_l[:, cut], True, True)
                mm.then_inc(L.ax_done, 1)

            pe.wait_ge(E.ht_lo, pre(2, TB))
            lru_project(pe, 0, "rec", (1,))
            lru_project(pe, 0, "gate", (1,))
            gates(0)
            with pe.Fori(1, CH) as n:
                lru_project(pe, n, "rec", (0, 1))
                lru_project(pe, n, "gate", (0, 1))
                gates(n)

        C = sems("const", "zeroed", "ident", "mask", "power", "rounded")
        block = ctx.enter_context(nc.Block())

        @block.sync
        def _(sp):
            end_loads(sp, 0)
            mla_in_loads(sp, range(4, 6))
            sp.dma_start(vec[:, :, 0:VEC_IN], lru_vec).then_inc(L.vec_in, 16)
            mla_loads(sp)
            proj_loads(sp, 1, w_o, [(B.hw_lo, HEADS - 1), (B.hw_lo, HEADS), (B.vw_lo, HEADS // 2), (B.pv, TURNS * GROUPS)])
            sp.wait_ge(PROJ[1].w_lo, KT)
            end_loads(sp, 1)
            end_x_loads(sp, 1)
            mlp_loads_first(sp, 2, 0, ("up",))
            end_sync(sp, 1)
            mlp_loads_first(sp, 2, 0, ("down",))
            mlp_sync(sp, 2, 0)
            sp.wait_ge(MLP[2].w_lo, 8 * MLP_GROUPS)
            end_loads(sp, 2)
            lru_loads_first(sp, ("rec", "gate"))
            sp.wait_ge(MLP[2].u_lo, 8 * MLP_GROUPS)
            end_x_loads(sp, 2)
            end_sync(sp, 2)
            lru_loads_first(sp, ("ax",))
            lru_sync(sp)
            proj_loads(sp, 3, w_out, [lru_split(CH - 1, slot) for slot in range(3)])
            sp.wait_ge(PROJ[3].w_lo, KT)
            end_loads(sp, 3)
            end_x_loads(sp, 3)
            mlp_loads_first(sp, 4, 1, ("up",))
            end_sync(sp, 3)
            mlp_loads_first(sp, 4, 1, ("down",))
            mlp_sync(sp, 4, 1)
            sp.wait_ge(MLP[4].w_lo, 8 * MLP_GROUPS)
            end_loads(sp, 4)
            sp.wait_ge(MLP[4].u_lo, 8 * MLP_GROUPS)
            end_x_loads(sp, 4)
            end_sync(sp, 4)

        @block.scalar
        def _(act):
            mla_in_scalar(act)
            act.wait_ge(C.mask, 1)
            act.activation(identr[:], ident[:], ACT.Copy).then_inc(C.rounded, 1)
            act.activation(maskr[:], mask[:], ACT.Copy).then_inc(C.rounded, 1)
            mla_scalar(act)
            proj1_scalar(act)
            for step in range(STEPS):
                end_scalar(act, 1, step, PROJ[1].y_done)
                if step in EARLY:
                    split_hi(act, MLP[2], mlp_first_up(2, EARLY.index(step)))
            mlp_scalar(act, 2)
            for step in range(STEPS):
                end_scalar(act, 2, step, None)
                if step in EARLY:
                    lru_split_hi(act, 0, ("rec", "gate")[EARLY.index(step)])
            lru_scalar(act)
            proj3_scalar(act)
            for step in range(STEPS):
                end_scalar(act, 3, step, PROJ[3].y_done)
                if step in EARLY:
                    split_hi(act, MLP[4], mlp_first_up(4, EARLY.index(step)))
            mlp_scalar(act, 4)
            for step in range(STEPS):
                end_scalar(act, 4, step, None)

        @block.vector
        def _(dve):
            mla_in_vector(dve)
            mla_vector(dve)
            proj1_vector(dve)
            for step in range(STEPS):
                end_vector(dve, 1, step)
                if step in EARLY:
                    split_lo(dve, MLP[2], mlp_first_up(2, EARLY.index(step)), EARLY.index(step) + 1)
            mlp_vector(dve, 2, lambda i: lru_split_lo(dve, 0, ("rec", "gate")[i]))
            lru_vector(dve)
            proj3_vector(dve)
            for step in range(STEPS):
                end_vector(dve, 3, step)
                if step in EARLY:
                    split_lo(dve, MLP[4], mlp_first_up(4, EARLY.index(step)), EARLY.index(step) + 1)
            mlp_vector(dve, 4, lambda i: None)

        @block.gpsimd
        def _(pool):
            pool.memset(ident[:], 0.0).then_inc(C.zeroed, 1)
            pool.memset(mask[:], 0.0).then_inc(C.zeroed, 1)
            pool.memset(power[:], -0.5).then_inc(C.power, 1)
            pool.wait_ge(C.zeroed, 2)
            pool.affine_select(out=ident[:], in_=ident[:], compare_op=ALU.not_equal, fill=1.0, base=0, pattern=[[-1, P]],
                               channel_multiplier=1).then_inc(C.ident, 1)
            pool.affine_select(out=mask[:], in_=mask[:], compare_op=ALU.is_ge, fill=MASKED, base=0, pattern=[[-1, P]],
                               channel_multiplier=1).then_inc(C.mask, 1)
            pool.wait_ge(C.power, 1)
            mla_in_gpsimd(pool)
            for step in range(STEPS):
                end_gpsimd(pool, 1, step)
            mlp_gpsimd(pool, 2)
            for step in range(STEPS):
                end_gpsimd(pool, 2, step)
            lru_gpsimd(pool)
            for step in range(STEPS):
                end_gpsimd(pool, 3, step)
            mlp_gpsimd(pool, 4)
            for step in range(STEPS):
                end_gpsimd(pool, 4, step)

        @block.tensor
        def _(pe):
            pe.wait_ge(C.ident, 1)
            mla_in_tensor(pe)
            pe.wait_ge(C.rounded, 2)
            mla_tensor(pe)
            proj_tensor(pe, 1, [lambda: mlp_up(pe, 2, 0, 0), lambda: mlp_up(pe, 2, 0, 1)])
            mlp_tensor(pe, 2, [lambda: lru_first(pe, "rec"), lambda: lru_first(pe, "gate")])
            lru_tensor(pe)
            proj_tensor(pe, 3, [lambda: mlp_up(pe, 4, 0, 0), lambda: mlp_up(pe, 4, 0, 1)])
            mlp_tensor(pe, 4, [])


def packed(inputs):
    f = lambda name: np.asarray(inputs[name])

    def by_partition(w):
        return w.reshape(-1, P, w.shape[1]).transpose(1, 0, 2).reshape(P, -1)

    w_in = f("mla_w_in")[0]
    uq = f("mla_w_uq")[0].reshape(QK, P, HEADS, NOPE + ROPE)
    ukv = f("mla_w_ukv")[0].reshape(KK, P, HEADS, NOPE + VDIM)
    heads = np.concatenate([
        uq[..., :NOPE].transpose(2, 1, 0, 3).reshape(HEADS, P, QK * NOPE),
        ukv[..., :NOPE].transpose(2, 1, 0, 3).reshape(HEADS, P, KK * NOPE)], axis=2)
    values = ukv[..., NOPE:].reshape(KK, P, HEADS // 2, 2 * VDIM).transpose(2, 1, 0, 3).reshape(HEADS // 2, P, PAIRW)
    rope = uq[..., NOPE:].reshape(QK, P, GROUPS, GH, ROPE).transpose(2, 1, 0, 3, 4).reshape(GROUPS, P, ROPEW)
    lru_in = f("lru_w_in")[0].reshape(KT, P, 2, CH, P).transpose(2, 3, 1, 0, 4).reshape(2, CH, P, KT * P)
    ax = np.stack([f("lru_w_a")[0], f("lru_w_x")[0]], axis=2).reshape(CH, P, 2 * P)
    vec = np.concatenate([f("lru_conv_w")[0], f("lru_conv_b"), f("lru_b_a"), f("lru_b_x"), f("lru_lambda")])
    gains = np.stack([f(k)[layer] for layer in range(2)
                      for k in ("mix_pre_norm", "mix_post_norm", "ffn_pre_norm", "ffn_post_norm")])
    up = f("ffn_w_up").reshape(2, KT, P, FFN // P, P).transpose(0, 3, 2, 1, 4).reshape(2, FFN // P, P, KT * P)
    return {
        "x": f("x").reshape(TB, P, D),
        "positions": f("positions").reshape(TB, P).T,
        "inv_freq": inverse_frequencies()[None],
        "gains": gains,
        "qkv_gain": np.concatenate([f("mla_q_norm"), f("mla_kv_norm")], axis=1),
        "w_in_q": by_partition(w_in[:, :QRANK]),
        "w_in_kv": by_partition(w_in[:, QRANK:]),
        "w_heads": heads,
        "w_values": values,
        "w_rope": rope,
        "w_o": f("mla_w_o")[0].reshape(KT, P, D),
        "w_rec": lru_in[1],
        "w_gate": lru_in[0],
        "w_ax": ax,
        "lru_vec": vec.reshape(VEC_IN, CH, P).transpose(2, 1, 0),
        "w_out": f("lru_w_out")[0].reshape(KT, P, D),
        "w_up": up,
        "w_down": f("ffn_w_down").reshape(2, FFN // P, P, D),
    }


def kernel(**inputs):
    import concourse.bacc as bacc
    from concourse.bass_utils import run_bass_kernel_spmd

    nc = bacc.Bacc("TRN2", target_bir_lowering=False, num_devices=1)
    arrays = {k: np.ascontiguousarray(v) for k, v in packed(inputs).items()}
    args = [nc.dram_tensor(k, a.shape, mybir.dt.from_np(a.dtype), kind="ExternalInput").ap() for k, a in arrays.items()]
    out = nc.dram_tensor("out", (TB, P, D), F32, kind="ExternalOutput").ap()
    trunk(nc, *args, out)
    r = run_bass_kernel_spmd(nc, [arrays], core_ids=[0])
    return r.results[0]["out"].reshape(1, SEQ, D)
```
